# Optimizing a Trainium2 kernel written in Bass

```python
import math
import jax, jax.numpy as jnp
from jax import lax
import numpy as np

D_MODEL = 1024
BATCH = 1
SEQ = 512
DEPTH = 1
DEC_BATCH = 8
DEC_SEQ = 4
PAST_LEN = 4096
PAGE_SIZE = 128

HEAD_DIM = D_MODEL // 16
NSA_HEADS = 6
NSA_KV_HEADS = 2
NSA_GROUP = NSA_HEADS // NSA_KV_HEADS
NSA_WIDTH = NSA_HEADS * HEAD_DIM
NSA_KV_WIDTH = NSA_KV_HEADS * HEAD_DIM
CMP_BLOCK = 32
CMP_STRIDE = 16
CMP_HIDDEN = 2 * HEAD_DIM
SLC_BLOCK = 64
SLC_TOP = 8
NSA_WINDOW = 512
FORCE_SCORE = 1.0e4
DIL_PAIRS = ((128, 1), (512, 4), (2048, 16))
DIL_HEADS_PER_PAIR = 2
DIL_HEADS = DIL_HEADS_PER_PAIR * len(DIL_PAIRS)
DIL_WIDTH = DIL_HEADS * HEAD_DIM
POOL_WINDOWS = (2, 4, 8, 16)
POOL_WIDTH = D_MODEL // 4
POOL_GROUP_WIDTH = POOL_WIDTH // len(POOL_WINDOWS)
POOL_BUF = max(POOL_WINDOWS) - 1
MIX_WIDTH = NSA_WIDTH + DIL_WIDTH + POOL_WIDTH
IN_SPLITS = (NSA_WIDTH, 6 * NSA_KV_WIDTH, 3 * NSA_HEADS, 3 * DIL_WIDTH, POOL_WIDTH)
IN_COLS = sum(IN_SPLITS)
D_FF = 2816
Q_BLOCK = 128
NORM_EPS = 1e-6
SCALE = HEAD_DIM ** -0.5

kernel_name = "hymba_nsa_dilated_pool_macaron_step"

def rms_norm(x, g):
    xf = x.astype(jnp.float32)
    y = xf * lax.rsqrt(jnp.mean(xf * xf, axis=-1, keepdims=True) + NORM_EPS)
    return (y * g.astype(jnp.float32)).astype(x.dtype)

def swiglu(h, w_io, w_o):
    gate, up = jnp.split(h @ w_io, 2, axis=-1)
    return (jax.nn.silu(gate) * up) @ w_o

def masked_softmax(s, mask, axes):
    s = jnp.where(mask, s, -jnp.inf)
    m = jnp.max(s, axis=axes, keepdims=True)
    m = jnp.where(jnp.isfinite(m), m, 0.0)
    e = jnp.exp(s - m)
    den = jnp.sum(e, axis=axes, keepdims=True)
    p = e / jnp.where(den > 0, den, 1.0)
    lse = jnp.squeeze(m + jnp.log(den), axis=axes)
    return p, lse

def blockwise(fn, args, in_axes, out_axes, n_q):
    qb = min(Q_BLOCK, n_q)
    if qb == n_q:
        return fn(*args)
    nb = n_q // qb

    def split(a, ax):
        a = a.reshape(a.shape[:ax] + (nb, qb) + a.shape[ax + 1:])
        return jnp.moveaxis(a, ax, 0)

    def merge(a, ax):
        a = jnp.moveaxis(a, 0, ax)
        return a.reshape(a.shape[:ax] + (nb * qb,) + a.shape[ax + 2:])

    outs = lax.map(lambda t: fn(*t), tuple(split(a, ax) for a, ax in zip(args, in_axes)))
    return tuple(merge(o, ax) for o, ax in zip(outs, out_axes))

def compress(rows, w1, b1, w2):
    B, L, H, dh = rows.shape
    n_sub = CMP_BLOCK // CMP_STRIDE
    n_p = L // CMP_STRIDE
    n_cmp = n_p - n_sub + 1
    pieces = rows[:, :n_p * CMP_STRIDE].reshape(B, n_p, CMP_STRIDE, H, dh)
    pieces = pieces.transpose(0, 1, 3, 2, 4).reshape(B, n_p, H, CMP_STRIDE * dh)
    w1 = w1.reshape(n_sub, CMP_STRIDE * dh, CMP_HIDDEN)
    hid = b1
    for c in range(n_sub):
        hid = hid + jnp.einsum('bphf,fe->bphe', pieces[:, c:c + n_cmp], w1[c])
    return jnp.einsum('bnhe,ed->bnhd', jax.nn.silu(hid), w2)

def slc_attend(q, qpos, kb, vb, idx):
    B, KVH = kb.shape[0], kb.shape[1]
    bi = jnp.arange(B)[:, None, None, None]
    hi = jnp.arange(KVH)[None, :, None, None]
    kg = kb[bi, hi, idx]
    vg = vb[bi, hi, idx]
    kpos = idx[..., None] * SLC_BLOCK + jnp.arange(SLC_BLOCK)
    s = jnp.einsum('bqhgd,bhqnsd->bhgqns', q, kg).astype(jnp.float32) * SCALE
    mask = (kpos <= qpos[None, None, :, None, None])[:, :, None]
    p, _ = masked_softmax(s, mask, (-2, -1))
    return jnp.einsum('bhgqns,bhqnsd->bqhgd', p.astype(vg.dtype), vg)

def window_attend(q, k_all, v_all, qpos):
    B, T, KVH, G, dh = q.shape
    Lw = k_all.shape[1]
    q0 = Lw - T
    qb = min(Q_BLOCK, T)
    nb = T // qb
    kidx = q0 + jnp.arange(nb)[:, None] * qb + jnp.arange(-NSA_WINDOW, qb)[None, :]
    kpos = qpos[0] - q0 + kidx
    qp = qpos.reshape(nb, qb)
    mask = ((kidx >= 0)[:, None, :] & (kpos[:, None, :] <= qp[:, :, None])
            & (kpos[:, None, :] > qp[:, :, None] - NSA_WINDOW))
    ci = jnp.clip(kidx, 0, Lw - 1)
    kg = k_all[:, ci]
    vg = v_all[:, ci]
    qq = q.reshape(B, nb, qb, KVH, G, dh)
    s = jnp.einsum('bnqhgd,bnkhd->bnhgqk', qq, kg).astype(jnp.float32) * SCALE
    p, _ = masked_softmax(s, mask[None, :, None, None], (-1,))
    o = jnp.einsum('bnhgqk,bnkhd->bnqhgd', p.astype(vg.dtype), vg)
    return o.reshape(B, T, KVH, G, dh)

def nsa(q, cmp_all, slc_all, win_all, gates, qpos, g_kc, cw1, cb1, cw2):
    B, T = q.shape[:2]
    ck = rms_norm(compress(cmp_all[:, :, 0], cw1[0], cb1[0], cw2[0]), g_kc)
    cv = compress(cmp_all[:, :, 1], cw1[1], cb1[1], cw2[1])
    n_cmp = ck.shape[1]
    cend = jnp.arange(n_cmp) * CMP_STRIDE + (CMP_BLOCK - 1)
    s = jnp.einsum('bqhgd,bchd->bhgqc', q, ck).astype(jnp.float32) * SCALE
    p_cmp, _ = masked_softmax(s, cend[None, :] <= qpos[:, None], (-1,))
    o_cmp = jnp.einsum('bhgqc,bchd->bqhgd', p_cmp.astype(cv.dtype), cv)
    L = slc_all.shape[1]
    n_slc = -(-L // SLC_BLOCK)
    ci = jnp.arange(n_cmp)[:, None] * CMP_STRIDE
    sj = jnp.arange(n_slc)[None, :] * SLC_BLOCK
    cover = ((ci < sj + SLC_BLOCK) & (ci + CMP_BLOCK > sj)).astype(jnp.float32)
    imp = jnp.einsum('bhgqc,cj->bhqj', p_cmp, cover)
    jq = qpos // SLC_BLOCK
    jj = jnp.arange(n_slc)[None, :]
    valid = jj <= jq[:, None]
    forced = (jj == 0) | (jj == jq[:, None]) | (jj == jq[:, None] - 1)
    score = jnp.where(valid, imp + jnp.where(forced, FORCE_SCORE, 0.0), -1.0)
    _, idx = lax.top_k(score, min(SLC_TOP, n_slc))
    kv_pad = jnp.pad(slc_all, ((0, 0), (0, n_slc * SLC_BLOCK - L), (0, 0), (0, 0), (0, 0)))
    kv_blk = kv_pad.reshape(B, n_slc, SLC_BLOCK, 2, NSA_KV_HEADS, HEAD_DIM).transpose(3, 0, 4, 1, 2, 5)
    (o_slc,) = blockwise(lambda qq, pp, ii: (slc_attend(qq, pp, kv_blk[0], kv_blk[1], ii),),
                         (q, qpos, idx), (1, 0, 2), (1,), T)
    o_win = window_attend(q, win_all[:, :, 0], win_all[:, :, 1], qpos)
    return gates[..., 0:1] * o_cmp + gates[..., 1:2] * o_slc + gates[..., 2:3] * o_win

def dilated_group(q, k_all, v_all, w, d):
    Lk, Tq = k_all.shape[1], q.shape[1]
    nk = w // d + 1
    qloc = (Lk - Tq) + jnp.arange(Tq)

    def one(qb, ql):
        kidx = ql[:, None] - d * jnp.arange(nk)[None, :]
        valid = kidx >= 0
        kidx = jnp.maximum(kidx, 0)
        kg = k_all[:, kidx]
        vg = v_all[:, kidx]
        s = jnp.einsum('bqhd,bqkhd->bhqk', qb, kg).astype(jnp.float32) * SCALE
        p, lse = masked_softmax(s, valid[None, None], (-1,))
        o = jnp.einsum('bhqk,bqkhd->bqhd', p.astype(vg.dtype), vg)
        return o, lse.transpose(0, 2, 1)

    return blockwise(one, (q, qloc), (1, 0), (1, 1), Tq)

def pool_mix(u_ext, qpos, pw, pscale):
    B, Le, C = u_ext.shape
    T = Le - POOL_BUF
    cs = jnp.concatenate([jnp.zeros((B, 1, C), jnp.float32),
                          jnp.cumsum(u_ext.astype(jnp.float32), axis=1)], axis=1)
    u = u_ext[:, POOL_BUF:].astype(jnp.float32)
    diffs = []
    for g, w in enumerate(POOL_WINDOWS):
        sl = slice(g * POOL_GROUP_WIDTH, (g + 1) * POOL_GROUP_WIDTH)
        win_sum = cs[:, POOL_BUF + 1:, sl] - cs[:, POOL_BUF + 1 - w:POOL_BUF + 1 - w + T, sl]
        cnt = jnp.minimum(w, qpos + 1).astype(jnp.float32)[None, :, None]
        diffs.append(win_sum / cnt - u[:, :, sl])
    dlt = jnp.stack(diffs, axis=2).astype(pw.dtype)
    y = jnp.einsum('btgc,gce->btge', dlt, pw).reshape(B, T, POOL_WIDTH)
    return y * pscale

def token_mixer(h, qpos0, past, w_in_l, qk_g, cw1, cb1, cw2, pw, pscale):
    past_cmp, past_slc, past_win, past_d0, past_d1, past_d2, past_pool = past
    B, T, _ = h.shape
    qpos = qpos0 + jnp.arange(T)
    proj = h @ w_in_l
    offs = np.cumsum(IN_SPLITS)[:-1].tolist()
    q_a, kv_a, g_a, qkv_b, u_c = jnp.split(proj, offs, axis=-1)

    q_a = rms_norm(q_a.reshape(B, T, NSA_KV_HEADS, NSA_GROUP, HEAD_DIM), qk_g[0])
    kv_a = kv_a.reshape(B, T, 6, NSA_KV_HEADS, HEAD_DIM)
    cmp_new = kv_a[:, :, 0:2]
    slc_new = jnp.stack([rms_norm(kv_a[:, :, 2], qk_g[2]), kv_a[:, :, 3]], axis=2)
    win_new = jnp.stack([rms_norm(kv_a[:, :, 4], qk_g[3]), kv_a[:, :, 5]], axis=2)
    cmp_all = jnp.concatenate([past_cmp, cmp_new], axis=1)
    slc_all = jnp.concatenate([past_slc, slc_new], axis=1)
    win_all = jnp.concatenate([past_win, win_new], axis=1)
    gates = jax.nn.sigmoid(g_a.reshape(B, T, NSA_KV_HEADS, NSA_GROUP, 3))
    o_a = nsa(q_a, cmp_all, slc_all, win_all, gates, qpos, qk_g[1], cw1, cb1, cw2)
    win_state = win_all[:, -min(NSA_WINDOW, win_all.shape[1]):]

    qkv_b = qkv_b.reshape(B, T, 3, len(DIL_PAIRS), DIL_HEADS_PER_PAIR, HEAD_DIM)
    q_b = rms_norm(qkv_b[:, :, 0], qk_g[4])
    k_b = rms_norm(qkv_b[:, :, 1], qk_g[5])
    v_b = qkv_b[:, :, 2]
    outs, lses, dil_states = [], [], []
    for g, ((w, d), past_d) in enumerate(zip(DIL_PAIRS, (past_d0, past_d1, past_d2))):
        kv_all = jnp.concatenate([past_d, jnp.stack([k_b[:, :, g], v_b[:, :, g]], axis=2)], axis=1)
        o, lse = dilated_group(q_b[:, :, g], kv_all[:, :, 0], kv_all[:, :, 1], w, d)
        outs.append(o)
        lses.append(lse)
        dil_states.append(kv_all[:, -min(w, kv_all.shape[1]):])
    alpha = jax.nn.softmax(jnp.stack(lses, axis=0), axis=0)
    o_b = jnp.concatenate([outs[g] * alpha[g][..., None].astype(outs[g].dtype)
                           for g in range(len(DIL_PAIRS))], axis=2)

    u_ext = jnp.concatenate([past_pool, u_c], axis=1)
    o_c = pool_mix(u_ext, qpos, pw, pscale)
    pool_state = u_ext[:, -POOL_BUF:]

    mix = jnp.concatenate([o_a.reshape(B, T, NSA_WIDTH), o_b.reshape(B, T, DIL_WIDTH), o_c], axis=-1)
    return mix, (cmp_new, slc_new, win_state, dil_states[0], dil_states[1], dil_states[2], pool_state)

def trunk(x, qpos0, past_fn, params):
    (w_in, w_out, norm_gain, qk_gain, ffn_in, ffn_out, cmp_w1, cmp_b1, cmp_w2, pool_w, pool_scale) = params
    states = []
    for l in range(DEPTH):
        x = x + 0.5 * swiglu(rms_norm(x, norm_gain[l, 0]), ffn_in[l, 0], ffn_out[l, 0])
        mix, st = token_mixer(rms_norm(x, norm_gain[l, 1]), qpos0, past_fn(l), w_in[l], qk_gain[l],
                              cmp_w1[l], cmp_b1[l], cmp_w2[l], pool_w[l], pool_scale[l])
        x = x + mix @ w_out[l]
        x = x + 0.5 * swiglu(rms_norm(x, norm_gain[l, 2]), ffn_in[l, 1], ffn_out[l, 1])
        states.append(st)
    stacked = [jnp.stack([s[i] for s in states], axis=0) for i in range(len(states[0]))]
    return x, stacked

def setup_inputs(seed: int = 0) -> dict:
    key = jax.random.key(seed)
    ks = jax.random.split(key, 24)
    f32 = jnp.float32
    n_pages = PAST_LEN // PAGE_SIZE
    n_used = DEC_BATCH * n_pages
    n_phys = n_used + n_used // 4

    def nrm(k, shape, scale=1.0):
        return jax.random.normal(k, shape, f32) * scale

    kv_row = (2, NSA_KV_HEADS, HEAD_DIM)
    dil_row = (2, DIL_HEADS_PER_PAIR, HEAD_DIM)
    return {
        "x_prompt": nrm(ks[0], (BATCH, SEQ, D_MODEL)),
        "x_sample": nrm(ks[1], (DEC_BATCH, DEC_SEQ, D_MODEL)),
        "cache_cmp_kv": nrm(ks[2], (DEPTH, n_phys, PAGE_SIZE) + kv_row),
        "cache_slc_kv": nrm(ks[3], (DEPTH, n_phys, PAGE_SIZE) + kv_row),
        "cache_win_kv": nrm(ks[4], (DEPTH, DEC_BATCH, min(NSA_WINDOW, PAST_LEN)) + kv_row),
        "cache_dil0_kv": nrm(ks[5], (DEPTH, DEC_BATCH, min(DIL_PAIRS[0][0], PAST_LEN)) + dil_row),
        "cache_dil1_kv": nrm(ks[6], (DEPTH, DEC_BATCH, min(DIL_PAIRS[1][0], PAST_LEN)) + dil_row),
        "cache_dil2_kv": nrm(ks[7], (DEPTH, DEC_BATCH, min(DIL_PAIRS[2][0], PAST_LEN)) + dil_row),
        "state_pool": nrm(ks[8], (DEPTH, DEC_BATCH, POOL_BUF, POOL_WIDTH)),
        "page_table": jax.random.permutation(ks[9], n_phys)[:n_used].reshape(DEC_BATCH, n_pages).astype(jnp.int32),
        "w_in": nrm(ks[10], (DEPTH, D_MODEL, IN_COLS), D_MODEL ** -0.5),
        "w_out": nrm(ks[11], (DEPTH, MIX_WIDTH, D_MODEL), MIX_WIDTH ** -0.5),
        "norm_gain": 1.0 + 0.1 * nrm(ks[12], (DEPTH, 3, D_MODEL)),
        "qk_gain": 1.0 + 0.1 * nrm(ks[13], (DEPTH, 6, HEAD_DIM)),
        "ffn_in": nrm(ks[14], (DEPTH, 2, D_MODEL, 2 * D_FF), D_MODEL ** -0.5),
        "ffn_out": nrm(ks[15], (DEPTH, 2, D_FF, D_MODEL), D_FF ** -0.5),
        "cmp_w1": nrm(ks[16], (DEPTH, 2, CMP_BLOCK * HEAD_DIM, CMP_HIDDEN), (CMP_BLOCK * HEAD_DIM) ** -0.5),
        "cmp_b1": 0.02 * nrm(ks[17], (DEPTH, 2, CMP_HIDDEN)),
        "cmp_w2": nrm(ks[18], (DEPTH, 2, CMP_HIDDEN, HEAD_DIM), CMP_HIDDEN ** -0.5),
        "pool_w": nrm(ks[19], (DEPTH, len(POOL_WINDOWS), POOL_GROUP_WIDTH, POOL_GROUP_WIDTH), POOL_GROUP_WIDTH ** -0.5),
        "pool_scale": 1.0 + 0.1 * nrm(ks[20], (DEPTH, POOL_WIDTH)),
    }

def reference(x_prompt, x_sample, cache_cmp_kv, cache_slc_kv, cache_win_kv, cache_dil0_kv,
              cache_dil1_kv, cache_dil2_kv, state_pool, page_table, w_in, w_out, norm_gain, qk_gain,
              ffn_in, ffn_out, cmp_w1, cmp_b1, cmp_w2, pool_w, pool_scale):
    params = (w_in, w_out, norm_gain, qk_gain, ffn_in, ffn_out, cmp_w1, cmp_b1, cmp_w2, pool_w, pool_scale)
    n_pages = PAST_LEN // PAGE_SIZE
    dt = x_prompt.dtype

    empty_kv = jnp.zeros((BATCH, 0, 2, NSA_KV_HEADS, HEAD_DIM), dt)
    empty_dil = jnp.zeros((BATCH, 0, 2, DIL_HEADS_PER_PAIR, HEAD_DIM), dt)
    pool0 = jnp.zeros((BATCH, POOL_BUF, POOL_WIDTH), dt)

    def prompt_past(l):
        return (empty_kv, empty_kv, empty_kv, empty_dil, empty_dil, empty_dil, pool0)

    def gather_pages(pool):
        return pool[page_table].reshape((DEC_BATCH, n_pages * PAGE_SIZE) + pool.shape[2:])

    def sample_past(l):
        return (gather_pages(cache_cmp_kv[l]), gather_pages(cache_slc_kv[l]), cache_win_kv[l],
                cache_dil0_kv[l], cache_dil1_kv[l], cache_dil2_kv[l], state_pool[l])

    y_prompt, sp = trunk(x_prompt, 0, prompt_past, params)
    y_sample, ss = trunk(x_sample, PAST_LEN, sample_past, params)
    return (y_prompt, y_sample, sp[0], ss[0], sp[1], ss[1], sp[2], ss[2], sp[3], ss[3],
            sp[4], ss[4], sp[5], ss[5], sp[6], ss[6])


_drawn_inputs = setup_inputs


def setup_inputs(seed=0):
    import zlib

    import numpy as np

    out = dict(_drawn_inputs(seed))
    spreads = {}
    factors = {'cmp_b1': 22.707}
    for name, (base, spread) in spreads.items():
        noise = np.random.default_rng([zlib.crc32(name.encode()), seed]).standard_normal(out[name].shape)
        drawn = base * np.exp(spread * noise) if base else spread * noise
        out[name] = __import__('jax').numpy.asarray(drawn.astype(out[name].dtype))
    for name, factor in factors.items():
        out[name] = (out[name] * factor).astype(out[name].dtype)
    return out
```

```python
from contextlib import ExitStack

import numpy as np

import concourse.bass as bass
from concourse import mybir

F32 = mybir.dt.float32
I32 = mybir.dt.int32
U32 = mybir.dt.uint32
ALU = mybir.AluOpType
ACT = mybir.ActivationFunctionType
AX = mybir.AxisListType

P = 128
D = 1024
KD = D // P
TP, NB, TS = 512, 8, 4
NS = NB * TS
T = TP + NS
HALF = T // 2
QT_TILES = TP // P
PAGE, PAST = 128, 4096
NPG = PAST // PAGE
HD = 64
FF = 2816
FCH = FF // P
GROUPS = FCH // 2
COLS = 2578
CG = 352
NCG = -(-COLS // CG)
SLOT = 2816
RING = 4
SCALE = HD ** -0.5
EPS = 1e-6
NEG = -1.0e30
WDIL = ((128, 1), (512, 4), (2048, 16))

C_Q, C_CMP, C_SLCK, C_SLCV, C_WINK, C_WINV, C_G = 0, 384, 640, 768, 896, 1024, 1152
C_QB, C_KB, C_VB, C_U = 1170, 1554, 1938, 2322
SECTIONS = ((C_Q, 6, 0, 0), (C_SLCK, 2, 2, 6), (C_WINK, 2, 3, 8), (C_QB, 6, 4, 10), (C_KB, 6, 5, 16))
IT_SLC, IT_WIN, IT_QB, IT_KB, IT_U, ITEMS = 3, 4, 5, 8, 11, 13


def const_layout():
    at, out = 0, {}
    for name, rows, n in (
        ("ident", P, P), ("ones", P, P), ("diag", P, P), ("band_prev", P, P),
        ("mod4_off", P, P), ("mod4_diag", P, P), ("mod16_off", P, P), ("mod16_diag", P, P),
        ("cmp_add", P, 4 * 32), ("cmp_keep", P, 4 * 32),
        ("win_past", 24, 512), ("d0_past", 8, P), ("d12_past", 8, 512),
        ("new_a", 24, NB * 32), ("new_d0", 8, NB * 32), ("new_d12", 8, NB * 32),
        ("sum_heads", 24, NB * 64), ("to_rows", 64, NB * 24), ("tok_rows", 32, NB * 24), ("gate_pick", 24, 18),
        ("pool_w", P, 2), ("pool_head", P, 32), ("force", 64, 65), ("eps", P, 1), ("p8", P, 1), ("p32", P, 1),
    ):
        out[name] = (at, rows, n)
        at += n
    return out, at


CL, CN = const_layout()


def constants():
    c = np.zeros((P, CN), np.float32)

    def put(name, a):
        at, rows, n = CL[name]
        c[:rows, at:at + n] = a.reshape(rows, n)

    q, k = np.arange(P)[:, None], np.arange(P)[None, :]
    add = lambda ok: np.where(ok, 0.0, NEG)
    put("ident", np.eye(P))
    put("ones", np.ones((P, P)))
    put("diag", add(k <= q))
    put("band_prev", add(k >= q))
    for d in (4, 16):
        put(f"mod{d}_off", add((q - k) % d == 0))
        put(f"mod{d}_diag", add(((q - k) % d == 0) & (k <= q)))
    pos = np.arange(4)[None, :, None] * P + np.arange(P)[:, None, None]
    seen = (np.arange(32)[None, None, :] * 16 + 31 <= pos) & (np.arange(32) < 31)[None, None, :]
    put("cmp_add", add(seen))
    put("cmp_keep", seen.astype(np.float32))
    ta, td = np.arange(24) % TS, np.arange(8) % TS
    key = np.arange(P)[None, :] * 4 + np.arange(4)[:, None]
    put("win_past", add(key.reshape(1, 512) > ta[:, None]))
    put("d0_past", add(np.arange(P)[None, :] >= td[:, None]))
    put("d12_past", add(np.repeat(np.arange(4), P)[None, :] == td[:, None]))
    tok_b, tok_t = np.arange(NS) // TS, np.arange(NS) % TS
    own = tok_b[None, None, :] == np.arange(NB)[None, :, None]
    put("new_a", add(own & (tok_t[None, None, :] <= ta[:, None, None])))
    put("new_d0", add(own & (tok_t[None, None, :] <= td[:, None, None])))
    put("new_d12", add(own & (tok_t[None, None, :] == td[:, None, None])))
    r64 = np.arange(64)
    rb, rh, rt = r64 // 8, r64 // 4 % 2, r64 % 4
    ra = np.arange(24)
    same = (rh[None, None, :] == (ra // 12)[:, None, None]) & (rt[None, None, :] == ta[:, None, None]) \
        & (rb[None, None, :] == np.arange(NB)[None, :, None])
    put("sum_heads", same.astype(np.float32))
    put("to_rows", same.transpose(2, 1, 0).astype(np.float32))
    tok = np.arange(NS)[:, None, None] == (np.arange(NB)[None, :, None] * TS + ta[None, None, :])
    put("tok_rows", tok.astype(np.float32))
    put("gate_pick", (np.repeat(np.arange(6), 3)[None, :] == (ra // 4)[:, None]).astype(np.float32))
    w = np.array([[2, 8], [4, 16]])[(np.arange(P) // 64)]
    put("pool_w", 1.0 / w)
    put("pool_head", 1.0 / np.minimum(w[:, :, None], np.arange(16)[None, None, :] + 1))
    f = np.zeros((64, 65))
    f[:, [0, 63, 64]] = 1.0e4
    put("force", f)
    put("eps", np.full((P, 1), EPS))
    put("p8", np.arange(P)[:, None] % 8)
    put("p32", np.arange(P)[:, None] % 32)
    return c


def page_selectors():
    s = np.zeros((NPG, 10, P), np.float32)
    for half in range(2):
        s[half * 16 + np.arange(P) // 8, half, np.arange(P)] = 1.0
    for g in range(8):
        s[4 * g + np.arange(P) // 32, 2 + g, np.arange(P)] = 1.0
    return s.reshape(NPG, 10 * P)


def build(nc, I, O):
    ctx = ExitStack()
    with ctx:
        ctx.enter_context(nc.allow_non_contiguous_dma(reason="small transposed tables"))

        def sb(name, shape, dt=F32):
            return ctx.enter_context(nc.sbuf_tensor(name, shape, dt))

        def sem(name):
            return ctx.enter_context(nc.semaphore(name))

        XT = sb("XT", [P, KD, T])
        HN = sb("HN", [P, KD * T])
        BIG = sb("BIG", [P, 5 * COLS])
        WR = sb("WR", [P, RING * SLOT])
        QTR = sb("QTR", [P, 11 * T])
        CKT = sb("CKT", [P, NB, 256])
        CV = sb("CV", [P, NB, 2, P])
        VV = sb("VV", [P, 5, 640])
        CO = sb("CO", [P, CN])
        NG = sb("NG", [P, 3, KD])
        QG = sb("QG", [P, 6, HD])
        B1 = sb("B1", [P, 2])
        W2 = sb("W2", [P, 2, HD])
        PW = sb("PW", [P, 2, HD])
        PSC = sb("PSC", [P, 2])
        IXC = sb("IXC", [P, 2, NB], U32)
        IXS = sb("IXS", [P, 8, NB], U32)
        PTI = sb("PTI", [NPG, NB], I32)
        PTF = sb("PTF", [NPG, NB])
        GT = sb("GT", [P, 5, 18])
        SM = sb("SM", [P, 420])
        QA = sb("QA", [P, NB, 24])
        QD = sb("QD", [P, 3, NB, 8])
        PS = ctx.enter_context(nc.psum_tensor("PS", [P, 8, 512], F32))

        HNk = HN[:, :].rearrange("p (k t) -> p k t", k=KD)
        MIXT = HNk
        HID = BIG[:, 0:FCH * T].rearrange("p (n t) -> p n t", n=FCH)
        PROJ = BIG[:, :].rearrange("p (t c) -> p t c", t=5)
        QT = QTR[:, :].rearrange("p (m t) -> p m t", m=11)
        slot = [WR[:, s * SLOT:(s + 1) * SLOT] for s in range(RING)]

        def const(name):
            at, rows, n = CL[name]
            return CO[0:rows, at:at + n]

        ident, ones = const("ident"), const("ones")
        eps = const("eps")

        GB = sb("GB", [P, 2, 2, HALF])
        RB = GB[:, 0, :, :]

        ld = {n: sem("ld_" + n) for n in ("const", "cw1", "small", "x", "selp", "cw1b", "pieces", "poolst")}
        d_ch, a_ch, = sem("dve_chain"), sem("act_chain")
        g_rows = [sem("g_rows0"), sem("g_rows1")]
        ix_f, ix_mm, ix_ok = sem("ix_f"), sem("ix_mm"), sem("ix_ok")
        x_tr, x_ev = sem("x_tr"), sem("x_ev")
        t_done, ev_act, ev_dve = sem("t_done"), sem("ev_act"), sem("ev_dve")
        m_done, silu_done, w_done, w_copied = sem("m_done"), sem("silu_done"), sem("w_done"), sem("w_copied")
        hid_zero = sem("hid_zero")
        ck_ss, ck_sq, ck_n, ck_t, ck_ev = sem("ck_ss"), sem("ck_sq"), sem("ck_n"), sem("ck_t"), sem("ck_ev")
        w_in_ring = [sem(f"ring{s}") for s in range(RING)]
        rs = [{n: sem(f"rms{r}_{n}") for n in ("sq", "sum", "root", "hn")} for r in range(3)]
        ff = [{n: sem(f"ffn{f}_{n}") for n in ("in", "silu", "mul", "out", "res")} for f in range(2)]
        pj_mm, pj_ev = sem("pj_mm"), sem("pj_ev")
        hn_ss, hn_rt, qn, cp_act = sem("hn_ss"), sem("hn_rt"), sem("qn"), sem("cp_act")
        qt_mm, qt_act, qt_dve = sem("qt_mm"), sem("qt_act"), sem("qt_dve")
        st_cmp, st_out = sem("st_cmp"), sem("st_out")
        pc = {n: sem("pc_" + n) for n in ("tr", "ev", "mm", "silu", "w", "ss", "rt", "n", "t", "ev2")}
        po = {n: sem("po_" + n) for n in ("zero", "st", "stev", "dl", "mm", "ev")}
        pa = {n: sem("pa_" + n) for n in ("s", "sev", "nb", "exp", "p", "t", "tev", "pv", "oev",
                                          "cs", "cnb", "cexp", "cp")}
        sa = {n: sem("sa_" + n) for n in ("kv", "kt", "ktev", "s", "sev", "nb", "exp", "w", "pt", "ptev", "pv", "oev",
                                          "gmm", "gts", "imp", "sel", "selmm", "selm", "q", "ex")}
        ld_kv = [sem("ld_kv0"), sem("ld_kv1")]
        ld_wd = sem("ld_wd")
        wo_mm, wo_ev = sem("wo_mm"), sem("wo_ev")
        y_tr, y_ev, y_out = sem("y_tr"), sem("y_ev"), sem("y_out")
        cpy = sem("state_copies")
        block = ctx.enter_context(nc.Block())

        XIN = WR[:, 0:5 * D].rearrange("p (t n) -> p t n", t=5)
        PB = [BIG[:, 0:8192].rearrange("p (h n) -> p h n", h=2), WR[:, 0:8192].rearrange("p (h n) -> p h n", h=2)]
        YO = BIG[:, 0:5 * D].rearrange("p (t n) -> p t n", t=5)
        PTB = [BIG[:, 8192:12288].rearrange("p (h s n) -> p h s n", h=2, s=8),
               HN[:, 0:4096].rearrange("p (h s n) -> p h s n", h=2, s=8)]
        HIDC = BIG[:, 12288:12800].rearrange("p (u n) -> p u n", u=2)
        CW1 = QTR[:, 0:4096].rearrange("p (v c e) -> p v c e", v=2, c=16)
        SELP = QTR[0:NPG, 4096:4096 + 10 * P].rearrange("p (s m) -> p s m", s=10)
        CK = VV[:, :, :].rearrange("p a b -> p (a b)")[:, 0:2048]
        CKS = BIG[:, 0:2048]
        QP = HN[:, 0:5 * 384].rearrange("p (t g h d) -> p t g h d", t=5, g=3, h=2)
        SQT = HN[:, 1920:1920 + 2 * 384].rearrange("p (u n) -> p u n", u=2)
        CW1B = WR[:, 0:4096].rearrange("p (v c e) -> p v c e", v=2, c=16)
        PCS = WR[0:32, 4096:8192]
        o = 8192
        UT = WR[:, o:o + 1056].rearrange("p (c t) -> p c t", c=2)
        UTS = WR[:, o + 1056:o + 1360].rearrange("p (c b t) -> p c b t", c=2, b=NB)
        PTC = WR[:, o + 1360:o + 2384].rearrange("p (v h s n) -> p v h s n", v=2, h=2, s=8)
        HIDP = WR[:, o + 2384:o + 2512].rearrange("p (q n) -> p q n", q=4)
        PST = WR[0:120, o + 2512:o + 2768]
        CKTP = WR[:, o + 2768:o + 2800]
        CVP = WR[0:31, o + 2800:o + 2928]
        CKP = WR[0:31, o + 2928:o + 3056]
        T1 = BIG[:, 6000:7056].rearrange("p (c t) -> p c t", c=2)
        T2 = BIG[:, 7056:8112].rearrange("p (c t) -> p c t", c=2)
        T1S = BIG[:, 8112:8416].rearrange("p (c b t) -> p c b t", c=2, b=NB)
        T2S = BIG[:, 8416:8720].rearrange("p (c b t) -> p c b t", c=2, b=NB)
        DL = BIG[:, 8720:9744].rearrange("p (c t) -> p c t", c=2)
        DLS = BIG[:, 9744:9808].rearrange("p (c b t) -> p c b t", c=2, b=NB)
        PHD = BIG[:, 9808:9840].rearrange("p (c t) -> p c t", c=2)
        CKPS = BIG[0:31, 9840:9968]
        SB = BIG[:, 0:3072].rearrange("p (u b n) -> p u b n", u=2, b=3)
        PTS = BIG[:, 3072:4608].rearrange("p (u n) -> p u n", u=3)
        SC = BIG[:, 4608:4800].rearrange("p (h n) -> p h n", h=6)
        SS = SM[:, 0:110].rearrange("p (t n) -> p t n", t=5)
        SSC = SM[:, 110:142]
        SSP = SM[0:31, 142:144]
        MX = SM[:, 144:150].rearrange("p (u n) -> p u n", u=2)
        DEN = SM[:, 150:156].rearrange("p (u n) -> p u n", u=2)
        WT = SM[:, 156:162].rearrange("p (u n) -> p u n", u=2)
        NBI = SM[:, 162:168].rearrange("p (u n) -> p u n", u=2)
        CMX, CDN, CWT = SM[:, 168:174], SM[:, 174:180], SM[:, 180:186]
        MX1 = SM[:, 186:188]

        def tile_rows(tt):
            return P if tt < QT_TILES else NS

        def tok(tt):
            return slice(tt * P, tt * P + tile_rows(tt))

        units = []
        s_count = 0
        for i in range(QT_TILES):
            for hq in range(6):
                h, g = hq // 3, hq % 3
                br = [dict(q=g, k=k, h=h, j0=0, v=v * P + h * HD, off=None, diag="diag")
                      for v, k in enumerate((IT_SLC, IT_WIN))]
                units.append(dict(i=i, nsa=True, hq=hq, h=h, br=br, s0=s_count, new=hq == 0))
                s_count += 2
            for h in range(2):
                br = [dict(q=IT_QB + g, k=IT_KB + g, h=h, j0=max(0, i - 1) if g == 0 else 0,
                           v=256 + g * P + h * HD, off=("band_prev", "mod4_off", "mod16_off")[g],
                           diag=("diag", "mod4_diag", "mod16_diag")[g]) for g in range(3)]
                units.append(dict(i=i, nsa=False, h=h, br=br, s0=s_count, new=False))
                s_count += 3
        NU = len(units)

        SL = BIG[0:24, 8192:8192 + 4128]
        KV = [BIG[:, 0:8192], WR[:, 0:8192]]
        KWD = [WR[:, 8192 + n * 1024:8192 + (n + 1) * 1024] for n in range(3)]
        VVf = VV[:, :, :].rearrange("p a b -> p (a b)")
        SWIN, SDIL = VVf[0:24, 0:544], VVf[0:8, 544:1792]
        SCS = VVf[0:24, 1792:2304].rearrange("p (u n) -> p u n", u=2)
        KD0 = QT[:, 7, 0:256]
        GX = QT[0:24, 8, 0:144].rearrange("p (b c) -> p b c", b=NB)
        IM = QT[0:64, 8, 150:406]
        SCR, RPL, SEL = QT[0:64, 9, 0:65], QT[0:64, 9, 70:135], QT[0:64, 9, 140:205]
        M8 = QT[0:64, 9, 210:218]
        SELM = QT[0:24, 10, 0:512]
        GS = SM[0:24, 190:214].rearrange("p (b c) -> p b c", b=NB)
        OA = QT[:, 2, 0:192].rearrange("p (b r) -> p b r", b=NB)
        OD = QT[:, 2, 200:392].rearrange("p (b g r) -> p b g r", b=NB, g=3)
        SDEN = SM[0:24, 220:228].rearrange("p (u n) -> p u n", u=2)
        SMX = SM[0:24, 228:232]
        SNB = SM[0:24, 232:234]
        SWT = SM[0:24, 234:236]
        DG = SM[0:24, 240:288].rearrange("p (u n) -> p u n", u=2)
        EXR = SM[0:24, 290:418].rearrange("p (u n) -> p u n", u=2)
        def KTB(n):
            return QT[:, (0, 1, 3)[n % 3], 0:512]

        newK = lambda item: QT[:, item, TP:T]
        newV = lambda c: VV[0:NS, 4, c:c + P]

        su = []
        cnt = dict(kt=0, s=0, pt=0)

        def add_unit(kind, b, buf, rows, tchunks, nchunks, tiles, ptdst, out):
            full = [t for t in tiles if t[1] == P]
            new = [t for t in tiles if t[1] != P]
            pts = [full[n:n + 16] for n in range(0, len(full), 16)] + ([new] if new else [])
            su.append(dict(kind=kind, b=b, buf=buf, rows=rows, tc=tchunks, nc=nchunks, pts=pts, ptdst=ptdst,
                           out=out, kt0=cnt["kt"], s0=cnt["s"], pt0=cnt["pt"], n=len(su)))
            cnt["kt"] += len(tchunks)
            cnt["s"] += len(tchunks) + len(nchunks)
            cnt["pt"] += len(pts)

        for b in range(NB):
            add_unit("cmp", b, SCS[:, b % 2, :], 24, [], [(CKT[:, b, 0:255], QA[:, b, :], 0, 255, None)],
                     [(ct * P, P, CV[:, b, ct, :], 0) for ct in range(2)],
                     [QT[:, 6, 300 + 48 * (b % 2):348 + 48 * (b % 2)]], OA[:, b, :])
        for b in range(NB):
            kv = KV[b % 2]
            add_unit("slc", b, SL, 24,
                     [([kv[:, (4 * G + j) * 256:(4 * G + j) * 256 + P] for j in range(4)], QA[:, b, :], 512 * G,
                       ("sel", G)) for G in range(8)],
                     [(newK(IT_SLC), QA[:, b, :], 4096, 32, ("new_a", b))],
                     [(n * P, P, kv[:, n * 256 + P:n * 256 + 2 * P], 0) for n in range(32)]
                     + [(4096, NS, newV(0), 0)],
                     [QT[:, 4, 0:384], QT[:, 5, 0:384], QT[:, 6, 0:24]], OA[:, b, :])
            kw = KWD[0]
            add_unit("win", b, SWIN, 24,
                     [([kw[:, j * 256:j * 256 + P] for j in range(4)], QA[:, b, :], 0, ("past", "win_past"))],
                     [(newK(IT_WIN), QA[:, b, :], 512, 32, ("new_a", b))],
                     [(j * P, P, kw[:, j * 256 + P:(j + 1) * 256], 0) for j in range(4)]
                     + [(512, NS, newV(P), 0)],
                     [QT[:, 6, 32:128], QT[:, 6, 128:152]], OA[:, b, :])
            k1, k2 = KWD[1], KWD[2]
            add_unit("dil", b, SDIL, 8,
                     [([KD0[:, 0:P]], QD[:, 0, b, :], 0, ("past", "d0_past"))]
                     + [([kk[:, j * 256:j * 256 + P] for j in range(4)], QD[:, 1 + n, b, :], P + 512 * n,
                         ("past", "d12_past")) for n, kk in enumerate((k1, k2))],
                     [(newK(IT_KB + g), QD[:, g, b, :], 1152 + 32 * g, 32, ("new_d0" if g == 0 else "new_d12", b))
                      for g in range(3)],
                     [(0, P, KD0[:, P:2 * P], 0)]
                     + [(P + 512 * n + j * P, P, kk[:, j * 256 + P:(j + 1) * 256], 1 + n)
                        for n, kk in enumerate((k1, k2)) for j in range(4)]
                     + [(1152 + 32 * g, NS, newV(256 + P * g), g) for g in range(3)],
                     [QT[:, 6, 160:232], QT[:, 6, 240:264]], OD[:, b, :, :])
        NSU = len(su)

        def out_bank(u):
            return u % 2 if u < NB else 6 + u % 2

        N_KT, N_S, N_PT = cnt["kt"], cnt["s"], cnt["pt"]

        @block.sync
        def _(sp):
            sp.dma_start(CO[:, :], I["consts"]).then_inc(ld["const"], 16)
            sp.dma_start(XIN[:, 0:4, :], I["x_prompt"][0].rearrange("(t p) n -> p t n", p=P)).then_inc(ld["x"], 16)
            sp.dma_start(XIN[0:NS, 4, :], I["x_sample"].rearrange("b t n -> (b t) n")).then_inc(ld["x"], 16)
            sp.dma_start(CW1, I["cmp_w1"][0].rearrange("v (c p) e -> p v c e", p=P)).then_inc(ld["cw1"], 16)

            sp.wait_ge(x_ev, KD + 1)
            sp.wait_ge(t_done, 16 * NB)

            def load_in(f, base, g, s, gs):
                src = I["ffn_in"][0, f].rearrange("(k p) n -> p k n", p=P)
                sl = (base + s) % RING
                dst = slot[sl][:, 0:KD * 256].rearrange("p (k n) -> p k n", k=KD)
                sp.dma_start(dst, src[:, :, bass.ds(g * 256 + gs * FF, 256)]).then_inc(w_in_ring[sl], 16)

            def ffn_loads(f, base):
                for g in range(2):
                    for gs in range(2):
                        load_in(f, base, g, 2 * g + gs, gs)
                with sp.Fori(0, (GROUPS - 3) // 2) as it:
                    for u in range(2):
                        sp.wait_ge(ff[f]["in"], it * 4 + 2 * (u + 1))
                        for gs in range(2):
                            load_in(f, base, it * 2 + 2 + u, 2 * u + gs, gs)
                g = GROUPS - 1
                sp.wait_ge(ff[f]["in"], 2 * (g - 1))
                for gs in range(2):
                    load_in(f, base, g, 2 * g + gs, gs)
                src = I["ffn_out"][0, f].rearrange("(k p) n -> p k n", p=P)
                for op in range(4):
                    if op < 2:
                        sp.wait_ge(ff[f]["in"], 2 * (GROUPS - 1 + op))
                    else:
                        sp.wait_ge(ff[f]["out"], 2 * (op - 1))
                    for s in range(2):
                        sl = (base + 2 * GROUPS + 2 * op + s) % RING
                        dst = slot[sl].rearrange("p (k n) -> p k n", k=11)
                        sp.dma_start(dst, src[:, 11 * s:11 * s + 11, op * 256:(op + 1) * 256])\
                            .then_inc(w_in_ring[sl], 16)

            ffn_loads(0, 0)
            w_in = I["w_in"][0].rearrange("(k p) n -> p k n", p=P)
            for c in range(NCG):
                sl = (30 + c) % RING
                if c < 4:
                    sp.wait_ge(ff[0]["out"], 2 * (3 + c // 2))
                else:
                    sp.wait_ge(pj_mm, 5 * (c - 3))
                n = min(CG, COLS - c * CG)
                sp.dma_start(slot[sl][:, 0:KD * n].rearrange("p (k n) -> p k n", k=KD),
                             w_in[:, :, c * CG:c * CG + n]).then_inc(w_in_ring[sl], 16)
            sp.wait_ge(pj_mm, 5 * NCG)
            sp.dma_start(CW1B, I["cmp_w1"][0].rearrange("v (c p) e -> p v c e", p=P)).then_inc(ld["cw1b"], 16)
            sp.dma_start(PST, I["state_pool"][0].rearrange("b t c -> (b t) c")).then_inc(ld["poolst"], 16)
            sp.wait_ge(pj_ev, 5 * NCG)
            cmp_p = O["cmp_p"].rearrange("a b t x h d -> (a b t) (x h d)")
            sp.dma_start(cmp_p.rearrange("(t p) c -> p t c", p=P), PROJ[:, 0:4, C_CMP:C_CMP + 256]).then_inc(st_cmp, 16)
            sp.wait_ge(st_cmp, 16)
            sp.dma_start(PCS, cmp_p.rearrange("(p s) c -> p (s c)", s=16)).then_inc(ld["pieces"], 16)

            def states():
                def flat(name):
                    return O[name].rearrange("a b t x h d -> (a b) t (x h d)")

                u_p, u_s = O["pool_p"][0, 0], O["pool_s"][0]
                yield O["cmp_s"].rearrange("a b t x h d -> (a b t) (x h d)"), PROJ[0:NS, 4, C_CMP:C_CMP + 256]
                yield u_p, PROJ[P - 15:P, 3, C_U:C_U + 256]
                yield u_s[:, 11:15, :], PROJ[0:NS, 4, C_U:C_U + 256]
                for name, c in (("slc", C_SLCK), ("win", C_WINK)):
                    yield flat(name + "_p")[0].rearrange("(t p) c -> p t c", p=P), PROJ[:, 0:4, c:c + 256]
                yield O["slc_s"].rearrange("a b t x h d -> (a b t) (x h d)"), PROJ[0:NS, 4, C_SLCK:C_SLCK + 256]
                yield flat("win_s")[:, 508:512, :], PROJ[0:NS, 4, C_WINK:C_WINK + 256]
                for g, (w, _) in enumerate(WDIL):
                    n = min(w, TP) // P
                    for x, c in enumerate((C_KB + g * P, C_VB + g * P)):
                        yield (flat(f"dil{g}_p")[0].rearrange("(t p) c -> p t c", p=P)[:, :, x * P:(x + 1) * P],
                               PROJ[:, 4 - n:4, c:c + P])
                        yield flat(f"dil{g}_s")[:, w - TS:w, x * P:(x + 1) * P], PROJ[0:NS, 4, c:c + P]

            sp.wait_ge(qn, 5)
            n_states = 0
            for dst, src in states():
                sp.dma_start(dst, src).then_inc(st_out, 16)
                n_states += 1

            sp.wait_ge(sa["pv"], NSU)
            w_out = I["w_out"][0].rearrange("(k p) n -> p k n", p=P)
            for c in range(4):
                sl = (38 + c) % RING
                sp.dma_start(slot[sl][:, 0:KD * 256].rearrange("p (k n) -> p k n", k=KD),
                             w_out[:, :, c * 256:(c + 1) * 256]).then_inc(w_in_ring[sl], 16)
            for c in range(4):
                sp.wait_ge(wo_mm, 2 * (c + 1))
                if c == 1 or c == 3:
                    g = c // 2
                    for gs in range(2):
                        load_in(1, 42, g, 2 * g + gs, gs)
            f, base = 1, 42
            with sp.Fori(0, (GROUPS - 3) // 2) as it:
                for u in range(2):
                    sp.wait_ge(ff[f]["in"], it * 4 + 2 * (u + 1))
                    for gs in range(2):
                        load_in(f, base, it * 2 + 2 + u, 2 * u + gs, gs)
            g = GROUPS - 1
            sp.wait_ge(ff[f]["in"], 2 * (g - 1))
            for gs in range(2):
                load_in(f, base, g, 2 * g + gs, gs)
            src = I["ffn_out"][0, f].rearrange("(k p) n -> p k n", p=P)
            for op in range(4):
                if op < 2:
                    sp.wait_ge(ff[f]["in"], 2 * (GROUPS - 1 + op))
                else:
                    sp.wait_ge(ff[f]["out"], 2 * (op - 1))
                for s in range(2):
                    sl = (base + 2 * GROUPS + 2 * op + s) % RING
                    dst = slot[sl].rearrange("p (k n) -> p k n", k=11)
                    sp.dma_start(dst, src[:, 11 * s:11 * s + 11, op * 256:(op + 1) * 256]).then_inc(w_in_ring[sl], 16)

            for tt in range(5):
                R = tile_rows(tt)
                sp.wait_ge(y_ev, 2 * (tt + 1))
                dst = O["y_p"][0, tt * P:(tt + 1) * P, :] if tt < 4 else O["y_s"].rearrange("b t n -> (b t) n")
                sp.dma_start(dst, YO[0:R, tt, :]).then_inc(y_out, 16)
            sp.wait_ge(y_out, 16 * 5)
            sp.wait_ge(st_out, 16 * n_states)
            sp.wait_ge(cpy, 16 * 5)

        @block.gpsimd
        def _(pool):
            cmp_rows = I["cache_cmp_kv"][0].rearrange("n (r s) x h d -> (n r) (s x h d)", s=16)
            slc_rows = I["cache_slc_kv"][0].rearrange("n (r s) x h d -> (n r) (s x h d)", s=4)
            pool.wait_ge(ix_ok, 2)
            for b in range(NB):
                if b == 1:
                    pool.wait_ge(x_ev, KD + 1)
                if b >= 2:
                    pool.wait_ge(t_done, 16 * (b - 1))
                for half in range(2):
                    pool.indirect_dma_start(PB[b % 2][:, half, :], None, cmp_rows,
                                            bass.IndirectOffsetOnAxis(ap=IXC[:, half, b:b + 1], axis=0))\
                        .then_inc(g_rows[b % 2], 16)
            def moved(dst, src, w):
                pool.dma_start(dst[:, 0:w - TS], src[:, TS:w]).then_inc(cpy, 16)

            pool.wait_ge(t_done, 16 * NB)
            for name, src, w in (("win_s", "cache_win_kv", 512), ("dil0_s", "cache_dil0_kv", 128),
                                 ("dil1_s", "cache_dil1_kv", 512), ("dil2_s", "cache_dil2_kv", 2048)):
                moved(O[name][0].rearrange("b t x h d -> b (t x h d)").rearrange("b (t c) -> b t c", c=256),
                      I[src][0].rearrange("b t x h d -> b t (x h d)"), w)
            moved(O["pool_s"][0], I["state_pool"][0], 15)

            def load_slc(b):
                for G in range(8):
                    pool.indirect_dma_start(KV[b % 2][:, G * 1024:(G + 1) * 1024], None, slc_rows,
                                            bass.IndirectOffsetOnAxis(ap=IXS[:, G, b:b + 1], axis=0))\
                        .then_inc(ld_kv[b % 2], 16)

            def load_wd(b):
                pool.dma_start(KWD[0], I["cache_win_kv"][0, b].rearrange("(p j) x h d -> p (j x h d)", j=4))\
                    .then_inc(ld_wd, 16)
                pool.dma_start(KD0, I["cache_dil0_kv"][0, b].rearrange("p x h d -> p (x h d)")).then_inc(ld_wd, 16)
                pool.dma_start(KWD[1], I["cache_dil1_kv"][0, b].rearrange("(p j) x h d -> p (j x h d)", j=4))\
                    .then_inc(ld_wd, 16)
                pool.dma_start(KWD[2], I["cache_dil2_kv"][0, b].rearrange("(p j) x h d -> p j (x h d)", j=16)[:, 0:4, :])\
                    .then_inc(ld_wd, 16)

            pool.wait_ge(pa["pv"], 3 * NU)
            pool.wait_ge(pa["oev"], NU)
            pool.wait_ge(po["ev"], 3)
            load_slc(0)
            load_wd(0)
            load_slc(1)
            for b in range(1, NB):
                pool.wait_ge(sa["pv"], NB + 3 * (b - 1) + 3)
                load_wd(b)
                if b + 1 < NB:
                    load_slc(b + 1)

        @block.tensor
        def _(pe):
            pe.sem_inc(m_done, 4)
            pe.wait_ge(ld["const"], 16)
            pe.wait_ge(ld["selp"], 16)
            pe.wait_ge(ix_f, 1)
            for s in range(10):
                mm = pe.matmul(PS[:, 7, s * NB:(s + 1) * NB], SELP[:, s, :], PTF[:, :], start=True, stop=True)
            mm.then_inc(ix_mm, 1)
            pe.wait_ge(ld["x"], 32)
            for k in range(KD):
                if k >= 6:
                    pe.wait_ge(x_ev, k - 5)
                for tt in range(4):
                    pe.transpose(PS[:, k % 6, tt * P:(tt + 1) * P], XIN[:, tt, k * P:(k + 1) * P], ident)
                pe.transpose(PS[:, 6, k * NS:(k + 1) * NS], XIN[0:NS, 4, k * P:(k + 1) * P], ident[0:NS, 0:NS])\
                    .then_inc(x_tr, 1)

            pe.wait_ge(x_ev, KD + 1)
            pe.wait_ge(ix_ok, 2)
            pe.wait_ge(ld["cw1"], 16)
            pe.wait_ge(ld["small"], SMALL)
            pe.wait_ge(hid_zero, 1)

            def tr_unit(b, par, kv, j, rows_ready):
                if rows_ready is not None:
                    pe.wait_ge(g_rows[par], rows_ready)
                n = b * 16 + (8 * kv + j + 1)
                pe.wait_ge(ev_act, n)
                pe.wait_ge(ev_dve, n)
                for s in range(2):
                    for half in range(2):
                        c = (2 * j + s) * 256 + kv * P
                        mm = pe.transpose(PS[:, j % 4, s * 256 + half * P:s * 256 + (half + 1) * P],
                                          PB[par][:, half, c:c + P], ident)
                mm.then_inc(t_done, 1)

            def hidden(b, kv, h, spread):
                m = 2 * kv + h
                pe.wait_ge(ev_act, b * 16 + (4 + 8 * kv + 8))
                pe.wait_ge(ev_dve, b * 16 + (4 + 8 * kv + 8))
                pe.wait_ge(silu_done, b * 4 + (m + 1))
                for c in range(2):
                    for s in range(8):
                        mm = pe.matmul(PS[:, 4 + m % 2, 0:255], CW1[:, kv, 8 * c + s, :], PTB[kv][:, h, s, c:c + 255],
                                       start=(c == 0 and s == 0), stop=(c == 1 and s == 7))
                        if (c, s) in spread:
                            spread[(c, s)]()
                mm.then_inc(m_done, 1)

            def second(b, m):
                pe.wait_ge(silu_done, b * 4 + (2 + m + 1))
                pe.wait_ge(w_copied, b * 4 + (m + 3))
                for ct in range(2):
                    c = (ct * 4 + m) * HD
                    mm = pe.matmul(PS[:, 6 + m % 2, c:c + HD], HIDC[:, m % 2, ct * P:(ct + 1) * P], W2[:, m // 2, :],
                                   start=True, stop=True)
                mm.then_inc(w_done, 1)

            def compress(b, par, count, last):
                T1u = lambda j: (lambda: tr_unit(b, par, 1, j, None))
                at = [(0, 1), (0, 4), (0, 7), (1, 2)]
                hidden(b, 0, 0, {at[n]: T1u(n) for n in range(4)})
                hidden(b, 0, 1, {**{at[n]: T1u(4 + n) for n in range(4)}, (1, 5): lambda: second(b, 0)})
                nxt = {} if last else {at[n]: (lambda n=n: tr_unit(b + 1, 1 - par, 0, n, count if n == 0 else None))
                                       for n in range(4)}
                hidden(b, 1, 0, {**nxt, (1, 5): lambda: second(b, 1)})
                nxt = {} if last else {at[n]: (lambda n=n: tr_unit(b + 1, 1 - par, 0, 4 + n, None)) for n in range(3)}
                hidden(b, 1, 1, {**nxt, (1, 5): lambda: second(b, 2)})
                if not last:
                    tr_unit(b + 1, 1 - par, 0, 7, None)
                second(b, 3)

            for j in range(8):
                tr_unit(0, 0, 0, j, 32 if j == 0 else None)
            with pe.Fori(0, NB // 2 - 1) as it:
                compress(it * 2, 0, it * 32 + 32, False)
                compress(it * 2 + 1, 1, it * 32 + 64, False)
            compress(NB - 2, 0, 32 * (NB // 2), False)
            compress(NB - 1, 1, 0, True)
            pe.wait_ge(ck_n, 1)
            pe.wait_ge(ev_act, 4 + 16 * NB)
            pe.wait_ge(ev_dve, 4 + 16 * NB)
            for b in range(NB):
                for ct in range(2):
                    n = 2 * b + ct
                    mm = pe.transpose(PS[:, n // 4, (n % 4) * P:(n % 4 + 1) * P], CK[:, n * P:(n + 1) * P], ident)
            mm.then_inc(ck_t, 1)
            pe.wait_ge(ck_ev, 1)
            pe.wait_ge(w_copied, 4 + 4 * NB)

            def rms(r):
                for k in range(KD):
                    pe.wait_ge(rs[r]["sq"], k + 1)
                    for hf in range(2):
                        mm = pe.matmul(PS[:, hf, 0:HALF], ones, HNk[:, k, hf * HALF:(hf + 1) * HALF],
                                       start=(k == 0), stop=(k == KD - 1))
                mm.then_inc(rs[r]["sum"], 1)

            def ring_wait(L, first):
                pe.wait_ge(w_in_ring[L % RING], first)

            def ffn(f, base, before):
                pe.sem_inc(ff[f]["mul"], 2)
                pe.sem_inc(ff[f]["res"], 2)
                pe.wait_ge(rs[2 * f]["hn"], KD)

                def group(g, sA, sB, count):
                    for c in range(2):
                        n = g * 2 + c
                        pe.wait_ge(ff[f]["mul"], n + 1)
                        for w, sl in enumerate((sA, sB)):
                            if c == 0:
                                pe.wait_ge(w_in_ring[sl], count[w])
                            wt = slot[sl][:, 0:KD * 256].rearrange("p (k n) -> p k n", k=KD)
                            for hf in range(2):
                                for k in range(KD):
                                    mm = pe.matmul(PS[:, 4 * c + 2 * w + hf, 0:HALF], wt[:, k, c * P:(c + 1) * P],
                                                   HNk[:, k, hf * HALF:(hf + 1) * HALF], start=(k == 0),
                                                   stop=(k == KD - 1))
                        mm.then_inc(ff[f]["in"], 1)

                with pe.Fori(0, (GROUPS - 1) // 2) as it:
                    for u in range(2):
                        s = [(base + 2 * u + w) % RING for w in range(2)]
                        group(it * 2 + u, s[0], s[1], [it * 16 + (before[x] + 16) for x in s])
                s = [(base + 2 * (GROUPS - 1) + w) % RING for w in range(2)]
                k0 = (GROUPS - 1) // 2
                group(GROUPS - 1, s[0], s[1], [before[x] + 16 * (k0 + 1) for x in s])
                done = [before[x] + 16 * (k0 + (x in s)) for x in range(RING)]
                pe.wait_ge(ff[f]["mul"], FCH + 2)
                for op in range(4):
                    s = [(base + 2 * GROUPS + 2 * op + w) % RING for w in range(2)]
                    for x in s:
                        done[x] += 16
                        pe.wait_ge(w_in_ring[x], done[x])
                    for c in range(2):
                        oc = 2 * op + c
                        pe.wait_ge(ff[f]["res"], oc + 1)
                        for hf in range(2):
                            for n in range(FCH):
                                wt = slot[s[n // 11]].rearrange("p (k n) -> p k n", k=11)
                                mm = pe.matmul(PS[:, 4 * c + hf, 0:HALF], wt[:, n % 11, c * P:(c + 1) * P],
                                               HID[:, n, hf * HALF:(hf + 1) * HALF], start=(n == 0),
                                               stop=(n == FCH - 1))
                        mm.then_inc(ff[f]["out"], 1)
                return done

            rms(0)
            done = ffn(0, 0, [0] * RING)
            pe.wait_ge(ff[0]["res"], 2 + KD)
            rms(1)
            pe.wait_ge(rs[1]["hn"], KD)
            for c in range(NCG):
                sl = (30 + c) % RING
                done[sl] += 16
                pe.wait_ge(w_in_ring[sl], done[sl])
                n = min(CG, COLS - c * CG)
                wt = slot[sl][:, 0:KD * n].rearrange("p (k n) -> p k n", k=KD)
                for tt in range(5):
                    x = c * 5 + tt
                    R = tile_rows(tt)
                    if x >= 8:
                        pe.wait_ge(pj_ev, x - 7)
                    for k in range(KD):
                        mm = pe.matmul(PS[0:R, x % 8, 0:n], HNk[:, k, tok(tt)], wt[:, k, :],
                                       start=(k == 0), stop=(k == KD - 1))
                    mm.then_inc(pj_mm, 1)
            pe.wait_ge(pj_ev, 5 * NCG)
            pe.wait_ge(qn, 5)
            pcol = {IT_SLC: C_SLCK, IT_WIN: C_WINK}
            pcol.update({IT_QB + g: C_QB + g * P for g in range(3)})
            pcol.update({IT_KB + g: C_KB + g * P for g in range(3)})
            pcol.update({IT_U + c: C_U + c * P for c in range(2)})
            for m in range(ITEMS):
                if m >= 4:
                    pe.wait_ge(qt_act, m - 3)
                    pe.wait_ge(qt_dve, m - 3)
                for tt in range(5):
                    R = tile_rows(tt)
                    src = QP[0:R, tt, m, :, :].rearrange("p h d -> p (h d)") if m < 3 else \
                        PROJ[0:R, tt, pcol[m]:pcol[m] + P]
                    dst = PS[:, 2 * (m % 4), tt * P:(tt + 1) * P] if tt < 4 else PS[:, 2 * (m % 4) + 1, 0:NS]
                    mm = pe.transpose(dst, src, ident[0:R, 0:R])
                mm.then_inc(qt_mm, 1)
            pe.wait_ge(qt_act, ITEMS)
            pe.wait_ge(qt_dve, ITEMS)
            pe.wait_ge(ld["poolst"], 16)
            for c in range(2):
                mm = pe.transpose(PS[:, 4, c * P:c * P + 120], PST[:, c * P:(c + 1) * P], ident[0:120, 0:120])
            mm.then_inc(po["st"], 1)
            pe.wait_ge(ld["pieces"], 16)
            for kv in range(2):
                for s in range(16):
                    c = s * 256 + kv * P
                    mm = pe.transpose(PS[:, kv, s * 32:(s + 1) * 32], PCS[:, c:c + P], ident[0:32, 0:32])
                mm.then_inc(pc["tr"], 1)
            pe.wait_ge(ld["cw1b"], 16)
            pe.wait_ge(pc["ev"], 2)
            for m in range(4):
                for c in range(2):
                    for s in range(8):
                        mm = pe.matmul(PS[:, 2, m * 32:m * 32 + 31], CW1B[:, m // 2, 8 * c + s, :],
                                       PTC[:, m // 2, m % 2, s, c:c + 31], start=(c == 0 and s == 0),
                                       stop=(c == 1 and s == 7))
            mm.then_inc(pc["mm"], 1)
            pe.wait_ge(pc["silu"], 2)
            for m in range(4):
                mm = pe.matmul(PS[0:31, 3, m * HD:(m + 1) * HD], HIDP[:, m, 0:31], W2[:, m // 2, :],
                               start=True, stop=True)
            mm.then_inc(pc["w"], 1)
            pe.wait_ge(po["dl"], 1)
            for c in range(2):
                for q in range(2):
                    r = slice(q * HD, (q + 1) * HD)
                    pe.matmul(PS[r, 5 + c, 0:TP], PW[r, c, :], DL[r, c, :], start=True, stop=True)
                    mm = pe.matmul(PS[r, 7, c * NS:(c + 1) * NS], PW[r, c, :],
                                   DLS[r, c, :, :].rearrange("p b t -> p (b t)"), start=True, stop=True)
            mm.then_inc(po["mm"], 1)
            pe.wait_ge(pc["n"], 1)
            pe.transpose(PS[:, 2, 0:31], CKP, ident[0:31, 0:31]).then_inc(pc["t"], 1)
            pe.wait_ge(pc["ev2"], 1)
            pe.wait_ge(po["ev"], 3)
            pe.wait_ge(po["stev"], 1)

            def scores(u):
                U = units[u]
                i = U["i"]
                if U["new"]:
                    if i:
                        pe.wait_ge(pa["cp"], i)
                    for hq in range(6):
                        r = slice(hq // 3 * HD, hq // 3 * HD + HD)
                        mm = pe.matmul(PS[:, 7, hq * 32:hq * 32 + 31], QT[r, hq % 3, i * P:(i + 1) * P],
                                       CKTP[r, 0:31], start=True, stop=True)
                        if hq % 3 == 2:
                            mm.then_inc(pa["cs"], 1)
                            pe.wait_ge(pa["cs"], 2 * i + hq // 3 + 1)
                for x, b in enumerate(U["br"]):
                    B = U["s0"] + x
                    if B >= 3:
                        pe.wait_ge(pa["sev"], B - 2)
                    r = slice(b["h"] * HD, b["h"] * HD + HD)
                    n = (i + 1 - b["j0"]) * P
                    pe.matmul(PS[:, B % 3, 0:n], QT[r, b["q"], i * P:(i + 1) * P],
                              QT[r, b["k"], b["j0"] * P:(i + 1) * P], start=True, stop=True).then_inc(pa["s"], 1)

            def turn(u, x):
                U = units[u]
                B = 3 * u + x
                if B >= 2:
                    pe.wait_ge(pa["tev"], B - 1)
                if U["nsa"] and x == 2:
                    pe.wait_ge(pa["cp"], U["i"] + 1)
                    pe.transpose(PS[0:31, 3 + B % 2, 0:P], SC[:, U["hq"], 0:31], ident).then_inc(pa["t"], 1)
                    return
                pe.wait_ge(pa["p"], u + 1)
                for y in range(U["i"] + 1 - U["br"][x]["j0"]):
                    mm = pe.transpose(PS[:, 3 + B % 2, y * P:(y + 1) * P], SB[:, u % 2, x, y * P:(y + 1) * P], ident)
                mm.then_inc(pa["t"], 1)

            def values(u, x):
                U = units[u]
                B = 3 * u + x
                if x == 0 and u >= 2:
                    pe.wait_ge(pa["oev"], u - 1)
                pe.wait_ge(pa["tev"], B + 1)
                if U["nsa"]:
                    e = U["hq"] % 2
                    out = PS[e * HD:(e + 1) * HD, 5 + u % 2, 0:P]
                else:
                    out = PS[U["h"] * HD:(U["h"] + 1) * HD, 5 + u % 2, x * P:(x + 1) * P]
                if U["nsa"] and x == 2:
                    pe.matmul(out, CVP[:, U["h"] * HD:(U["h"] + 1) * HD], PTS[0:31, B % 3, 0:P],
                              start=False, stop=True).then_inc(pa["pv"], 1)
                    return
                b = U["br"][x]
                n = U["i"] + 1 - b["j0"]
                for y in range(n):
                    mm = pe.matmul(out, VV[:, b["j0"] + y, b["v"]:b["v"] + HD], PTS[:, B % 3, y * P:(y + 1) * P],
                                   start=(y == 0 and (x == 0 or not U["nsa"])),
                                   stop=(y == n - 1 and not U["nsa"]))
                mm.then_inc(pa["pv"], 1)

            scores(0)
            for u in range(NU):
                if u + 1 < NU:
                    scores(u + 1)
                turn(u, 0)
                turn(u, 1)
                values(u, 0)
                turn(u, 2)
                values(u, 1)
                values(u, 2)

            pe.wait_ge(pa["oev"], NU)
            for b in range(NB):
                mm = pe.matmul(PS[0:24, 5, b * 18:(b + 1) * 18], const("tok_rows")[:, b * 24:(b + 1) * 24],
                               GT[0:NS, 4, :], start=True, stop=True)
            mm.then_inc(sa["gmm"], 1)
            pe.wait_ge(sa["q"], 1)
            pe.wait_ge(sa["gts"], 1)

            def front(u):
                U = su[u]
                if U["kind"] == "slc":
                    pe.wait_ge(ld_kv[U["b"] % 2], 128 * (U["b"] // 2 + 1))
                elif U["kind"] == "win":
                    pe.wait_ge(ld_wd, 64 * (U["b"] + 1))

                def kturn(x):
                    n = U["kt0"] + x
                    if n >= 2:
                        pe.wait_ge(sa["ktev"], n - 1)
                    for y, kt in enumerate(U["tc"][x][0]):
                        mm = pe.transpose(PS[:, n % 2, y * P:(y + 1) * P], kt, ident)
                    mm.then_inc(sa["kt"], 1)

                def kscore(x):
                    n, s = U["kt0"] + x, U["s0"] + x
                    w = len(U["tc"][x][0]) * P
                    pe.wait_ge(sa["ktev"], n + 1)
                    if s >= 2:
                        pe.wait_ge(sa["sev"], s - 1)
                    pe.matmul(PS[0:U["rows"], 2 + s % 2, 0:w], U["tc"][x][1], KTB(n)[:, 0:w],
                              start=True, stop=True).then_inc(sa["s"], 1)

                for x in range(len(U["tc"]) + 1):
                    if x < len(U["tc"]):
                        kturn(x)
                    if x:
                        kscore(x - 1)
                for x, (k, q, _, w, _) in enumerate(U["nc"]):
                    s = U["s0"] + len(U["tc"]) + x
                    if s >= 2:
                        pe.wait_ge(sa["sev"], s - 1)
                    pe.matmul(PS[0:U["rows"], 2 + s % 2, 0:w], q, k, start=True, stop=True).then_inc(sa["s"], 1)

            def back(u):
                U = su[u]
                R = U["rows"]
                pe.wait_ge(sa["w"], u + 1)
                if U["kind"] == "cmp":
                    mm = pe.matmul(PS[0:64, 7, 0:255], EXR[:, u % 2, :], U["buf"][:, 0:255], start=(u == 0),
                                   stop=(u == NB - 1))
                    if u == NB - 1:
                        mm.then_inc(sa["imp"], 1)
                for x, tiles in enumerate(U["pts"]):
                    n = U["pt0"] + x
                    if n >= 2:
                        pe.wait_ge(sa["ptev"], n - 1)
                    for y, (c, rows, _, _) in enumerate(tiles):
                        mm = pe.matmul(PS[0:rows, 4 + n % 2, y * R:(y + 1) * R], U["buf"][:, c:c + rows],
                                       DG[0:R, u % 2, 0:R], start=True, stop=True)
                    mm.then_inc(sa["pt"], 1)
                pe.wait_ge(sa["ptev"], U["pt0"] + len(U["pts"]))
                if u >= 2:
                    pe.wait_ge(sa["oev"], u - 1)
                flat = [(t, U["ptdst"][x][:, y * R:(y + 1) * R]) for x, ts in enumerate(U["pts"])
                        for y, t in enumerate(ts)]
                for g in range(3 if U["kind"] == "dil" else 1):
                    mine = [(t, pt) for t, pt in flat if t[3] == g]
                    for y, ((_, rows, v, _), pt) in enumerate(mine):
                        mm = pe.matmul(PS[:, out_bank(u), g * 8:g * 8 + R], v, pt[0:rows, :],
                                       start=(y == 0), stop=(y == len(mine) - 1))
                mm.then_inc(sa["pv"], 1)

            def pick():
                pe.wait_ge(sa["sel"], 1)
                for b in range(NB):
                    mm = pe.matmul(PS[0:24, 7, b * 64:(b + 1) * 64], const("to_rows")[:, b * 24:(b + 1) * 24],
                                   SEL[:, 0:64], start=True, stop=True)
                mm.then_inc(sa["selmm"], 1)

            front(0)
            for u in range(NB):
                if u + 1 < NB:
                    front(u + 1)
                back(u)
            pick()
            pe.wait_ge(sa["oev"], NB)
            front(NB)
            for u in range(NB, NSU):
                if u + 1 < NSU:
                    front(u + 1)
                back(u)

            pe.wait_ge(sa["ex"], 1)
            pe.wait_ge(sa["oev"], NSU)
            pe.wait_ge(sa["selm"], 1)
            for c in range(4):
                sl = (38 + c) % RING
                done[sl] += 16
                pe.wait_ge(w_in_ring[sl], done[sl])
                wt = slot[sl][:, 0:KD * 256].rearrange("p (k n) -> p k n", k=KD)
                for e in range(2):
                    oc = 2 * c + e
                    if oc >= 2:
                        pe.wait_ge(wo_ev, oc - 1)
                    for hf in range(2):
                        for k in range(KD):
                            mm = pe.matmul(PS[:, 4 * e + hf, 0:HALF], wt[:, k, e * P:(e + 1) * P],
                                           MIXT[:, k, hf * HALF:(hf + 1) * HALF], start=(k == 0), stop=(k == KD - 1))
                    mm.then_inc(wo_mm, 1)
            pe.wait_ge(wo_ev, KD)
            rms(2)
            ffn(1, 42, done)
            pe.wait_ge(ff[1]["res"], 2 + KD)
            for tt in range(5):
                R = tile_rows(tt)
                for hf in range(2):
                    x = 2 * tt + hf
                    if x >= 4:
                        pe.wait_ge(y_ev, x - 3)
                    for k in range(4):
                        mm = pe.transpose(PS[0:R, x % 4, k * P:(k + 1) * P], XT[:, 4 * hf + k, tok(tt)], ident)
                    mm.then_inc(y_tr, 1)

        @block.scalar
        def _(act):
            act.sem_inc(ev_act, 4)
            act.sem_inc(silu_done, 2)
            act.dma_start(PTI[:, :], I["page_table"].rearrange("b n -> n b")).then_inc(ld["small"], 16)
            act.dma_start(SELP, I["selp"].rearrange("p (s m) -> p s m", s=10)).then_inc(ld["selp"], 16)
            act.dma_start(NG[:, :, :], I["norm_gain"][0].rearrange("r (k p) -> p r k", p=P)).then_inc(ld["small"], 16)
            act.dma_start(QG[:, :, :].rearrange("p a d -> p (a d)"),
                          I["qk_gain"].rearrange("l a d -> l (a d)").to_broadcast([P, 6 * HD])).then_inc(ld["small"], 16)
            act.dma_start(B1[:, :], I["cmp_b1"][0].rearrange("v e -> e v")).then_inc(ld["small"], 16)
            act.dma_start(W2[:, :, :], I["cmp_w2"][0].rearrange("v e d -> e v d")).then_inc(ld["small"], 16)
            for q in range(2):
                act.dma_start(PW[q * HD:(q + 1) * HD, :, :],
                              I["pool_w"][0].rearrange("(c q) i e -> q i c e", q=2)[q]).then_inc(ld["small"], 16)
            act.dma_start(PSC[:, :], I["pool_scale"][0].rearrange("(c p) -> p c", p=P)).then_inc(ld["small"], 16)
            act.wait_ge(ld["small"], SMALL)
            act.wait_ge(ld["const"], 16)

            def evac(b, kv, j):
                n = 8 * kv + j
                act.wait_ge(t_done, b * 16 + (n + 1))
                act.wait_ge(m_done, b * 4 + (2 * kv + 2))
                for s in range(2):
                    last = act.activation(PTB[kv][s * HD:(s + 1) * HD, 0, j, :], PS[0:HD, j % 4, s * 256:(s + 1) * 256],
                                          ACT.Copy)
                last.then_inc(ev_act, 1)

            def silu(b, m):
                act.wait_ge(m_done, b * 4 + (4 + m + 1))
                act.wait_ge(w_done, b * 4 + (m + 1))
                act.activation(HIDC[:, m % 2, 0:255], PS[:, 4 + m % 2, 0:255], ACT.Silu, bias=B1[:, m // 2:m // 2 + 1])\
                    .then_inc(silu_done, 1)

            def compress(b, last):
                for j in range(4):
                    evac(b, 1, j)
                silu(b, 0)
                for j in range(4, 8):
                    evac(b, 1, j)
                silu(b, 1)
                if not last:
                    for j in range(4):
                        evac(b + 1, 0, j)
                silu(b, 2)
                if not last:
                    for j in range(4, 7):
                        evac(b + 1, 0, j)
                silu(b, 3)
                if not last:
                    evac(b + 1, 0, 7)

            act.sem_inc(w_done, 2)
            act.wait_ge(hid_zero, 1)
            for j in range(8):
                evac(0, 0, j)
            with act.Fori(0, NB - 1) as it:
                compress(it, False)
            compress(NB - 1, True)
            act.wait_ge(ck_ss, 1)
            act.activation(SSC, SSC, ACT.Sqrt, bias=eps, scale=1.0 / HD).then_inc(ck_sq, 1)

            def rms(r):
                act.wait_ge(rs[r]["sum"], 1)
                act.activation(RB, PS[:, 0:2, 0:HALF], ACT.Sqrt, bias=eps, scale=1.0 / D).then_inc(rs[r]["root"], 1)

            def ffn(f):
                with act.Fori(0, FCH // 2) as it:
                    for u in range(2):
                        act.wait_ge(ff[f]["in"], it * 2 + u + 1)
                        act.wait_ge(ff[f]["mul"], it * 2 + u + 1)
                        act.activation(GB[:, u, :, :], PS[:, 4 * u:4 * u + 2, 0:HALF], ACT.Silu).then_inc(ff[f]["silu"], 1)

            rms(0)
            act.wait_ge(rs[0]["hn"], KD)
            ffn(0)
            rms(1)
            for x in range(5 * NCG):
                c, tt = x // 5, x % 5
                R, n = tile_rows(tt), min(CG, COLS - c * CG)
                act.wait_ge(pj_mm, x + 1)
                act.activation(PROJ[0:R, tt, c * CG:c * CG + n], PS[0:R, x % 8, 0:n], ACT.Copy).then_inc(pj_ev, 1)
            act.wait_ge(pj_ev, 5 * NCG)
            for rr, ts in ((P, slice(0, 4)), (NS, slice(4, 5))):
                act.activation(GT[0:rr, ts, :], PROJ[0:rr, ts, C_G:C_G + 18], ACT.Sigmoid).then_inc(cp_act, 1)
                for at, c, n in ((0, C_SLCV, P), (P, C_WINV, P), (256, C_VB, 384)):
                    act.activation(VV[0:rr, ts, at:at + n], PROJ[0:rr, ts, c:c + n], ACT.Copy).then_inc(cp_act, 1)
            act.wait_ge(hn_ss, 1)
            act.activation(SS[:, 0:4, :], SS[:, 0:4, :], ACT.Sqrt, bias=eps, scale=1.0 / HD)
            act.activation(SS[0:NS, 4, :], SS[0:NS, 4, :], ACT.Sqrt, bias=eps[0:NS, :], scale=1.0 / HD)\
                .then_inc(hn_rt, 1)
            for m in range(ITEMS):
                act.wait_ge(qt_mm, m + 1)
                if m == 0:
                    act.wait_ge(ck_ev, 1)
                dst = QT[:, m, 0:TP] if m < IT_U else UT[:, m - IT_U, 16:528]
                act.activation(dst, PS[:, 2 * (m % 4), :], ACT.Copy).then_inc(qt_act, 1)
            for kv in range(2):
                act.wait_ge(pc["tr"], kv + 1)
                for h in range(2):
                    for s in range(2):
                        src = PS[h * HD:(h + 1) * HD, kv, :].rearrange("p (s u n) -> p s u n", s=8, u=2)[:, :, s, :]
                        last = act.activation(PTC[s * HD:(s + 1) * HD, kv, h, :, :], src, ACT.Copy)
                last.then_inc(pc["ev"], 1)
            act.wait_ge(pc["mm"], 1)
            for kv in range(2):
                act.activation(HIDP[:, 2 * kv:2 * kv + 2, 0:31],
                               PS[:, 2, 64 * kv:64 * kv + 64].rearrange("p (q n) -> p q n", q=2)[:, :, 0:31],
                               ACT.Silu, bias=B1[:, kv:kv + 1]).then_inc(pc["silu"], 1)
            act.wait_ge(pc["ss"], 1)
            act.activation(SSP, SSP, ACT.Sqrt, bias=eps[0:31, :], scale=1.0 / HD).then_inc(pc["rt"], 1)
            act.wait_ge(po["mm"], 1)
            for c in range(2):
                act.activation(MIXT[:, 6 + c, 0:TP], PS[:, 5 + c, :], ACT.Copy, scale=PSC[:, c:c + 1]).then_inc(po["ev"], 1)
                last = act.activation(MIXT[:, 6 + c, TP:T], PS[:, 7, c * NS:(c + 1) * NS], ACT.Copy,
                                      scale=PSC[:, c:c + 1])
            last.then_inc(po["ev"], 1)

            def exps(u):
                U = units[u]
                i = U["i"]
                if U["new"]:
                    act.wait_ge(pa["cnb"], i + 1)
                    act.activation(SC[:, :, 0:31], SC[:, :, 0:31], ACT.Exp, scale=SCALE).then_inc(pa["cexp"], 1)
                act.wait_ge(pa["nb"], u + 1)
                for x, b in enumerate(U["br"]):
                    n = (i + 1 - b["j0"]) * P
                    last = act.activation(SB[:, u % 2, x, 0:n], SB[:, u % 2, x, 0:n], ACT.Exp,
                                          bias=NBI[:, u % 2, x if U["nsa"] else 0:(x if U["nsa"] else 0) + 1],
                                          scale=SCALE, accum_out=DEN[:, u % 2, x:x + 1])
                last.then_inc(pa["exp"], 1)

            def tevac(u):
                U = units[u]
                for x in range(3):
                    B = 3 * u + x
                    act.wait_ge(pa["t"], B + 1)
                    if B >= 3:
                        act.wait_ge(pa["pv"], B - 2)
                    if U["nsa"] and x == 2:
                        act.activation(PTS[0:31, B % 3, 0:P], PS[0:31, 3 + B % 2, 0:P], ACT.Copy).then_inc(pa["tev"], 1)
                    else:
                        n = (U["i"] + 1 - U["br"][x]["j0"]) * P
                        act.activation(PTS[:, B % 3, 0:n], PS[:, 3 + B % 2, 0:n], ACT.Copy).then_inc(pa["tev"], 1)

            exps(0)
            for u in range(NU):
                if u + 1 < NU:
                    exps(u + 1)
                tevac(u)

            def front(u):
                U = su[u]
                for x in range(len(U["tc"])):
                    n = U["kt0"] + x
                    w = len(U["tc"][x][0]) * P
                    act.wait_ge(sa["kt"], n + 1)
                    if n >= 3:
                        act.wait_ge(sa["s"], score_of[n - 3] + 1)
                    act.activation(KTB(n)[:, 0:w], PS[:, n % 2, 0:w], ACT.Copy).then_inc(sa["ktev"], 1)

            def expo(u):
                U = su[u]
                R = U["rows"]
                act.wait_ge(sa["nb"], u + 1)
                n = 255 if U["kind"] == "cmp" else U["buf"].shape[1]
                act.activation(U["buf"][:, 0:n], U["buf"][:, 0:n], ACT.Exp, bias=SNB[0:R, u % 2:u % 2 + 1],
                               scale=SCALE, accum_out=SDEN[0:R, u % 2, 0:1]).then_inc(sa["exp"], 1)

            def pev(u):
                U = su[u]
                R = U["rows"]
                for x, tiles in enumerate(U["pts"]):
                    n = U["pt0"] + x
                    rows = tiles[0][1]
                    act.wait_ge(sa["pt"], n + 1)
                    if u >= 3:
                        act.wait_ge(sa["pv"], u - 1 if U["kind"] == "cmp" else u - 2)
                    elif u == 2:
                        act.wait_ge(sa["pv"], 1)
                    w = len(tiles) * R
                    act.activation(U["ptdst"][x][0:rows, 0:w], PS[0:rows, 4 + n % 2, 0:w], ACT.Copy)\
                        .then_inc(sa["ptev"], 1)

            score_of = {U["kt0"] + x: U["s0"] + x for U in su for x in range(len(U["tc"]))}
            front(0)
            for u in range(NSU):
                expo(u)
                if u + 1 < NSU and u != NB - 1:
                    front(u + 1)
                pev(u)
                if u == NB - 1:
                    front(u + 1)

            rms(2)
            act.wait_ge(rs[2]["hn"], KD)
            ffn(1)
            for x in range(1, 10, 2):
                R = tile_rows(x // 2)
                act.wait_ge(y_tr, x + 1)
                act.wait_ge(y_ev, x)
                act.activation(YO[0:R, x // 2, 512:1024], PS[0:R, x % 4, :], ACT.Copy).then_inc(y_ev, 1)

        @block.vector
        def _(dve):
            n_link = [0]

            def link(ins):
                n_link[0] += 1
                ins.then_inc(d_ch, 1)
                dve.wait_ge(d_ch, n_link[0])

            V = nc.vector
            dve.sem_inc(ev_dve, 4)
            dve.sem_inc(w_copied, 4)
            dve.wait_ge(ld["small"], SMALL)
            dve.wait_ge(ld["const"], 16)
            V.tensor_copy(PTF[:, :], PTI[:, :]).then_inc(ix_f, 1)
            dve.wait_ge(ix_mm, 1)
            V.tensor_scalar(IXC[:, :, :], PS[:, 7, 0:2 * NB].rearrange("p (s b) -> p s b", s=2), 8.0, const("p8"),
                            ALU.mult, ALU.add).then_inc(ix_ok, 1)
            V.tensor_scalar(IXS[:, :, :], PS[:, 7, 2 * NB:10 * NB].rearrange("p (s b) -> p s b", s=8), 32.0,
                            const("p32"), ALU.mult, ALU.add).then_inc(ix_ok, 1)
            for k in range(KD):
                dve.wait_ge(x_tr, k + 1)
                V.tensor_copy(XT[:, k, 0:TP], PS[:, k % 6, :]).then_inc(x_ev, 1)
            V.tensor_copy(XT[:, :, TP:T], PS[:, 6, 0:KD * NS].rearrange("p (k t) -> p k t", k=KD)).then_inc(x_ev, 1)
            V.memset(HIDC[:, :, 255:256], 0.0).then_inc(hid_zero, 1)

            def evac(b, kv, j):
                n = 8 * kv + j
                dve.wait_ge(t_done, b * 16 + (n + 1))
                dve.wait_ge(m_done, b * 4 + (2 * kv + 2))
                for s in range(2):
                    last = V.tensor_copy(PTB[kv][s * HD:(s + 1) * HD, 1, j, :],
                                         PS[HD:P, j % 4, s * 256:(s + 1) * 256])
                last.then_inc(ev_dve, 1)

            CKb = CK.rearrange("p (b c n) -> p b c n", b=NB, c=2)

            def rows_out(b, m):
                dve.wait_ge(w_done, b * 4 + (2 + m + 1))
                src = PS[:, 6 + m % 2, :].rearrange("p (c q d) -> p c q d", c=2, q=4)[:, :, m, :]
                dst = CKb if m < 2 else CV[:, :, :, :]
                h = m % 2
                bb = bass.ds(b, 1) if not isinstance(b, int) else slice(b, b + 1)
                V.tensor_copy(dst[:, bb, :, h * HD:(h + 1) * HD].rearrange("p a c d -> p (a c) d"), src)\
                    .then_inc(w_copied, 1)

            def compress(b, last):
                for j in range(8):
                    evac(b, 1, j)
                rows_out(b, 0)
                if not last:
                    for j in range(4):
                        evac(b + 1, 0, j)
                rows_out(b, 1)
                if not last:
                    for j in range(4, 7):
                        evac(b + 1, 0, j)
                rows_out(b, 2)
                if not last:
                    evac(b + 1, 0, 7)
                rows_out(b, 3)

            for j in range(8):
                evac(0, 0, j)
            with dve.Fori(0, NB - 1) as it:
                compress(it, False)
            compress(NB - 1, True)
            dve.wait_ge(w_copied, 4 + 4 * NB)
            link(V.tensor_tensor(CKS, CK, CK, ALU.mult))
            V.tensor_reduce(SSC, CKS.rearrange("p (n d) -> p n d", d=HD), AX.X, ALU.add).then_inc(ck_ss, 1)
            dve.wait_ge(ck_sq, 1)
            link(V.reciprocal(SSC, SSC))
            ck3 = CK.rearrange("p (n d) -> p n d", d=HD)
            link(V.tensor_tensor(ck3, ck3, SSC.unsqueeze(2).to_broadcast([P, 32, HD]), ALU.mult))
            V.tensor_tensor(ck3, ck3, QG[:, 1:2, :].to_broadcast([P, 32, HD]), ALU.mult).then_inc(ck_n, 1)
            dve.wait_ge(ck_t, 1)
            for n in range(4):
                last = V.tensor_copy(CKT[:, 2 * n:2 * n + 2, :], PS[:, n, :].rearrange("p (b c) -> p b c", b=2))
            last.then_inc(ck_ev, 1)

            def rms(r):
                for k in range(KD):
                    V.tensor_tensor(HNk[:, k, :], XT[:, k, :], XT[:, k, :], ALU.mult).then_inc(rs[r]["sq"], 1)
                dve.wait_ge(rs[r]["root"], 1)
                link(V.reciprocal(RB, RB))
                for k in range(KD):
                    V.scalar_tensor_tensor(HNk[:, k, :].rearrange("p (h t) -> p h t", h=2),
                                           XT[:, k, :].rearrange("p (h t) -> p h t", h=2), NG[:, r, k:k + 1], RB,
                                           ALU.mult, ALU.mult).then_inc(rs[r]["hn"], 1)

            def ffn(f):
                with dve.Fori(0, FCH // 2) as it:
                    for u in range(2):
                        dve.wait_ge(ff[f]["silu"], it * 2 + u + 1)
                        V.tensor_tensor(HID[:, bass.ds(it * 2 + u, 1), :].rearrange("p a (h t) -> p (a h) t", h=2),
                                        GB[:, u, :, :], PS[:, 4 * u + 2:4 * u + 4, 0:HALF], ALU.mult)\
                            .then_inc(ff[f]["mul"], 1)
                for oc in range(KD):
                    dve.wait_ge(ff[f]["out"], oc + 1)
                    x = XT[:, oc, :].rearrange("p (h t) -> p h t", h=2)
                    V.scalar_tensor_tensor(x, PS[:, 4 * (oc % 2):4 * (oc % 2) + 2, 0:HALF], 0.5, x, ALU.mult, ALU.add)\
                        .then_inc(ff[f]["res"], 1)

            dve.wait_ge(m_done, 4 + 4 * NB)
            rms(0)
            ffn(0)
            dve.wait_ge(ff[0]["res"], 2 + KD)
            rms(1)
            dve.wait_ge(pj_ev, 5 * NCG)
            for tt in range(5):
                R = tile_rows(tt)
                for n, (c, nh, _, off) in enumerate(SECTIONS):
                    x = PROJ[0:R, tt, c:c + nh * HD]
                    link(V.tensor_tensor(SQT[0:R, 0, 0:nh * HD], x, x, ALU.mult))
                    ins = V.tensor_reduce(SS[0:R, tt, off:off + nh],
                                          SQT[0:R, 0, 0:nh * HD].rearrange("p (n d) -> p n d", d=HD), AX.X, ALU.add)
                    if tt == 4 and n == len(SECTIONS) - 1:
                        ins.then_inc(hn_ss, 1)
                    else:
                        link(ins)
            dve.wait_ge(hn_rt, 1)
            link(V.reciprocal(SS[:, 0:4, :], SS[:, 0:4, :]))
            link(V.reciprocal(SS[0:NS, 4, :], SS[0:NS, 4, :]))
            for tt in range(5):
                R = tile_rows(tt)
                for n, (c, nh, g, off) in enumerate(SECTIONS):
                    x = PROJ[0:R, tt, c:c + nh * HD].rearrange("p (n d) -> p n d", d=HD)
                    link(V.tensor_tensor(x, x, SS[0:R, tt, off:off + nh].unsqueeze(2).to_broadcast([R, nh, HD]),
                                         ALU.mult))
                    gain = QG[0:R, g:g + 1, :]
                    if n == 0:
                        for h in range(2):
                            V.tensor_tensor(QP[0:R, tt, :, h, :], x[:, 3 * h:3 * h + 3, :],
                                            gain.to_broadcast([R, 3, HD]), ALU.mult)
                    else:
                        ins = V.tensor_tensor(x, x, gain.to_broadcast([R, nh, HD]), ALU.mult)
                ins.then_inc(qn, 1)
            V.memset(UT[:, :, 0:16], 0.0).then_inc(po["zero"], 1)
            for m in range(ITEMS):
                dve.wait_ge(qt_mm, m + 1)
                dst = QT[:, m, TP:T] if m < IT_U else UTS[:, m - IT_U, :, 15:19]
                src = PS[:, 2 * (m % 4) + 1, 0:NS]
                if m >= IT_U:
                    src = src.rearrange("p (b t) -> p b t", b=NB)
                V.tensor_copy(dst, src).then_inc(qt_dve, 1)
            dve.wait_ge(po["st"], 1)
            for c in range(2):
                last = V.tensor_copy(UTS[:, c, :, 0:15], PS[:, 4, c * P:c * P + 120].rearrange("p (b t) -> p b t", b=NB))
            last.then_inc(po["stev"], 1)
            dve.wait_ge(po["stev"], 1)
            dve.wait_ge(po["zero"], 1)
            dve.wait_ge(qt_act, ITEMS)
            dve.wait_ge(qt_dve, ITEMS)
            dve.wait_ge(qt_mm, ITEMS)
            dve.wait_ge(cp_act, 8)
            dve.wait_ge(st_cmp, 16)
            dve.wait_ge(st_out, 16 * N_STATES)

            def windows(u, a, b_, dl, n0, n, head, nt):
                src, dst = u, a
                for step, w in enumerate((2, 4, 8, 16)):
                    sh = w // 2
                    link(V.tensor_tensor(dst[..., w - 1:n], src[..., w - 1:n], src[..., w - 1 - sh:n - sh], ALU.add))
                    c, q = step // 2, step % 2
                    r = slice(q * HD, (q + 1) * HD)
                    pw = const("pool_w")[r, c:c + 1]
                    link(V.scalar_tensor_tensor(dl[r, c], dst[r, c][..., n0:n], pw, u[r, c][..., n0:n],
                                                ALU.mult, ALU.subtract))
                    if head:
                        hd = const("pool_head")[r, c * 16:(c + 1) * 16]
                        link(V.tensor_tensor(PHD[r, c, :], dst[r, c, n0:n0 + 16], hd, ALU.mult))
                        link(V.tensor_tensor(dl[r, c, 0:16], PHD[r, c, :], u[r, c, n0:n0 + 16], ALU.subtract))
                    src, dst = dst, (b_ if dst is a else a)

            windows(UT, T1, T2, DL, 16, 528, True, TP)
            windows(UTS, T1S, T2S, DLS, 15, 19, False, NS)
            V.sem_inc(po["dl"], 1)
            dve.wait_ge(pc["w"], 1)
            V.tensor_copy(CVP, PS[0:31, 3, 2 * HD:4 * HD])
            link(V.tensor_copy(CKP, PS[0:31, 3, 0:2 * HD]))
            link(V.tensor_tensor(CKPS, CKP, CKP, ALU.mult))
            V.tensor_reduce(SSP, CKPS.rearrange("p (n d) -> p n d", d=HD), AX.X, ALU.add).then_inc(pc["ss"], 1)
            dve.wait_ge(pc["rt"], 1)
            link(V.reciprocal(SSP, SSP))
            kp = CKP.rearrange("p (n d) -> p n d", d=HD)
            link(V.tensor_tensor(kp, kp, SSP.unsqueeze(2).to_broadcast([31, 2, HD]), ALU.mult))
            V.tensor_tensor(kp, kp, QG[0:31, 1:2, :].to_broadcast([31, 2, HD]), ALU.mult).then_inc(pc["n"], 1)
            dve.wait_ge(pc["t"], 1)
            V.tensor_copy(CKTP[:, 0:31], PS[:, 2, 0:31]).then_inc(pc["ev2"], 1)

            def cmp_scores(i):
                dve.wait_ge(pa["cs"], 2 * i + 2)
                if i:
                    dve.wait_ge(pa["t"], 3 * (8 * (i - 1) + 5) + 3)
                s = SC[:, :, 0:31]
                add = const("cmp_add")[:, i * 32:i * 32 + 31].unsqueeze(1).to_broadcast([P, 6, 31])
                keep = const("cmp_keep")[:, i * 32:i * 32 + 31].unsqueeze(1).to_broadcast([P, 6, 31])
                link(V.tensor_tensor(s, PS[:, 7, 0:192].rearrange("p (h n) -> p h n", h=6)[:, :, 0:31], add, ALU.add))
                link(V.tensor_reduce(CMX, s, AX.X, ALU.max))
                V.tensor_tensor(s, s, CMX.unsqueeze(2).to_broadcast([P, 6, 31]), ALU.subtract).then_inc(pa["cnb"], 1)
                dve.wait_ge(pa["cexp"], i + 1)
                link(V.tensor_tensor(s, s, keep, ALU.mult))
                link(V.tensor_reduce(CDN, s, AX.X, ALU.add))
                link(V.tensor_scalar(CDN, CDN, 1.0e-30, None, ALU.max))
                link(V.reciprocal(CDN, CDN))
                link(V.tensor_tensor(CWT, CDN, GT[:, i, :].rearrange("p (h c) -> p h c", c=3)[:, :, 0], ALU.mult))
                V.tensor_tensor(s, s, CWT.unsqueeze(2).to_broadcast([P, 6, 31]), ALU.mult).then_inc(pa["cp"], 1)

            def lift(u):
                U = units[u]
                i = U["i"]
                if U["new"]:
                    cmp_scores(i)
                if u >= 2:
                    dve.wait_ge(pa["t"], 3 * (u - 2) + 3)
                for x, b in enumerate(U["br"]):
                    B = U["s0"] + x
                    dve.wait_ge(pa["s"], B + 1)
                    n = i - b["j0"]
                    s = SB[:, u % 2, x, :]
                    if n:
                        src, dst = PS[:, B % 3, 0:n * P], s[:, 0:n * P]
                        if b["off"] is None:
                            V.tensor_copy(dst, src)
                        else:
                            m = const(b["off"]).unsqueeze(1).to_broadcast([P, n, P])
                            V.tensor_tensor(dst.rearrange("p (j c) -> p j c", c=P),
                                            src.rearrange("p (j c) -> p j c", c=P), m, ALU.add)
                    V.tensor_tensor(s[:, n * P:(n + 1) * P], PS[:, B % 3, n * P:(n + 1) * P], const(b["diag"]),
                                    ALU.add).then_inc(pa["sev"], 1)
                dve.wait_ge(pa["sev"], U["s0"] + len(U["br"]))
                nb = NBI[:, u % 2, :]
                if U["nsa"]:
                    link(V.tensor_reduce(MX[:, u % 2, 0:2], SB[:, u % 2, 0:2, 0:(i + 1) * P], AX.X, ALU.max))
                    V.tensor_scalar(nb[:, 0:2], MX[:, u % 2, 0:2], -SCALE, None, ALU.mult).then_inc(pa["nb"], 1)
                else:
                    for x, b in enumerate(U["br"]):
                        ins = V.tensor_reduce(MX[:, u % 2, x:x + 1], SB[:, u % 2, x, 0:(i + 1 - b["j0"]) * P], AX.X,
                                              ALU.max)
                    link(ins)
                    link(V.tensor_reduce(MX1[:, u % 2:u % 2 + 1], MX[:, u % 2, :], AX.X, ALU.max))
                    V.tensor_scalar(nb[:, 0:1], MX1[:, u % 2:u % 2 + 1], -SCALE, None, ALU.mult).then_inc(pa["nb"], 1)

            def weigh(u):
                U = units[u]
                i = U["i"]
                dve.wait_ge(pa["exp"], u + 1)
                w, d = WT[:, u % 2, :], DEN[:, u % 2, :]
                if U["nsa"]:
                    link(V.reciprocal(w[:, 0:2], d[:, 0:2]))
                    link(V.tensor_tensor(w[:, 0:2], w[:, 0:2], GT[:, i, U["hq"] * 3 + 1:U["hq"] * 3 + 3], ALU.mult))
                else:
                    link(V.tensor_reduce(w[:, 2:3], d, AX.X, ALU.add))
                    link(V.reciprocal(w[:, 0:1], w[:, 2:3]))
                for x, b in enumerate(U["br"]):
                    n = (i + 1 - b["j0"]) * P
                    y = x if U["nsa"] else 0
                    ins = V.tensor_scalar(SB[:, u % 2, x, 0:n], SB[:, u % 2, x, 0:n], w[:, y:y + 1], None, ALU.mult)
                ins.then_inc(pa["p"], 1)

            def out(u):
                U = units[u]
                c = slice(U["i"] * P, (U["i"] + 1) * P)
                dve.wait_ge(pa["pv"], 3 * u + 3)
                if U["nsa"]:
                    r = slice(U["hq"] % 2 * HD, U["hq"] % 2 * HD + HD)
                    V.tensor_copy(MIXT[r, U["hq"] // 2, c], PS[r, 5 + u % 2, 0:P]).then_inc(pa["oev"], 1)
                else:
                    r = slice(U["h"] * HD, (U["h"] + 1) * HD)
                    V.tensor_copy(MIXT[r, 3:6, c], PS[r, 5 + u % 2, 0:3 * P].rearrange("p (g t) -> p g t", g=3))\
                        .then_inc(pa["oev"], 1)

            lift(0)
            for u in range(NU):
                if u + 1 < NU:
                    lift(u + 1)
                weigh(u)
                if u >= 1:
                    out(u - 1)
            out(NU - 1)

            dve.wait_ge(pa["oev"], NU)
            link(V.memset(QA[:, :, :], 0.0))
            link(V.memset(QD[:, :, :, :], 0.0))
            for h in range(2):
                r = slice(h * HD, (h + 1) * HD)
                for g in range(3):
                    V.tensor_copy(QA[r, :, (h * 3 + g) * TS:(h * 3 + g + 1) * TS],
                                  QT[r, g, TP:T].rearrange("p (b t) -> p b t", b=NB))
                    ins = V.tensor_copy(QD[r, g, :, h * TS:(h + 1) * TS],
                                        QT[r, IT_QB + g, TP:T].rearrange("p (b t) -> p b t", b=NB))
            V.memset(SCS[:, :, 255:256], 0.0).then_inc(sa["q"], 1)
            dve.wait_ge(sa["gmm"], 1)
            link(V.tensor_tensor(GX, PS[0:24, 5, 0:144].rearrange("p (b c) -> p b c", b=NB),
                                 const("gate_pick").unsqueeze(1).to_broadcast([24, NB, 18]), ALU.mult))
            V.tensor_reduce(GS, GX.rearrange("p b (h c) -> p b c h", c=3), AX.X, ALU.add).then_inc(sa["gts"], 1)
            dve.wait_ge(sa["gts"], 1)
            n_sev = [0]

            def front(u):
                U = su[u]
                R = U["rows"]
                kind_gap = {"cmp": 2, "slc": 3, "win": 3, "dil": 3}[U["kind"]]
                if u >= (2 if U["kind"] == "cmp" else NB + 3):
                    dve.wait_ge(sa["pv"], u - kind_gap + 1)
                for x, (tl, _, c, mask) in enumerate(U["tc"]):
                    s = U["s0"] + x
                    w = len(tl) * P
                    dve.wait_ge(sa["s"], s + 1)
                    src, dst = PS[0:R, 2 + s % 2, 0:w], U["buf"][:, c:c + w]
                    if mask[0] == "sel":
                        m = SELM[:, U["b"] * 64 + 8 * mask[1]:U["b"] * 64 + 8 * mask[1] + 8]
                        m = m.unsqueeze(1).unsqueeze(3).to_broadcast([24, 4, 8, 16])
                        V.tensor_tensor(dst.rearrange("p (j a r) -> p j a r", j=4, a=8),
                                        src.rearrange("p (j a r) -> p j a r", j=4, a=8), m, ALU.add)\
                            .then_inc(sa["sev"], 1)
                    else:
                        V.tensor_tensor(dst, src, const(mask[1]), ALU.add).then_inc(sa["sev"], 1)
                for x, (_, _, c, w, mask) in enumerate(U["nc"]):
                    s = U["s0"] + len(U["tc"]) + x
                    dve.wait_ge(sa["s"], s + 1)
                    src, dst = PS[0:R, 2 + s % 2, 0:w], U["buf"][:, c:c + w]
                    if mask is None:
                        V.tensor_copy(dst, src).then_inc(sa["sev"], 1)
                    else:
                        V.tensor_tensor(dst, src, const(mask[0])[:, mask[1] * 32:mask[1] * 32 + 32], ALU.add)\
                            .then_inc(sa["sev"], 1)
                dve.wait_ge(sa["sev"], U["s0"] + len(U["tc"]) + len(U["nc"]))
                n = 255 if U["kind"] == "cmp" else U["buf"].shape[1]
                link(V.tensor_reduce(SMX[0:R, u % 2:u % 2 + 1], U["buf"][:, 0:n], AX.X, ALU.max))
                V.tensor_scalar(SNB[0:R, u % 2:u % 2 + 1], SMX[0:R, u % 2:u % 2 + 1], -SCALE, None, ALU.mult)\
                    .then_inc(sa["nb"], 1)

            def weights(u):
                U = su[u]
                R = U["rows"]
                dve.wait_ge(sa["exp"], u + 1)
                w = SWT[0:R, u % 2:u % 2 + 1]
                link(V.reciprocal(w, SDEN[0:R, u % 2, 0:1]))
                if u >= 2:
                    dve.wait_ge(sa["pv"], u - 1)
                if U["kind"] == "cmp":
                    link(V.tensor_scalar(EXR[:, u % 2, :], const("sum_heads")[:, U["b"] * 64:(U["b"] + 1) * 64], w, None,
                                         ALU.mult))
                if U["kind"] != "dil":
                    br = ("cmp", "slc", "win").index(U["kind"])
                    link(V.tensor_tensor(w, w, GS[:, U["b"], br:br + 1], ALU.mult))
                V.tensor_scalar(DG[0:R, u % 2, 0:R], ident[0:R, 0:R], w, None, ALU.mult).then_inc(sa["w"], 1)

            def outs(u):
                U = su[u]
                dve.wait_ge(sa["pv"], u + 1)
                src = PS[:, out_bank(u), 0:24]
                if U["kind"] == "cmp":
                    V.tensor_copy(U["out"], src).then_inc(sa["oev"], 1)
                elif U["kind"] == "dil":
                    V.tensor_copy(U["out"], src.rearrange("p (g r) -> p g r", g=3)).then_inc(sa["oev"], 1)
                else:
                    dve.wait_ge(sa["oev"], u)
                    V.tensor_tensor(U["out"], src, U["out"], ALU.add).then_inc(sa["oev"], 1)

            def choose():
                dve.wait_ge(sa["imp"], 1)
                V.memset(SCR[:, 64:65], 0.0)
                link(V.memset(IM[:, 255:256], 0.0))
                link(V.tensor_copy(IM[:, 0:255], PS[0:64, 7, 0:255]))
                link(V.tensor_reduce(SCR[:, 0:64], IM.rearrange("p (j c) -> p j c", c=4), AX.X, ALU.add))
                link(V.tensor_tensor(SCR[:, 1:64], SCR[:, 1:64], IM[:, 3:252:4], ALU.add))
                link(V.tensor_tensor(SCR, SCR, const("force"), ALU.add))
                link(V.max(M8, SCR))
                link(V.match_replace(RPL, M8, SCR, NEG))
                V.tensor_tensor(SEL, RPL, SCR, ALU.not_equal).then_inc(sa["sel"], 1)
                dve.wait_ge(sa["selmm"], 1)
                V.tensor_scalar(SELM, PS[0:24, 7, :], -1.0, -NEG, ALU.add, ALU.mult).then_inc(sa["selm"], 1)
                dve.wait_ge(sa["selm"], 1)

            def run(lo, hi):
                front(lo)
                for u in range(lo, hi):
                    weights(u)
                    if u + 1 < hi:
                        front(u + 1)
                    outs(u)

            run(0, NB)
            choose()
            run(NB, NSU)
            dve.wait_ge(sa["oev"], NSU)
            for hq in range(6):
                h, g = hq // 3, hq % 3
                e = slice(hq % 2 * HD, hq % 2 * HD + HD)
                V.tensor_copy(MIXT[e, hq // 2, TP:T].rearrange("p (b t) -> p b t", b=NB),
                              OA[h * HD:(h + 1) * HD, :, hq * TS:(hq + 1) * TS])
            for h in range(2):
                r = slice(h * HD, (h + 1) * HD)
                for g in range(3):
                    ins = V.tensor_copy(MIXT[r, 3 + g, TP:T].rearrange("p (b t) -> p b t", b=NB),
                                        OD[r, :, g, h * TS:(h + 1) * TS])
            ins.then_inc(sa["ex"], 1)
            for oc in range(KD):
                dve.wait_ge(wo_mm, oc + 1)
                x = XT[:, oc, :].rearrange("p (h t) -> p h t", h=2)
                V.tensor_tensor(x, x, PS[:, 4 * (oc % 2):4 * (oc % 2) + 2, 0:HALF], ALU.add).then_inc(wo_ev, 1)
            dve.wait_ge(wo_ev, KD)
            rms(2)
            ffn(1)
            for x in range(0, 10, 2):
                R = tile_rows(x // 2)
                dve.wait_ge(y_tr, x + 1)
                dve.wait_ge(ff[1]["out"], KD)
                if x:
                    dve.wait_ge(y_ev, x)
                V.tensor_copy(YO[0:R, x // 2, 0:512], PS[0:R, x % 4, :]).then_inc(y_ev, 1)


SMALL = 16 * 8
N_STATES = 7 + 12

_INS = ["x_prompt", "x_sample", "cache_cmp_kv", "cache_slc_kv", "cache_win_kv", "cache_dil0_kv", "cache_dil1_kv",
        "cache_dil2_kv", "state_pool", "page_table", "w_in", "w_out", "norm_gain", "qk_gain", "ffn_in", "ffn_out",
        "cmp_w1", "cmp_b1", "cmp_w2", "pool_w", "pool_scale"]
_OUTS = [("y_p", (1, TP, D)), ("y_s", (NB, TS, D)),
         ("cmp_p", (1, 1, TP, 2, 2, HD)), ("cmp_s", (1, NB, TS, 2, 2, HD)),
         ("slc_p", (1, 1, TP, 2, 2, HD)), ("slc_s", (1, NB, TS, 2, 2, HD)),
         ("win_p", (1, 1, 512, 2, 2, HD)), ("win_s", (1, NB, 512, 2, 2, HD)),
         ("dil0_p", (1, 1, 128, 2, 2, HD)), ("dil0_s", (1, NB, 128, 2, 2, HD)),
         ("dil1_p", (1, 1, 512, 2, 2, HD)), ("dil1_s", (1, NB, 512, 2, 2, HD)),
         ("dil2_p", (1, 1, 512, 2, 2, HD)), ("dil2_s", (1, NB, 2048, 2, 2, HD)),
         ("pool_p", (1, 1, 15, 256)), ("pool_s", (1, NB, 15, 256))]


def kernel(**inputs):
    import concourse.bacc as _bacc
    from concourse.bass_utils import run_bass_kernel_spmd as _run

    nc = _bacc.Bacc("TRN2", target_bir_lowering=False, num_devices=1)
    arrays, ins, outs = {}, {}, {}
    given = {n: np.ascontiguousarray(inputs[n]) for n in _INS}
    given["consts"] = constants()
    given["selp"] = page_selectors()
    for name, a in given.items():
        arrays[f"in_{name}"] = a
        ins[name] = nc.dram_tensor(f"in_{name}", a.shape, mybir.dt.from_np(a.dtype), kind="ExternalInput").ap()
    for name, shape in _OUTS:
        outs[name] = nc.dram_tensor(f"out_{name}", shape, F32, kind="ExternalOutput").ap()
    build(nc, ins, outs)
    r = _run(nc, [arrays], core_ids=[0])
    return tuple(r.results[0][f"out_{name}"] for name, _ in _OUTS)
```

```python
from contextlib import ExitStack

import numpy as np

import concourse.bass as bass
from concourse import mybir

F32 = mybir.dt.float32
F32R = mybir.dt.float32r
I32 = mybir.dt.int32
U32 = mybir.dt.uint32
ALU = mybir.AluOpType
ACT = mybir.ActivationFunctionType
AX = mybir.AxisListType

P = 128
D = 1024
KD = D // P
TP, NB, TS = 512, 8, 4
NS = NB * TS
T = TP + NS
HALF = T // 2
QT_TILES = TP // P
PAGE, PAST = 128, 4096
NPG = PAST // PAGE
HD = 64
FF = 2816
FCH = FF // P
BCH = FCH // 2
COLS = 2578
SLOT = BCH * P
RING = 4
NCG = 8
CG = -(-COLS // (2 * NCG)) * 2
KH = KD // 2
L_BLOCK = 2 * BCH + KD
L_IN = 2 * L_BLOCK
L_OUT = L_IN + 2 * NCG
L_FFN = (0, L_OUT + KD)
L_ALL = L_FFN[1] + 2 * L_BLOCK
SCALE = HD ** -0.5
EPS = 1e-6
NEG = -1.0e30
WDIL = ((128, 1), (512, 4), (2048, 16))

C_Q, C_CMP, C_SLCK, C_SLCV, C_WINK, C_WINV, C_G = 0, 384, 640, 768, 896, 1024, 1152
C_QB, C_KB, C_VB, C_U = 1170, 1554, 1938, 2322
SECTIONS = ((C_Q, 6, 0, 0), (C_SLCK, 2, 2, 6), (C_WINK, 2, 3, 8), (C_QB, 6, 4, 10), (C_KB, 6, 5, 16))
IT_SLC, IT_WIN, IT_QB, IT_KB, IT_U, ITEMS = 3, 4, 5, 8, 11, 13


def const_layout():
    at, out = 0, {}
    for name, rows, n in (
        ("ident", P, P), ("ones", P, P), ("diag", P, P), ("band_prev", P, P),
        ("mod4_off", P, P), ("mod4_diag", P, P), ("mod16_off", P, P), ("mod16_diag", P, P),
        ("cmp_add", P, 4 * 32), ("cmp_keep", P, 4 * 32),
        ("win_past", 24, 512), ("d0_past", 8, P), ("d12_past", 8, 4),
        ("new_a", 24, NB * 32), ("new_d0", 8, NB * 32), ("new_d12", 8, NB * 32),
        ("sum_heads", 24, NB * 64), ("to_rows", 64, NB * 24), ("tok_rows", 32, NB * 24), ("gate_pick", 24, 18),
        ("pool_w", P, 2), ("pool_head", P, 32), ("force", 64, 65), ("eps", P, 1),
    ):
        out[name] = (at, rows, n)
        at += n
    return out, at


CL, CN = const_layout()


def constants():
    c = np.zeros((P, CN), np.float32)

    def put(name, a):
        at, rows, n = CL[name]
        c[:rows, at:at + n] = a.reshape(rows, n)

    q, k = np.arange(P)[:, None], np.arange(P)[None, :]
    add = lambda ok: np.where(ok, 0.0, NEG)
    put("ident", np.eye(P))
    put("ones", np.ones((P, P)))
    put("diag", add(k <= q))
    put("band_prev", add(k >= q))
    for d in (4, 16):
        put(f"mod{d}_off", add((q - k) % d == 0))
        put(f"mod{d}_diag", add(((q - k) % d == 0) & (k <= q)))
    pos = np.arange(4)[None, :, None] * P + np.arange(P)[:, None, None]
    seen = (np.arange(32)[None, None, :] * 16 + 31 <= pos) & (np.arange(32) < 31)[None, None, :]
    put("cmp_add", add(seen))
    put("cmp_keep", seen.astype(np.float32))
    ta, td = np.arange(24) % TS, np.arange(8) % TS
    key = np.arange(P)[None, :] * 4 + np.arange(4)[:, None]
    put("win_past", add(key.reshape(1, 512) > ta[:, None]))
    put("d0_past", add(np.arange(P)[None, :] >= td[:, None]))
    put("d12_past", add(np.arange(4)[None, :] == td[:, None]))
    tok_b, tok_t = np.arange(NS) // TS, np.arange(NS) % TS
    own = tok_b[None, None, :] == np.arange(NB)[None, :, None]
    put("new_a", add(own & (tok_t[None, None, :] <= ta[:, None, None])))
    put("new_d0", add(own & (tok_t[None, None, :] <= td[:, None, None])))
    put("new_d12", add(own & (tok_t[None, None, :] == td[:, None, None])))
    r64 = np.arange(64)
    rb, rh, rt = r64 // 8, r64 // 4 % 2, r64 % 4
    ra = np.arange(24)
    same = (rh[None, None, :] == (ra // 12)[:, None, None]) & (rt[None, None, :] == ta[:, None, None]) \
        & (rb[None, None, :] == np.arange(NB)[None, :, None])
    put("sum_heads", same.astype(np.float32))
    put("to_rows", same.transpose(2, 1, 0).astype(np.float32))
    tok = np.arange(NS)[:, None, None] == (np.arange(NB)[None, :, None] * TS + ta[None, None, :])
    put("tok_rows", tok.astype(np.float32))
    put("gate_pick", (np.repeat(np.arange(6), 3)[None, :] == (ra // 4)[:, None]).astype(np.float32))
    w = np.array([[2, 8], [4, 16]])[(np.arange(P) // 64)]
    put("pool_w", 1.0 / w)
    put("pool_head", 1.0 / np.minimum(w[:, :, None], np.arange(16)[None, None, :] + 1))
    f = np.zeros((64, 65))
    f[:, [0, 63, 64]] = 1.0e4
    put("force", f)
    put("eps", np.full((P, 1), EPS))
    return c


def row_in_page():
    p = np.arange(P)
    return np.stack([p % 8, p % 32], 1).astype(np.float32)


def page_selectors():
    s = np.zeros((NPG, 10, P), np.float32)
    for half in range(2):
        s[half * 16 + np.arange(P) // 8, half, np.arange(P)] = 1.0
    for g in range(8):
        s[4 * g + np.arange(P) // 32, 2 + g, np.arange(P)] = 1.0
    return s.reshape(NPG, 10 * P)


def build(nc, I, O):
    ctx = ExitStack()
    with ctx:
        ctx.enter_context(nc.allow_non_contiguous_dma(reason="small transposed tables"))

        def sb(name, shape, dt=F32):
            return ctx.enter_context(nc.sbuf_tensor(name, shape, dt))

        def sem(name):
            return ctx.enter_context(nc.semaphore(name))

        FLOATS = dict(XT=KD * T, H=KD * T, BIG=5 * COLS, WR=2 * RING * SLOT, QTR=11 * TP, CKT=NB * 256, CV=NB * 2 * P,
                      VV=5 * 640, CO=CN, GB=4 * HALF)
        total = sum(8 * -(-n // 8) for n in FLOATS.values()) + 8
        sb("arena", [P, total])
        base = -(-(nc.sbuf_base - 4 * total) // 32) * 32
        place, at = {}, base
        for name, n in FLOATS.items():
            place[name] = at
            at += 32 * -(-n // 8)

        def put(name, shape, region, off=0, dt=F32):
            return nc.alloc_sbuf_tensor_at(name, shape, dt, offset=place[region] + 4 * off)

        XT = put("XT", [P, KD, T], "XT")
        HN = put("HN", [P, KD * T], "H")
        HNH = put("HNH", [P, KD, T], "H", dt=F32R)
        BIG = put("BIG", [P, 5 * COLS], "BIG")
        HIDH = put("HIDH", [P, BCH, T], "BIG", dt=F32R)
        HIDL = put("HIDL", [P, BCH, T], "BIG", BCH * T, dt=F32R)
        WR = put("WR", [P, 2 * RING * SLOT], "WR")
        WLO = put("WLO", [P, RING, SLOT], "WR", dt=F32R)
        WHI = put("WHI", [P, RING, SLOT], "WR", RING * SLOT, dt=F32R)
        QTR = put("QTR", [P, 11 * TP], "QTR")
        HNL = put("HNL", [P, KD, T], "QTR", dt=F32R)
        CKT = put("CKT", [P, NB, 256], "CKT")
        CV = put("CV", [P, NB, 2, P], "CV")
        VV = put("VV", [P, 5, 640], "VV")
        CO = put("CO", [P, CN], "CO")
        GB = put("GB", [P, 2, 2, HALF], "GB")
        NG = sb("NG", [P, 3, KD])
        QG = sb("QG", [P, 6, HD])
        B1 = sb("B1", [P, 2])
        W2 = sb("W2", [P, 2, HD])
        PW = sb("PW", [P, 2, HD])
        PSC = sb("PSC", [P, 2])
        RIP = sb("RIP", [P, 2])
        IXC = sb("IXC", [P, 2, NB], U32)
        IXS = sb("IXS", [P, 8, NB], U32)
        PTI = sb("PTI", [NPG, NB], I32)
        PTF = sb("PTF", [NPG, NB])
        GT = sb("GT", [P, 5, 18])
        SM = sb("SM", [P, 600])
        QA = sb("QA", [P, NB, 24])
        QD = sb("QD", [P, 3, NB, 8])
        QN = sb("QN", [P, 11, NS])
        PS = ctx.enter_context(nc.psum_tensor("PS", [P, 8, 512], F32))

        HNk = HN[:, :].rearrange("p (k t) -> p k t", k=KD)
        MIXT = HNk
        PROJ = BIG[:, :].rearrange("p (t c) -> p t c", t=5)
        QT = QTR[:, :].rearrange("p (m t) -> p m t", m=11)
        RAW = WR[:, 0:RING * SLOT].rearrange("p (s n) -> p s n", s=RING)
        HNF = QTR[:, 0:KD * T].rearrange("p (k t) -> p k t", k=KD)
        HIDF = BIG[:, BCH * T:2 * BCH * T].rearrange("p (n t) -> p n t", n=BCH)

        def const(name):
            at, rows, n = CL[name]
            return CO[0:rows, at:at + n]

        ident, ones = const("ident"), const("ones")
        eps = const("eps")
        RB = GB[:, 0, :, :]

        ld = {n: sem("ld_" + n) for n in ("const", "cw1", "small", "x", "page", "cw1b", "pieces", "poolst")}
        d_ch, a_ch, = sem("dve_chain"), sem("act_chain")
        g_rows = [sem("g_rows0"), sem("g_rows1")]
        ix_f, ix_mm, ix_ok = sem("ix_f"), sem("ix_mm"), sem("ix_ok")
        x_tr, x_ev = sem("x_tr"), sem("x_ev")
        t_done, ev_act, ev_dve = sem("t_done"), sem("ev_act"), sem("ev_dve")
        m_done, silu_done, w_done, w_copied = sem("m_done"), sem("silu_done"), sem("w_done"), sem("w_copied")
        hid_zero = sem("hid_zero")
        ck_ss, ck_sq, ck_n, ck_t, ck_ev = sem("ck_ss"), sem("ck_sq"), sem("ck_n"), sem("ck_t"), sem("ck_ev")
        landed = [sem(f"ring{s}_landed") for s in range(RING)]
        w_hi, w_lo, w_used = sem("w_hi"), sem("w_lo"), sem("w_used")
        rs = [{n: sem(f"rms{r}_{n}") for n in ("sq", "sum", "root", "f", "hi", "lo")} for r in range(3)]
        ff = [{n: sem(f"ffn{f}_{n}") for n in ("silu", "free", "mul", "hi", "lo")} for f in range(2)]
        pj_mm, pj_ev = sem("pj_mm"), sem("pj_ev")
        hn_ss, hn_rt, qn, cp_act = sem("hn_ss"), sem("hn_rt"), sem("qn"), sem("cp_act")
        qt_mm, qt_act, qt_dve = sem("qt_mm"), sem("qt_act"), sem("qt_dve")
        st_cmp, st_out = sem("st_cmp"), sem("st_out")
        pc = {n: sem("pc_" + n) for n in ("tr", "ev", "mm", "silu", "w", "ss", "rt", "n", "t", "ev2")}
        po = {n: sem("po_" + n) for n in ("zero", "st", "stev", "dl", "mm", "ev")}
        pa = {n: sem("pa_" + n) for n in ("s", "sev", "nb", "exp", "p", "t", "tev", "pv", "oev",
                                          "cs", "cnb", "cexp", "cp")}
        sa = {n: sem("sa_" + n) for n in ("kt", "ktev", "s", "sev", "nb", "exp", "pt", "ptev", "pv", "oev",
                                          "gmm", "gts", "imp", "sel", "selmm", "selm", "q", "ex")}
        sw = {n: sem("sa_weights_" + n) for n in ("cmp", "slc", "win", "dil")}
        ld_kv = [[sem(f"ld_kv{u}_{g}") for g in range(8)] for u in range(2)]
        ld_wd = [sem("ld_wd0"), sem("ld_wd1")]
        wo_ev = sem("wo_ev")
        y_tr, y_ev, y_out = sem("y_tr"), sem("y_ev"), sem("y_out")
        cpy = sem("state_copies")
        block = ctx.enter_context(nc.Block())

        XIN = WR[:, 0:5 * D].rearrange("p (t n) -> p t n", t=5)
        PB = [BIG[:, 0:8192].rearrange("p (h n) -> p h n", h=2), WR[:, 0:8192].rearrange("p (h n) -> p h n", h=2)]
        YO = BIG[:, 0:5 * D].rearrange("p (t n) -> p t n", t=5)
        PTB = [BIG[:, 8192:12288].rearrange("p (h s n) -> p h s n", h=2, s=8),
               HN[:, 0:4096].rearrange("p (h s n) -> p h s n", h=2, s=8)]
        HIDC = BIG[:, 12288:12800].rearrange("p (u n) -> p u n", u=2)
        CW1 = QTR[:, 0:4096].rearrange("p (v c e) -> p v c e", v=2, c=16)
        SELP = QTR[0:NPG, 4096:4096 + 10 * P].rearrange("p (s m) -> p s m", s=10)
        CK = VV[:, :, :].rearrange("p a b -> p (a b)")[:, 0:2048]
        CKS = BIG[:, 0:2048]
        QP = VV[:, :, :].rearrange("p a b -> p (a b)")[:, 0:5 * 384].rearrange("p (t g h d) -> p t g h d", t=5, g=3, h=2)
        SQT = GB[:, :, :, :].rearrange("p a b c -> p (a b c)")
        CW1B = WR[:, 0:4096].rearrange("p (v c e) -> p v c e", v=2, c=16)
        PCS = HN[0:32, 0:4096]
        o = 8192
        UT = WR[:, o:o + 1056].rearrange("p (c t) -> p c t", c=2)
        UTS = WR[:, o + 1056:o + 1360].rearrange("p (c b t) -> p c b t", c=2, b=NB)
        PTC = WR[:, o + 1360:o + 2384].rearrange("p (v h s n) -> p v h s n", v=2, h=2, s=8)
        HIDP = WR[:, o + 2384:o + 2512].rearrange("p (q n) -> p q n", q=4)
        PST = WR[0:120, o + 2512:o + 2768]
        CKTP = WR[:, o + 2768:o + 2800]
        CVP = WR[0:31, o + 2800:o + 2928]
        CKP = WR[0:31, o + 2928:o + 3056]
        T1 = BIG[:, 6400:7456].rearrange("p (c t) -> p c t", c=2)
        T2 = BIG[:, 7456:8512].rearrange("p (c t) -> p c t", c=2)
        T1S = BIG[:, 8512:8816].rearrange("p (c b t) -> p c b t", c=2, b=NB)
        T2S = BIG[:, 8816:9120].rearrange("p (c b t) -> p c b t", c=2, b=NB)
        DL = BIG[:, 9120:10144].rearrange("p (c t) -> p c t", c=2)
        DLS = BIG[:, 10144:10208].rearrange("p (c b t) -> p c b t", c=2, b=NB)
        PHD = BIG[:, 10208:10240].rearrange("p (c t) -> p c t", c=2)
        CKPS = BIG[0:31, 10240:10368]
        SB = BIG[:, 0:4608].rearrange("p (u b n) -> p u b n", u=3, b=3)
        PTS = BIG[:, 4608:6144].rearrange("p (u n) -> p u n", u=3)
        SC = BIG[:, 6144:6336].rearrange("p (h n) -> p h n", h=6)
        SS = SM[:, 0:110].rearrange("p (t n) -> p t n", t=5)
        SSC = SM[:, 110:142]
        SSP = SM[0:31, 142:144]
        MX, DEN, WT, NBI = (SM[:, 144 + 9 * n:153 + 9 * n].rearrange("p (u n) -> p u n", u=3) for n in range(4))
        CMX, CDN, CWT = SM[:, 180:186], SM[:, 186:192], SM[:, 192:198]
        MX1 = SM[:, 198:201]

        def section_end(n):
            return -(-(SECTIONS[n][0] + SECTIONS[n][1] * HD) // CG)

        def tile_rows(tt):
            return P if tt < QT_TILES else NS

        def tok(tt):
            return slice(tt * P, tt * P + tile_rows(tt))

        units = []
        s_count = 0
        for i in range(QT_TILES):
            for hq in range(6):
                h, g = hq // 3, hq % 3
                br = [dict(q=g, k=k, h=h, j0=0, v=v * P + h * HD, off=None, diag="diag")
                      for v, k in enumerate((IT_SLC, IT_WIN))]
                units.append(dict(i=i, nsa=True, hq=hq, h=h, br=br, s0=s_count, new=hq == 0))
                s_count += 2
            for h in range(2):
                br = [dict(q=IT_QB + g, k=IT_KB + g, h=h, j0=max(0, i - 1) if g == 0 else 0,
                           v=256 + g * P + h * HD, off=("band_prev", "mod4_off", "mod16_off")[g],
                           diag=("diag", "mod4_diag", "mod16_diag")[g]) for g in range(3)]
                units.append(dict(i=i, nsa=False, h=h, br=br, s0=s_count, new=False))
                s_count += 3
        NU = len(units)

        SLB = [BIG[0:24, 8192:8192 + 4128], QTR[0:24, 0:4128]]
        KV = [BIG[:, 0:8192], WR[:, 0:8192]]
        CKf = CKT[:, :, :].rearrange("p a b -> p (a b)")
        CVf = CV[:, :, :, :].rearrange("p a b c -> p (a b c)")
        KWIN = [WR[:, 8192:9216], CKf[:, 0:1024]]
        KDL1 = [WR[:, 9216:10240], CKf[:, 1024:2048]]
        KDL2 = [WR[:, 10240:11264], CVf[:, 0:1024]]
        KDL0 = [CVf[:, 1280:1536], CVf[:, 1024:1280]]
        VVf = VV[:, :, :].rearrange("p a b -> p (a b)")
        SWIN, SDIL, PTSL = VVf[0:24, 0:544], VVf[0:8, 544:1792], VVf[:, 1792:2560]
        SCS = VVf[0:24, 0:512].rearrange("p (u n) -> p u n", u=2)
        KTBS = [QTR[:, 4128:4640], QTR[:, 4640:5152], BIG[:, 12320:12832]]
        OA = QTR[:, 5152:5344].rearrange("p (b r) -> p b r", b=NB)
        OD = QTR[:, 5344:5536].rearrange("p (b g r) -> p b g r", b=NB, g=3)
        GBf = GB[:, :, :, :].rearrange("p a b c -> p (a b c)")
        GX = GBf[0:24, 0:144].rearrange("p (b c) -> p b c", b=NB)
        IM, SCR, M8 = GBf[0:64, 144:400], GBf[0:64, 400:465], GBf[0:64, 466:474]
        RPL, SEL = GBf[0:64, 144:209], GBf[0:64, 209:274]
        SELM = GBf[0:24, 480:992]
        KINDS = ("cmp", "slc", "win", "dil")
        GS = SM[0:24, 204:228].rearrange("p (b c) -> p b c", b=NB)
        SDEN, SMX, SNB, SWT = (SM[0:24, 230 + 8 * n:238 + 8 * n] for n in range(4))
        DG = SM[0:24, 264:264 + 192].rearrange("p (u n) -> p u n", u=8)
        EXR = SM[0:24, 460:588].rearrange("p (u n) -> p u n", u=2)

        def KTB(n):
            return KTBS[n % 3]

        newK = lambda item: QN[:, item, :]
        newV = lambda c: VV[0:NS, 4, c:c + P]

        def sample_unit(kind, b):
            x = b % 2
            if kind == "cmp":
                buf, rows, tc, out = SCS[:, x, :], 24, [], OA[:, b, :]
                nch = [(CKT[:, b, 0:255], QA[:, b, :], 0, 255, None)]
                tiles = [(ct * P, P, CV[:, b, ct, :], 0) for ct in range(2)]
                ptdst = [QTR[:, 5536 + 48 * x:5584 + 48 * x]]
            elif kind == "slc":
                kv, buf, rows, out = KV[x], SLB[x], 24, OA[:, b, :]
                tc = [([kv[:, (4 * G + j) * 256:(4 * G + j) * 256 + P] for j in range(4)], QA[:, b, :], 512 * G,
                       ("sel", G)) for G in range(8)]
                nch = [(newK(IT_SLC), QA[:, b, :], 4096, 32, ("new_a", b))]
                tiles = [(n * P, P, kv[:, n * 256 + P:n * 256 + 2 * P], 0) for n in range(32)] \
                    + [(4096, NS, newV(0), 0)]
                ptdst = [PTSL[:, 0:384], PTSL[:, 384:768], CVf[:, 1536:1560]]
            elif kind == "win":
                kw, buf, rows, out = KWIN[x], SWIN, 24, OA[:, b, :]
                tc = [([kw[:, j * 256:j * 256 + P] for j in range(4)], QA[:, b, :], 0, ("past", "win_past"))]
                nch = [(newK(IT_WIN), QA[:, b, :], 512, 32, ("new_a", b))]
                tiles = [(j * P, P, kw[:, j * 256 + P:(j + 1) * 256], 0) for j in range(4)] + [(512, NS, newV(P), 0)]
                ptdst = [CVf[:, 1560:1656], CVf[:, 1656:1680]]
            else:
                buf, rows, out = SDIL, 8, OD[:, b, :, :]
                kk = (KDL1[x], KDL2[x])
                tc = [([KDL0[x][:, 0:P]], QD[:, 0, b, :], 0, ("past", "d0_past"))]
                tc += [([kk[n][:, j * 256:j * 256 + P] for j in range(4)], QD[:, 1 + n, b, :], P + 512 * n,
                        ("step", "d12_past")) for n in range(2)]
                nch = [(newK(IT_KB + g), QD[:, g, b, :], 1152 + 32 * g, 32, ("new_d0" if g == 0 else "new_d12", b))
                       for g in range(3)]
                tiles = [(0, P, KDL0[x][:, P:2 * P], 0)]
                tiles += [(P + 512 * n + j * P, P, kk[n][:, j * 256 + P:(j + 1) * 256], 1 + n)
                          for n in range(2) for j in range(4)]
                tiles += [(1152 + 32 * g, NS, newV(256 + P * g), g) for g in range(3)]
                ptdst = [CVf[:, 1680:1752], CVf[:, 1752:1776]]
            full = [t for t in tiles if t[1] == P]
            new = [t for t in tiles if t[1] != P]
            pts = [full[n:n + 16] for n in range(0, len(full), 16)] + ([new] if new else [])
            return dict(kind=kind, b=b, buf=buf, rows=rows, tc=tc, nc=nch, pts=pts, ptdst=ptdst, out=out,
                        x=2 * KINDS.index(kind) + x)

        U_ = {(k, b): sample_unit(k, b) for k in KINDS for b in range(NB)}
        cmp_units = [U_["cmp", b] for b in range(NB)]
        front_order = cmp_units + [U_["slc", 0]]
        back_order = list(cmp_units)
        for b in range(NB):
            front_order += [U_["win", b], U_["dil", b]] + ([U_["slc", b + 1]] if b + 1 < NB else [])
            back_order += [U_["win", b], U_["dil", b], U_["slc", b]]
        kt0 = s0 = pt0 = 0
        for n, U in enumerate(front_order):
            U.update(f=n, kt0=kt0, s0=s0)
            kt0 += len(U["tc"])
            s0 += len(U["tc"]) + len(U["nc"])
        for n, U in enumerate(back_order):
            U.update(n=n, pt0=pt0)
            pt0 += len(U["pts"])
        score_of = {U["kt0"] + x: U["s0"] + x for U in front_order for x in range(len(U["tc"]))}
        NSU = len(back_order)

        def out_bank(U):
            return U["n"] % 2 if U["kind"] == "cmp" else 6 + U["n"] % 2

        def former(U):
            k, b = U["kind"], U["b"]
            if k == "win" and b == 0:
                return U_["cmp", NB - 1]
            back = 2 if k in ("cmp", "slc") else 1
            return U_[k, b - back] if b >= back else None

        @block.sync
        def _(sp):
            sp.dma_start(XIN[:, 0:4, :], I["x_prompt"][0].rearrange("(t p) n -> p t n", p=P)).then_inc(ld["x"], 16)
            sp.dma_start(XIN[0:NS, 4, :], I["x_sample"].rearrange("b t n -> (b t) n")).then_inc(ld["x"], 16)
            sp.dma_start(CO[:, :], I["consts"]).then_inc(ld["const"], 16)
            sp.dma_start(CW1, I["cmp_w1"][0].rearrange("v (c p) e -> p v c e", p=P)).then_inc(ld["cw1"], 16)

            sp.wait_ge(x_ev, KD + 1)
            sp.wait_ge(t_done, 16 * NB)

            def chunk_loads(f, first, c, used):
                src = I["ffn_in"][0, f].rearrange("(k p) n -> p k n", p=P)
                for gs in range(2):
                    sl = (first + gs) % RING
                    if used is not None:
                        sp.wait_ge(w_used, used + gs)
                    dst = RAW[:, sl, 0:KD * P].rearrange("p (k n) -> p k n", k=KD)
                    sp.dma_start(dst, src[:, :, bass.ds(c * P + gs * FF, P)]).then_inc(landed[sl], 16)

            def ffn_loads(f):
                for blk in range(2):
                    L = L_FFN[f] + blk * L_BLOCK
                    c = blk * BCH
                    n = 0
                    if L == 0:
                        for n in range(2):
                            chunk_loads(f, L + 2 * n, c + n, None)
                        n = 2
                    else:
                        chunk_loads(f, L, c, L - RING + 1)
                        n = 1
                    pairs = (BCH - n) // 2
                    with sp.Fori(0, pairs) as it:
                        for u in range(2):
                            m = n + u
                            chunk_loads(f, L + 2 * m, it * 2 + (c + m), it * 4 + (L + 2 * m - RING + 1))
                    for m in range(n + 2 * pairs, BCH):
                        chunk_loads(f, L + 2 * m, c + m, L + 2 * m - RING + 1)
                    L += 2 * BCH
                    src = I["ffn_out"][0, f].rearrange("(k p) n -> p k n", p=P)[:, blk * BCH:(blk + 1) * BCH, :]
                    for oc in range(KD):
                        sl = (L + oc) % RING
                        sp.wait_ge(w_used, L + oc - RING + 1)
                        sp.dma_start(RAW[:, sl, :].rearrange("p (k n) -> p k n", k=BCH),
                                     src[:, :, oc * P:(oc + 1) * P]).then_inc(landed[sl], 16)

            ffn_loads(0)
            w_in = I["w_in"][0].rearrange("(k p) n -> p k n", p=P)
            for c in range(NCG):
                n = min(CG, COLS - c * CG)
                for x in range(2):
                    L = L_IN + 2 * c + x
                    sp.wait_ge(w_used, L - RING + 1)
                    sp.dma_start(RAW[:, L % RING, 0:KH * n].rearrange("p (k n) -> p k n", k=KH),
                                 w_in[:, x * KH:(x + 1) * KH, c * CG:c * CG + n]).then_inc(landed[L % RING], 16)
                if c == 4:
                    sp.wait_ge(pj_ev, 5 * -(-(C_CMP + 256) // CG))
                    cmp_p = O["cmp_p"].rearrange("a b t x h d -> (a b t) (x h d)")
                    sp.dma_start(cmp_p.rearrange("(t p) c -> p t c", p=P), PROJ[:, 0:4, C_CMP:C_CMP + 256])\
                        .then_inc(st_cmp, 16)
            sp.wait_ge(w_used, L_OUT)
            sp.wait_ge(st_cmp, 16)
            sp.dma_start(PCS, cmp_p.rearrange("(p s) c -> p (s c)", s=16)).then_inc(ld["pieces"], 16)
            sp.dma_start(PST, I["state_pool"][0].rearrange("b t c -> (b t) c")).then_inc(ld["poolst"], 16)
            sp.dma_start(CW1B, I["cmp_w1"][0].rearrange("v (c p) e -> p v c e", p=P)).then_inc(ld["cw1b"], 16)

            def states():
                def flat(name):
                    return O[name].rearrange("a b t x h d -> (a b) t (x h d)")

                u_p, u_s = O["pool_p"][0, 0], O["pool_s"][0]
                yield O["cmp_s"].rearrange("a b t x h d -> (a b t) (x h d)"), PROJ[0:NS, 4, C_CMP:C_CMP + 256]
                yield u_p, PROJ[P - 15:P, 3, C_U:C_U + 256]
                yield u_s[:, 11:15, :], PROJ[0:NS, 4, C_U:C_U + 256]
                for name, c in (("slc", C_SLCK), ("win", C_WINK)):
                    yield flat(name + "_p")[0].rearrange("(t p) c -> p t c", p=P), PROJ[:, 0:4, c:c + 256]
                yield O["slc_s"].rearrange("a b t x h d -> (a b t) (x h d)"), PROJ[0:NS, 4, C_SLCK:C_SLCK + 256]
                yield flat("win_s")[:, 508:512, :], PROJ[0:NS, 4, C_WINK:C_WINK + 256]
                for g, (w, _) in enumerate(WDIL):
                    n = min(w, TP) // P
                    for x, c in enumerate((C_KB + g * P, C_VB + g * P)):
                        yield (flat(f"dil{g}_p")[0].rearrange("(t p) c -> p t c", p=P)[:, :, x * P:(x + 1) * P],
                               PROJ[:, 4 - n:4, c:c + P])
                        yield flat(f"dil{g}_s")[:, w - TS:w, x * P:(x + 1) * P], PROJ[0:NS, 4, c:c + P]

            sp.wait_ge(qn, 5)
            sp.wait_ge(pj_ev, 5 * NCG)
            n_states = 0
            for dst, src in states():
                sp.dma_start(dst, src).then_inc(st_out, 16)
                n_states += 1
            assert n_states == N_STATES

            sp.wait_ge(sa["pv"], NSU)
            w_out = I["w_out"][0].rearrange("(k p) n -> p k n", p=P)
            for c in range(KD):
                L = L_OUT + c
                if c >= RING:
                    sp.wait_ge(w_used, L - RING + 1)
                sp.dma_start(RAW[:, L % RING, 0:KD * P].rearrange("p (k n) -> p k n", k=KD),
                             w_out[:, :, c * P:(c + 1) * P]).then_inc(landed[L % RING], 16)
            ffn_loads(1)

            for tt in range(5):
                R = tile_rows(tt)
                sp.wait_ge(y_ev, 2 * (tt + 1))
                dst = O["y_p"][0, tt * P:(tt + 1) * P, :] if tt < 4 else O["y_s"].rearrange("b t n -> (b t) n")
                sp.dma_start(dst, YO[0:R, tt, :]).then_inc(y_out, 16)
            sp.wait_ge(y_out, 16 * 5)
            sp.wait_ge(st_out, 16 * n_states)
            sp.wait_ge(cpy, 16 * 5)

        @block.gpsimd
        def _(pool):
            cmp_rows = I["cache_cmp_kv"][0].rearrange("n (r s) x h d -> (n r) (s x h d)", s=16)
            slc_rows = I["cache_slc_kv"][0].rearrange("n (r s) x h d -> (n r) (s x h d)", s=4)
            pool.wait_ge(ix_ok, 2)
            for b in range(NB):
                if b == 1:
                    pool.wait_ge(x_ev, KD + 1)
                if b >= 2:
                    pool.wait_ge(t_done, 16 * (b - 1))
                for half in range(2):
                    pool.indirect_dma_start(PB[b % 2][:, half, :], None, cmp_rows,
                                            bass.IndirectOffsetOnAxis(ap=IXC[:, half, b:b + 1], axis=0))\
                        .then_inc(g_rows[b % 2], 16)
            def moved(dst, src, w):
                pool.dma_start(dst[:, 0:w - TS], src[:, TS:w]).then_inc(cpy, 16)

            pool.wait_ge(t_done, 16 * NB)
            for name, src, w in (("win_s", "cache_win_kv", 512), ("dil0_s", "cache_dil0_kv", 128),
                                 ("dil1_s", "cache_dil1_kv", 512), ("dil2_s", "cache_dil2_kv", 2048)):
                moved(O[name][0].rearrange("b t x h d -> b (t x h d)").rearrange("b (t c) -> b t c", c=256),
                      I[src][0].rearrange("b t x h d -> b t (x h d)"), w)
            moved(O["pool_s"][0], I["state_pool"][0], 15)

            def load_slc(b):
                for G in range(8):
                    pool.indirect_dma_start(KV[b % 2][:, G * 1024:(G + 1) * 1024], None, slc_rows,
                                            bass.IndirectOffsetOnAxis(ap=IXS[:, G, b:b + 1], axis=0))\
                        .then_inc(ld_kv[b % 2][G], 16)

            def load_wd(b):
                x = b % 2
                pool.dma_start(KWIN[x], I["cache_win_kv"][0, b].rearrange("(p j) x h d -> p (j x h d)", j=4))\
                    .then_inc(ld_wd[x], 16)
                pool.dma_start(KDL0[x], I["cache_dil0_kv"][0, b].rearrange("p x h d -> p (x h d)")).then_inc(ld_wd[x], 16)
                pool.dma_start(KDL1[x], I["cache_dil1_kv"][0, b].rearrange("(p j) x h d -> p (j x h d)", j=4))\
                    .then_inc(ld_wd[x], 16)
                pool.dma_start(KDL2[x], I["cache_dil2_kv"][0, b].rearrange("(p j) x h d -> p j (x h d)", j=16)[:, 0:4, :])\
                    .then_inc(ld_wd[x], 16)

            pool.wait_ge(pa["pv"], 3 * NU)
            pool.wait_ge(pa["oev"], NU)
            pool.wait_ge(po["ev"], 4)
            load_slc(0)
            load_slc(1)
            pool.wait_ge(sa["pv"], NB)
            load_wd(0)
            load_wd(1)
            for b in range(2, NB):
                pool.wait_ge(sa["pv"], U_["dil", b - 2]["n"] + 1)
                load_wd(b)
                pool.wait_ge(sa["pv"], U_["slc", b - 2]["n"] + 1)
                load_slc(b)

        @block.tensor
        def _(pe):
            pe.sem_inc(m_done, 4)
            pe.wait_ge(ld["page"], 48)
            pe.wait_ge(ix_f, 1)
            for s in range(10):
                mm = pe.matmul(PS[:, 7, s * NB:(s + 1) * NB], SELP[:, s, :], PTF[:, :], start=True, stop=True)
            mm.then_inc(ix_mm, 1)
            pe.wait_ge(ld["x"], 32)
            pe.wait_ge(ld["const"], 16)
            for k in range(KD):
                if k >= 6:
                    pe.wait_ge(x_ev, k - 5)
                for tt in range(4):
                    pe.transpose(PS[:, k % 6, tt * P:(tt + 1) * P], XIN[:, tt, k * P:(k + 1) * P], ident)
                pe.transpose(PS[:, 6, k * NS:(k + 1) * NS], XIN[0:NS, 4, k * P:(k + 1) * P], ident[0:NS, 0:NS])\
                    .then_inc(x_tr, 1)

            def rms(r):
                for k in range(KD):
                    pe.wait_ge(rs[r]["sq"], k + 1)
                    for hf in range(2):
                        mm = pe.matmul(PS[:, hf, 0:HALF], ones, HNk[:, k, hf * HALF:(hf + 1) * HALF],
                                       start=(k == 0), stop=(k == KD - 1))
                mm.then_inc(rs[r]["sum"], 1)

            pe.wait_ge(x_ev, KD + 1)
            rms(0)
            pe.wait_ge(rs[0]["root"], 1)
            pe.wait_ge(ix_ok, 2)
            pe.wait_ge(ld["cw1"], 16)
            pe.wait_ge(ld["small"], SMALL)
            pe.wait_ge(hid_zero, 1)

            def tr_unit(b, par, kv, j, rows_ready):
                if rows_ready is not None:
                    pe.wait_ge(g_rows[par], rows_ready)
                n = b * 16 + (8 * kv + j + 1)
                pe.wait_ge(ev_act, n)
                pe.wait_ge(ev_dve, n)
                for s in range(2):
                    for half in range(2):
                        c = (2 * j + s) * 256 + kv * P
                        mm = pe.transpose(PS[:, j % 4, s * 256 + half * P:s * 256 + (half + 1) * P],
                                          PB[par][:, half, c:c + P], ident)
                mm.then_inc(t_done, 1)

            def hidden(b, kv, h, spread):
                m = 2 * kv + h
                pe.wait_ge(ev_act, b * 16 + (4 + 8 * kv + 8))
                pe.wait_ge(ev_dve, b * 16 + (4 + 8 * kv + 8))
                pe.wait_ge(silu_done, b * 4 + (m + 1))
                for c in range(2):
                    for s in range(8):
                        mm = pe.matmul(PS[:, 4 + m % 2, 0:255], CW1[:, kv, 8 * c + s, :], PTB[kv][:, h, s, c:c + 255],
                                       start=(c == 0 and s == 0), stop=(c == 1 and s == 7))
                        if (c, s) in spread:
                            spread[(c, s)]()
                mm.then_inc(m_done, 1)

            def second(b, m):
                pe.wait_ge(silu_done, b * 4 + (2 + m + 1))
                pe.wait_ge(w_copied, b * 4 + (m + 3))
                for ct in range(2):
                    c = (ct * 4 + m) * HD
                    mm = pe.matmul(PS[:, 6 + m % 2, c:c + HD], HIDC[:, m % 2, ct * P:(ct + 1) * P], W2[:, m // 2, :],
                                   start=True, stop=True)
                mm.then_inc(w_done, 1)

            def compress(b, par, count, last):
                T1u = lambda j: (lambda: tr_unit(b, par, 1, j, None))
                at = [(0, 1), (0, 4), (0, 7), (1, 2)]
                hidden(b, 0, 0, {at[n]: T1u(n) for n in range(4)})
                hidden(b, 0, 1, {**{at[n]: T1u(4 + n) for n in range(4)}, (1, 5): lambda: second(b, 0)})
                nxt = {} if last else {at[n]: (lambda n=n: tr_unit(b + 1, 1 - par, 0, n, count if n == 0 else None))
                                       for n in range(4)}
                hidden(b, 1, 0, {**nxt, (1, 5): lambda: second(b, 1)})
                nxt = {} if last else {at[n]: (lambda n=n: tr_unit(b + 1, 1 - par, 0, 4 + n, None)) for n in range(3)}
                hidden(b, 1, 1, {**nxt, (1, 5): lambda: second(b, 2)})
                if not last:
                    tr_unit(b + 1, 1 - par, 0, 7, None)
                second(b, 3)

            for j in range(8):
                tr_unit(0, 0, 0, j, 32 if j == 0 else None)
            with pe.Fori(0, NB // 2 - 1) as it:
                compress(it * 2, 0, it * 32 + 32, False)
                compress(it * 2 + 1, 1, it * 32 + 64, False)
            compress(NB - 2, 0, 32 * (NB // 2), False)
            compress(NB - 1, 1, 0, True)
            pe.wait_ge(ev_act, 4 + 16 * NB)
            pe.wait_ge(ev_dve, 4 + 16 * NB)
            pe.wait_ge(w_copied, 4 + 4 * NB)

            def split(L):
                return L if L <= L_OUT else L - KD

            def three(out, a, b, first, last):
                pe.matmul(out, a[0], b[0], start=first, stop=False)
                pe.matmul(out, a[0], b[1], start=False, stop=False)
                return pe.matmul(out, a[1], b[0], start=False, stop=last)

            def weights(sl, k, n, w):
                return tuple(t[:, sl, k * w + n[0]:k * w + n[1]] for t in (WHI, WLO))

            def halves(hf):
                return slice(hf * HALF, (hf + 1) * HALF)

            def ffn(f):
                pe.sem_inc(ff[f]["free"], 2)
                r = rs[2 * f]
                for blk in range(2):
                    L0 = L_FFN[f] + blk * L_BLOCK
                    e0 = blk * (BCH + KD)

                    def chunk(m, it, step):
                        L, e = split(L0) + 2 * m, e0 + m
                        pe.wait_ge(ff[f]["free"], it * step + (e + 1))
                        for gs in range(2):
                            pe.wait_ge(w_hi, it * (2 * step) + (L + gs + 1))
                            pe.wait_ge(w_lo, it * (2 * step) + (L + gs + 1))
                            sl = (L0 + 2 * m + gs) % RING
                            for hf in range(2):
                                for k in range(KD):
                                    if m == 0 and gs == 0 and hf == 0 and blk == 0:
                                        pe.wait_ge(r["hi"], k + 1)
                                        pe.wait_ge(r["lo"], k + 1)
                                    mm = three(PS[:, 4 * (e % 2) + 2 * gs + hf, 0:HALF], weights(sl, k, (0, P), P),
                                               (HNH[:, k, halves(hf)], HNL[:, k, halves(hf)]), k == 0, k == KD - 1)
                            mm.then_inc(w_used, 1)

                    with pe.Fori(0, BCH // 2) as it:
                        for u in range(2):
                            chunk(u, it, 2)
                    chunk(BCH - 1, 0, 0)
                    LO, eo = L0 + 2 * BCH, e0 + BCH

                    def out_chunk(oc, it, step, wait_last):
                        L, e = split(LO) + oc, eo + oc
                        pe.wait_ge(ff[f]["free"], it * step + (e + 1))
                        pe.wait_ge(w_hi, it * step + (L + 1))
                        pe.wait_ge(w_lo, it * step + (L + 1))
                        sl = (LO + oc) % RING
                        for hf in range(2):
                            for n in range(BCH):
                                if wait_last and hf == 0 and n >= BCH - 2:
                                    pe.wait_ge(ff[f]["hi"], blk * BCH + n + 1)
                                    pe.wait_ge(ff[f]["lo"], blk * BCH + n + 1)
                                mm = three(PS[:, 4 * (e % 2) + hf, 0:HALF], weights(sl, n, (0, P), P),
                                           (HIDH[:, n, halves(hf)], HIDL[:, n, halves(hf)]), n == 0, n == BCH - 1)
                        mm.then_inc(w_used, 1)

                    pe.wait_ge(ff[f]["hi"], blk * BCH + BCH - 2)
                    pe.wait_ge(ff[f]["lo"], blk * BCH + BCH - 2)
                    with pe.Fori(0, KD // 4) as it:
                        for oc in range(4):
                            out_chunk(oc, it, 4, oc == 0)
                pe.wait_ge(ff[f]["free"], 2 + 2 * (BCH + KD))

            ffn(0)
            pe.wait_ge(ck_n, 1)
            for b in range(NB):
                for ct in range(2):
                    n = 2 * b + ct
                    mm = pe.transpose(PS[:, 4 + n // 4, (n % 4) * P:(n % 4 + 1) * P], CK[:, n * P:(n + 1) * P], ident)
            mm.then_inc(ck_t, 1)
            rms(1)
            pe.wait_ge(rs[1]["root"], 1)
            pe.wait_ge(ck_ev, 1)
            for c in range(NCG):
                L = L_IN + 2 * c
                pe.wait_ge(w_hi, L + 2)
                pe.wait_ge(w_lo, L + 2)
                n = min(CG, COLS - c * CG)
                for tt in range(5):
                    x = c * 5 + tt
                    ts = tok(tt) if tt < 4 else slice(T - P, T)
                    if x >= 8:
                        pe.wait_ge(pj_ev, x - 7)
                    for k in range(KD):
                        if x == 0:
                            pe.wait_ge(rs[1]["hi"], k + 1)
                            pe.wait_ge(rs[1]["lo"], k + 1)
                        mm = three(PS[:, x % 8, 0:n], (HNH[:, k, ts], HNL[:, k, ts]),
                                   weights((L + k // KH) % RING, k % KH, (0, n), n), k == 0, k == KD - 1)
                    mm.then_inc(pj_mm, 1)
                    if tt == 4:
                        pe.wait_ge(pj_mm, x + 1)
                        pe.sem_inc(w_used, 2)
            pe.wait_ge(pj_ev, 5 * NCG)
            pe.wait_ge(qn, 5)
            pcol = {IT_SLC: C_SLCK, IT_WIN: C_WINK}
            pcol.update({IT_QB + g: C_QB + g * P for g in range(3)})
            pcol.update({IT_KB + g: C_KB + g * P for g in range(3)})
            pcol.update({IT_U + c: C_U + c * P for c in range(2)})
            for m in range(ITEMS):
                if m >= 4:
                    pe.wait_ge(qt_act, m - 3)
                    pe.wait_ge(qt_dve, m - 3)
                for tt in range(5):
                    R = tile_rows(tt)
                    src = QP[0:R, tt, m, :, :].rearrange("p h d -> p (h d)") if m < 3 else \
                        PROJ[0:R, tt, pcol[m]:pcol[m] + P]
                    dst = PS[:, 2 * (m % 4), tt * P:(tt + 1) * P] if tt < 4 else PS[:, 2 * (m % 4) + 1, 0:NS]
                    mm = pe.transpose(dst, src, ident[0:R, 0:R])
                mm.then_inc(qt_mm, 1)
            pe.wait_ge(qt_act, ITEMS)
            pe.wait_ge(qt_dve, ITEMS)
            pe.wait_ge(ld["poolst"], 16)
            for c in range(2):
                mm = pe.transpose(PS[:, 4, c * P:c * P + 120], PST[:, c * P:(c + 1) * P], ident[0:120, 0:120])
            mm.then_inc(po["st"], 1)
            pe.wait_ge(ld["pieces"], 16)
            for kv in range(2):
                for s in range(16):
                    c = s * 256 + kv * P
                    mm = pe.transpose(PS[:, kv, s * 32:(s + 1) * 32], PCS[:, c:c + P], ident[0:32, 0:32])
                mm.then_inc(pc["tr"], 1)
            pe.wait_ge(ld["cw1b"], 16)
            pe.wait_ge(pc["ev"], 2)
            for m in range(4):
                for c in range(2):
                    for s in range(8):
                        mm = pe.matmul(PS[:, 2, m * 32:m * 32 + 31], CW1B[:, m // 2, 8 * c + s, :],
                                       PTC[:, m // 2, m % 2, s, c:c + 31], start=(c == 0 and s == 0),
                                       stop=(c == 1 and s == 7))
            mm.then_inc(pc["mm"], 1)
            pe.wait_ge(pc["silu"], 2)
            for m in range(4):
                mm = pe.matmul(PS[0:31, 3, m * HD:(m + 1) * HD], HIDP[:, m, 0:31], W2[:, m // 2, :],
                               start=True, stop=True)
            mm.then_inc(pc["w"], 1)
            pe.wait_ge(po["dl"], 1)
            for c in range(2):
                for q in range(2):
                    r = slice(q * HD, (q + 1) * HD)
                    pe.matmul(PS[r, 5 + c, 0:TP], PW[r, c, :], DL[r, c, :], start=True, stop=True)
                    mm = pe.matmul(PS[r, 7, c * NS:(c + 1) * NS], PW[r, c, :],
                                   DLS[r, c, :, :].rearrange("p b t -> p (b t)"), start=True, stop=True)
            mm.then_inc(po["mm"], 1)
            pe.wait_ge(pc["n"], 1)
            pe.transpose(PS[:, 2, 0:31], CKP, ident[0:31, 0:31]).then_inc(pc["t"], 1)
            pe.wait_ge(pc["ev2"], 1)
            pe.wait_ge(po["ev"], 4)
            pe.wait_ge(po["stev"], 1)

            def scores(u):
                U = units[u]
                i = U["i"]
                if U["new"]:
                    if i:
                        pe.wait_ge(pa["cp"], i)
                    for hq in range(6):
                        r = slice(hq // 3 * HD, hq // 3 * HD + HD)
                        mm = pe.matmul(PS[:, 7, hq * 32:hq * 32 + 31], QT[r, hq % 3, i * P:(i + 1) * P],
                                       CKTP[r, 0:31], start=True, stop=True)
                        if hq % 3 == 2:
                            mm.then_inc(pa["cs"], 1)
                            pe.wait_ge(pa["cs"], 2 * i + hq // 3 + 1)
                for x, b in enumerate(U["br"]):
                    B = U["s0"] + x
                    if B >= 3:
                        pe.wait_ge(pa["sev"], B - 2)
                    r = slice(b["h"] * HD, b["h"] * HD + HD)
                    n = (i + 1 - b["j0"]) * P
                    pe.matmul(PS[:, B % 3, 0:n], QT[r, b["q"], i * P:(i + 1) * P],
                              QT[r, b["k"], b["j0"] * P:(i + 1) * P], start=True, stop=True).then_inc(pa["s"], 1)

            def turn(u, x):
                U = units[u]
                B = 3 * u + x
                if B >= 2:
                    pe.wait_ge(pa["tev"], B - 1)
                if U["nsa"] and x == 2:
                    pe.wait_ge(pa["cp"], U["i"] + 1)
                    pe.transpose(PS[0:31, 3 + B % 2, 0:P], SC[:, U["hq"], 0:31], ident).then_inc(pa["t"], 1)
                    return
                pe.wait_ge(pa["p"], u + 1)
                for y in range(U["i"] + 1 - U["br"][x]["j0"]):
                    mm = pe.transpose(PS[:, 3 + B % 2, y * P:(y + 1) * P], SB[:, u % 3, x, y * P:(y + 1) * P], ident)
                mm.then_inc(pa["t"], 1)

            def values(u, x):
                U = units[u]
                B = 3 * u + x
                if x == 0 and u >= 2:
                    pe.wait_ge(pa["oev"], u - 1)
                pe.wait_ge(pa["tev"], B + 1)
                if U["nsa"]:
                    e = U["hq"] % 2
                    out = PS[e * HD:(e + 1) * HD, 5 + u % 2, 0:P]
                else:
                    out = PS[U["h"] * HD:(U["h"] + 1) * HD, 5 + u % 2, x * P:(x + 1) * P]
                if U["nsa"] and x == 2:
                    pe.matmul(out, CVP[:, U["h"] * HD:(U["h"] + 1) * HD], PTS[0:31, B % 3, 0:P],
                              start=False, stop=True).then_inc(pa["pv"], 1)
                    return
                b = U["br"][x]
                n = U["i"] + 1 - b["j0"]
                for y in range(n):
                    mm = pe.matmul(out, VV[:, b["j0"] + y, b["v"]:b["v"] + HD], PTS[:, B % 3, y * P:(y + 1) * P],
                                   start=(y == 0 and (x == 0 or not U["nsa"])),
                                   stop=(y == n - 1 and not U["nsa"]))
                mm.then_inc(pa["pv"], 1)

            scores(0)
            scores(1)
            for u in range(NU):
                if u + 2 < NU:
                    scores(u + 2)
                turn(u, 0)
                turn(u, 1)
                values(u, 0)
                turn(u, 2)
                values(u, 1)
                values(u, 2)

            pe.wait_ge(pa["oev"], NU)
            for b in range(NB):
                mm = pe.matmul(PS[0:24, 5, b * 18:(b + 1) * 18], const("tok_rows")[:, b * 24:(b + 1) * 24],
                               GT[0:NS, 4, :], start=True, stop=True)
            mm.then_inc(sa["gmm"], 1)
            pe.wait_ge(sa["q"], 1)
            pe.wait_ge(sa["gts"], 1)

            def front(U):
                b = U["b"]
                if U["kind"] == "win":
                    pe.wait_ge(ld_wd[b % 2], 64 * (b // 2 + 1))

                def kturn(x):
                    n = U["kt0"] + x
                    if U["kind"] == "slc":
                        pe.wait_ge(ld_kv[b % 2][x], 16 * (b // 2 + 1))
                    if n >= 2:
                        pe.wait_ge(sa["ktev"], n - 1)
                    for y, kt in enumerate(U["tc"][x][0]):
                        mm = pe.transpose(PS[:, n % 2, y * P:(y + 1) * P], kt, ident)
                    mm.then_inc(sa["kt"], 1)

                def kscore(x):
                    n, s = U["kt0"] + x, U["s0"] + x
                    w = len(U["tc"][x][0]) * P
                    pe.wait_ge(sa["ktev"], n + 1)
                    if s >= 2:
                        pe.wait_ge(sa["sev"], s - 1)
                    pe.matmul(PS[0:U["rows"], 2 + s % 2, 0:w], U["tc"][x][1], KTB(n)[:, 0:w],
                              start=True, stop=True).then_inc(sa["s"], 1)

                for x in range(len(U["tc"]) + 1):
                    if x < len(U["tc"]):
                        kturn(x)
                    if x:
                        kscore(x - 1)
                for x, (k, q, _, w, _) in enumerate(U["nc"]):
                    s = U["s0"] + len(U["tc"]) + x
                    if s >= 2:
                        pe.wait_ge(sa["sev"], s - 1)
                    pe.matmul(PS[0:U["rows"], 2 + s % 2, 0:w], q, k, start=True, stop=True).then_inc(sa["s"], 1)

            def back(U):
                R, b = U["rows"], U["b"]
                pe.wait_ge(sw[U["kind"]], b + 1)
                if U["kind"] == "cmp":
                    mm = pe.matmul(PS[0:64, 7, 0:255], EXR[:, b % 2, :], U["buf"][:, 0:255], start=(b == 0),
                                   stop=(b == NB - 1))
                    if b == NB - 1:
                        mm.then_inc(sa["imp"], 1)

                def turn(x):
                    n = U["pt0"] + x
                    if n >= 2:
                        pe.wait_ge(sa["ptev"], n - 1)
                    for y, (c, rows, _, _) in enumerate(U["pts"][x]):
                        mm = pe.matmul(PS[0:rows, 4 + n % 2, y * R:(y + 1) * R], U["buf"][:, c:c + rows],
                                       DG[0:R, U["x"], 0:R], start=True, stop=True)
                    mm.then_inc(sa["pt"], 1)

                if U["n"] >= 2:
                    pe.wait_ge(sa["oev"], U["n"] - 1)
                groups = len(U["pts"])
                if U["kind"] != "dil":
                    total = sum(len(t) for t in U["pts"])
                    done = 0
                    for x in range(groups + 1):
                        if x < groups:
                            turn(x)
                        if x:
                            pe.wait_ge(sa["ptev"], U["pt0"] + x)
                            for y, (_, rows, v, _) in enumerate(U["pts"][x - 1]):
                                pt = U["ptdst"][x - 1][:, y * R:(y + 1) * R]
                                mm = pe.matmul(PS[:, out_bank(U), 0:R], v, pt[0:rows, :], start=(done == 0),
                                               stop=(done == total - 1))
                                done += 1
                else:
                    for x in range(groups):
                        turn(x)
                    pe.wait_ge(sa["ptev"], U["pt0"] + groups)
                    flat = [(t, U["ptdst"][x][:, y * R:(y + 1) * R]) for x, ts in enumerate(U["pts"])
                            for y, t in enumerate(ts)]
                    for g in range(3):
                        mine = [(t, pt) for t, pt in flat if t[3] == g]
                        for y, ((_, rows, v, _), pt) in enumerate(mine):
                            mm = pe.matmul(PS[:, out_bank(U), g * 8:g * 8 + R], v, pt[0:rows, :],
                                           start=(y == 0), stop=(y == len(mine) - 1))
                mm.then_inc(sa["pv"], 1)

            def pick():
                pe.wait_ge(sa["sel"], 1)
                for b in range(NB):
                    mm = pe.matmul(PS[0:24, 7, b * 64:(b + 1) * 64], const("to_rows")[:, b * 24:(b + 1) * 24],
                                   SEL[:, 0:64], start=True, stop=True)
                mm.then_inc(sa["selmm"], 1)

            front(cmp_units[0])
            for b in range(NB):
                if b + 1 < NB:
                    front(cmp_units[b + 1])
                back(cmp_units[b])
            pick()
            pe.wait_ge(sa["oev"], NB)
            front(U_["slc", 0])
            for b in range(NB):
                front(U_["win", b])
                front(U_["dil", b])
                if b + 1 < NB:
                    front(U_["slc", b + 1])
                back(U_["win", b])
                back(U_["dil", b])
                back(U_["slc", b])

            pe.wait_ge(sa["ex"], 1)
            pe.wait_ge(sa["oev"], NSU)
            pe.wait_ge(sa["selm"], 1)
            for oc in range(KD):
                L = L_OUT + oc
                pe.wait_ge(landed[L % RING], 16 * (L // RING + 1))
                if oc >= 2:
                    pe.wait_ge(wo_ev, oc - 1)
                for hf in range(2):
                    for k in range(KD):
                        mm = pe.matmul(PS[:, 4 * (oc % 2) + hf, 0:HALF], RAW[:, L % RING, k * P:(k + 1) * P],
                                       MIXT[:, k, halves(hf)], start=(k == 0), stop=(k == KD - 1))
                mm.then_inc(w_used, 1)
            pe.wait_ge(wo_ev, KD)
            rms(2)
            pe.wait_ge(rs[2]["root"], 1)
            ffn(1)
            for tt in range(5):
                R = tile_rows(tt)
                for hf in range(2):
                    x = 2 * tt + hf
                    if x >= 4:
                        pe.wait_ge(y_ev, x - 3)
                    for k in range(4):
                        mm = pe.transpose(PS[0:R, x % 4, k * P:(k + 1) * P], XT[:, 4 * hf + k, tok(tt)], ident)
                    mm.then_inc(y_tr, 1)

        @block.scalar
        def _(act):
            act.sem_inc(ev_act, 4)
            act.sem_inc(silu_done, 2)
            act.dma_start(PTI[:, :], I["page_table"].rearrange("b n -> n b")).then_inc(ld["page"], 16)
            act.dma_start(SELP, I["selp"].rearrange("p (s m) -> p s m", s=10)).then_inc(ld["page"], 16)
            act.dma_start(RIP[:, :], I["rip"]).then_inc(ld["page"], 16)
            act.dma_start(NG[:, :, :], I["norm_gain"][0].rearrange("r (k p) -> p r k", p=P)).then_inc(ld["small"], 16)
            act.dma_start(QG[:, :, :].rearrange("p a d -> p (a d)"),
                          I["qk_gain"].rearrange("l a d -> l (a d)").to_broadcast([P, 6 * HD])).then_inc(ld["small"], 16)
            act.dma_start(B1[:, :], I["cmp_b1"][0].rearrange("v e -> e v")).then_inc(ld["small"], 16)
            act.dma_start(W2[:, :, :], I["cmp_w2"][0].rearrange("v e d -> e v d")).then_inc(ld["small"], 16)
            for q in range(2):
                act.dma_start(PW[q * HD:(q + 1) * HD, :, :],
                              I["pool_w"][0].rearrange("(c q) i e -> q i c e", q=2)[q]).then_inc(ld["small"], 16)
            act.dma_start(PSC[:, :], I["pool_scale"][0].rearrange("(c p) -> p c", p=P)).then_inc(ld["small"], 16)
            act.wait_ge(ld["small"], SMALL)
            act.wait_ge(ld["const"], 16)

            def evac(b, kv, j):
                n = 8 * kv + j
                act.wait_ge(t_done, b * 16 + (n + 1))
                act.wait_ge(m_done, b * 4 + (2 * kv + 2))
                for s in range(2):
                    last = act.activation(PTB[kv][s * HD:(s + 1) * HD, 0, j, :], PS[0:HD, j % 4, s * 256:(s + 1) * 256],
                                          ACT.Copy)
                last.then_inc(ev_act, 1)

            def silu(b, m):
                act.wait_ge(m_done, b * 4 + (4 + m + 1))
                act.wait_ge(w_done, b * 4 + (m + 1))
                act.activation(HIDC[:, m % 2, 0:255], PS[:, 4 + m % 2, 0:255], ACT.Silu, bias=B1[:, m // 2:m // 2 + 1])\
                    .then_inc(silu_done, 1)

            def compress(b, last):
                for j in range(4):
                    evac(b, 1, j)
                silu(b, 0)
                for j in range(4, 8):
                    evac(b, 1, j)
                silu(b, 1)
                if not last:
                    for j in range(4):
                        evac(b + 1, 0, j)
                silu(b, 2)
                if not last:
                    for j in range(4, 7):
                        evac(b + 1, 0, j)
                silu(b, 3)
                if not last:
                    evac(b + 1, 0, 7)

            def rms(r):
                act.wait_ge(rs[r]["sum"], 1)
                act.activation(RB, PS[:, 0:2, 0:HALF], ACT.Sqrt, bias=eps, scale=1.0 / D).then_inc(rs[r]["root"], 1)

            rms(0)
            act.sem_inc(w_done, 2)
            act.wait_ge(hid_zero, 1)
            for j in range(8):
                evac(0, 0, j)
            with act.Fori(0, NB - 1) as it:
                compress(it, False)
            compress(NB - 1, True)
            def parts(r):
                for k in range(KD):
                    act.wait_ge(rs[r]["f"], k + 1)
                    act.activation(HNH[:, k, :], HNF[:, k, :], ACT.Copy).then_inc(rs[r]["hi"], 1)

            def lead(L, n, it=0, step=0, shift=0):
                sl = L % RING
                act.wait_ge(landed[sl], it * (4 * step) + 16 * (L // RING + 1))
                act.activation(WHI[:, sl, 0:n], RAW[:, sl, 0:n], ACT.Copy).then_inc(w_hi, 1)

            def ffn(f, after):
                for blk in range(2):
                    L0 = L_FFN[f] + blk * L_BLOCK
                    e0 = blk * (BCH + KD)

                    def chunk(m, it, step, nxt):
                        e = e0 + m
                        lead(L0 + 2 * m + 2, nxt, it, 2 * step)
                        lead(L0 + 2 * m + 3, nxt, it, 2 * step)
                        act.wait_ge(w_used, it * (2 * step) + (L0 + 2 * m + 1))
                        act.wait_ge(ff[f]["free"], it * step + (e + 1))
                        act.activation(GB[:, e % 2, :, :], PS[:, 4 * (e % 2):4 * (e % 2) + 2, 0:HALF], ACT.Silu)\
                            .then_inc(ff[f]["silu"], 1)
                        act.wait_ge(ff[f]["mul"], it * step + (blk * BCH + m + 1))
                        row = bass.ds(it * step + m, 1) if step else slice(m, m + 1)
                        act.activation(HIDH[:, row, :], HIDF[:, row, :], ACT.Copy).then_inc(ff[f]["hi"], 1)

                    with act.Fori(0, BCH // 2) as it:
                        for u in range(2):
                            chunk(u, it, 2, KD * P)
                    chunk(BCH - 1, 0, 0, SLOT)
                    LO = L0 + 2 * BCH
                    for oc in range(KD):
                        if oc + 2 < KD:
                            lead(LO + oc + 2, SLOT)
                        elif blk == 0:
                            lead(LO + oc + 2, KD * P)
                        elif after:
                            lead(LO + oc + 2, after)

            lead(0, KD * P)
            lead(1, KD * P)
            parts(0)
            act.wait_ge(ck_ss, 1)
            act.activation(SSC, SSC, ACT.Sqrt, bias=eps, scale=1.0 / HD).then_inc(ck_sq, 1)
            ffn(0, KH * CG)
            rms(1)
            parts(1)
            due = {}
            for n, (_, nh, _, off) in enumerate(SECTIONS):
                due.setdefault(5 * section_end(n) + 9, []).append((n, nh, off))
            for x in range(5 * NCG):
                c, tt = x // 5, x % 5
                R, n = tile_rows(tt), min(CG, COLS - c * CG)
                if tt == 0 and c + 1 < NCG:
                    m = min(CG, COLS - (c + 1) * CG)
                    lead(L_IN + 2 * c + 2, KH * m)
                    lead(L_IN + 2 * c + 3, KH * m)
                act.wait_ge(pj_mm, x + 1)
                src = PS[0:P, x % 8, 0:n] if tt < 4 else PS[P - NS:P, x % 8, 0:n]
                act.activation(PROJ[0:R, tt, c * CG:c * CG + n], src, ACT.Copy).then_inc(pj_ev, 1)
                for m, nh, off in due.get(x, []):
                    act.wait_ge(hn_ss, m + 1)
                    ss = slice(off, off + nh)
                    act.activation(SS[:, 0:4, ss], SS[:, 0:4, ss], ACT.Sqrt, bias=eps, scale=1.0 / HD)
                    act.activation(SS[0:NS, 4, ss], SS[0:NS, 4, ss], ACT.Sqrt, bias=eps[0:NS, :], scale=1.0 / HD)\
                        .then_inc(hn_rt, 1)
            act.wait_ge(pj_ev, 5 * NCG)
            for m in range(ITEMS):
                act.wait_ge(qt_mm, m + 1)
                dst = QT[:, m, :] if m < IT_U else UT[:, m - IT_U, 16:528]
                act.activation(dst, PS[:, 2 * (m % 4), :], ACT.Copy).then_inc(qt_act, 1)
            for rr, ts in ((P, slice(0, 4)), (NS, slice(4, 5))):
                act.activation(GT[0:rr, ts, :], PROJ[0:rr, ts, C_G:C_G + 18], ACT.Sigmoid).then_inc(cp_act, 1)
                for at, c, n in ((0, C_SLCV, P), (P, C_WINV, P), (256, C_VB, 384)):
                    act.activation(VV[0:rr, ts, at:at + n], PROJ[0:rr, ts, c:c + n], ACT.Copy).then_inc(cp_act, 1)
            for kv in range(2):
                act.wait_ge(pc["tr"], kv + 1)
                for h in range(2):
                    for s in range(2):
                        src = PS[h * HD:(h + 1) * HD, kv, :].rearrange("p (s u n) -> p s u n", s=8, u=2)[:, :, s, :]
                        last = act.activation(PTC[s * HD:(s + 1) * HD, kv, h, :, :], src, ACT.Copy)
                last.then_inc(pc["ev"], 1)
            act.wait_ge(pc["mm"], 1)
            for kv in range(2):
                act.activation(HIDP[:, 2 * kv:2 * kv + 2, 0:31],
                               PS[:, 2, 64 * kv:64 * kv + 64].rearrange("p (q n) -> p q n", q=2)[:, :, 0:31],
                               ACT.Silu, bias=B1[:, kv:kv + 1]).then_inc(pc["silu"], 1)
            act.wait_ge(pc["ss"], 1)
            act.activation(SSP, SSP, ACT.Sqrt, bias=eps[0:31, :], scale=1.0 / HD).then_inc(pc["rt"], 1)
            act.wait_ge(po["mm"], 1)
            for c in range(2):
                act.activation(MIXT[:, 6 + c, 0:TP], PS[:, 5 + c, :], ACT.Copy, scale=PSC[:, c:c + 1]).then_inc(po["ev"], 1)
                act.activation(MIXT[:, 6 + c, TP:T], PS[:, 7, c * NS:(c + 1) * NS], ACT.Copy, scale=PSC[:, c:c + 1])\
                    .then_inc(po["ev"], 1)

            def exps(u):
                U = units[u]
                i = U["i"]
                if U["new"]:
                    act.wait_ge(pa["cnb"], i + 1)
                    act.activation(SC[:, :, 0:31], SC[:, :, 0:31], ACT.Exp, scale=SCALE).then_inc(pa["cexp"], 1)
                act.wait_ge(pa["nb"], u + 1)
                for x, b in enumerate(U["br"]):
                    n = (i + 1 - b["j0"]) * P
                    y = x if U["nsa"] else 0
                    last = act.activation(SB[:, u % 3, x, 0:n], SB[:, u % 3, x, 0:n], ACT.Exp,
                                          bias=NBI[:, u % 3, y:y + 1], scale=SCALE, accum_out=DEN[:, u % 3, x:x + 1])
                last.then_inc(pa["exp"], 1)

            def tevac(u):
                U = units[u]
                for x in range(3):
                    B = 3 * u + x
                    act.wait_ge(pa["t"], B + 1)
                    if B >= 3:
                        act.wait_ge(pa["pv"], B - 2)
                    if U["nsa"] and x == 2:
                        act.activation(PTS[0:31, B % 3, 0:P], PS[0:31, 3 + B % 2, 0:P], ACT.Copy).then_inc(pa["tev"], 1)
                    else:
                        n = (U["i"] + 1 - U["br"][x]["j0"]) * P
                        act.activation(PTS[:, B % 3, 0:n], PS[:, 3 + B % 2, 0:n], ACT.Copy).then_inc(pa["tev"], 1)

            exps(0)
            for u in range(NU):
                if u + 1 < NU:
                    exps(u + 1)
                tevac(u)

            def front(U, between=None):
                for x in range(len(U["tc"])):
                    n = U["kt0"] + x
                    w = len(U["tc"][x][0]) * P
                    if between and x == 2:
                        between()
                    act.wait_ge(sa["kt"], n + 1)
                    if n >= 3:
                        act.wait_ge(sa["s"], score_of[n - 3] + 1)
                    act.activation(KTB(n)[:, 0:w], PS[:, n % 2, 0:w], ACT.Copy).then_inc(sa["ktev"], 1)

            def expo(U):
                R, x = U["rows"], U["x"]
                act.wait_ge(sa["nb"], U["f"] + 1)
                n = 255 if U["kind"] == "cmp" else U["buf"].shape[1]
                act.activation(U["buf"][:, 0:n], U["buf"][:, 0:n], ACT.Exp, bias=SNB[0:R, x:x + 1],
                               scale=SCALE, accum_out=SDEN[0:R, x:x + 1]).then_inc(sa["exp"], 1)

            def pev(U):
                R, k, b = U["rows"], U["kind"], U["b"]
                back = 2 if k == "cmp" else 1
                if b >= back:
                    act.wait_ge(sa["pv"], U_[k, b - back]["n"] + 1)
                elif k != "cmp":
                    act.wait_ge(sa["pv"], NB)
                for x, tiles in enumerate(U["pts"]):
                    n = U["pt0"] + x
                    rows = tiles[0][1]
                    act.wait_ge(sa["pt"], n + 1)
                    w = len(tiles) * R
                    act.activation(U["ptdst"][x][0:rows, 0:w], PS[0:rows, 4 + n % 2, 0:w], ACT.Copy)\
                        .then_inc(sa["ptev"], 1)

            for b in range(NB):
                expo(cmp_units[b])
                pev(cmp_units[b])
            front(U_["slc", 0])
            expo(U_["slc", 0])
            for b in range(NB):
                front(U_["win", b])
                front(U_["dil", b])
                expo(U_["win", b])
                if b + 1 < NB:
                    front(U_["slc", b + 1], lambda: expo(U_["dil", b]))
                else:
                    expo(U_["dil", b])
                pev(U_["win", b])
                pev(U_["dil", b])
                if b + 1 < NB:
                    expo(U_["slc", b + 1])
                pev(U_["slc", b])

            rms(2)
            L0 = L_FFN[1]
            lead(L0, KD * P)
            lead(L0 + 1, KD * P)
            parts(2)
            ffn(1, 0)
            for x in range(1, 10, 2):
                R = tile_rows(x // 2)
                act.wait_ge(y_tr, x + 1)
                act.wait_ge(y_ev, x)
                act.activation(YO[0:R, x // 2, 512:1024], PS[0:R, x % 4, :], ACT.Copy).then_inc(y_ev, 1)

        @block.vector
        def _(dve):
            n_link = [0]

            def link(ins):
                n_link[0] += 1
                ins.then_inc(d_ch, 1)
                dve.wait_ge(d_ch, n_link[0])

            V = nc.vector
            dve.sem_inc(ev_dve, 4)
            dve.sem_inc(w_copied, 4)
            dve.wait_ge(ld["page"], 48)
            V.tensor_copy(PTF[:, :], PTI[:, :]).then_inc(ix_f, 1)
            dve.wait_ge(ix_mm, 1)
            V.tensor_scalar(IXC[:, :, :], PS[:, 7, 0:2 * NB].rearrange("p (s b) -> p s b", s=2), 8.0, RIP[:, 0:1],
                            ALU.mult, ALU.add).then_inc(ix_ok, 1)
            V.tensor_scalar(IXS[:, :, :], PS[:, 7, 2 * NB:10 * NB].rearrange("p (s b) -> p s b", s=8), 32.0,
                            RIP[:, 1:2], ALU.mult, ALU.add).then_inc(ix_ok, 1)
            for k in range(KD):
                dve.wait_ge(x_tr, k + 1)
                V.tensor_copy(XT[:, k, 0:TP], PS[:, k % 6, :]).then_inc(x_ev, 1)
            V.tensor_copy(XT[:, :, TP:T], PS[:, 6, 0:KD * NS].rearrange("p (k t) -> p k t", k=KD)).then_inc(x_ev, 1)
            V.memset(HIDC[:, :, 255:256], 0.0).then_inc(hid_zero, 1)

            def squares(r):
                for k in range(KD):
                    V.tensor_tensor(HNk[:, k, :], XT[:, k, :], XT[:, k, :], ALU.mult).then_inc(rs[r]["sq"], 1)
                dve.wait_ge(rs[r]["root"], 1)
                link(V.reciprocal(RB, RB))

            dve.wait_ge(x_ev, KD + 1)
            squares(0)
            dve.wait_ge(ld["small"], SMALL)

            def evac(b, kv, j):
                n = 8 * kv + j
                dve.wait_ge(t_done, b * 16 + (n + 1))
                dve.wait_ge(m_done, b * 4 + (2 * kv + 2))
                for s in range(2):
                    last = V.tensor_copy(PTB[kv][s * HD:(s + 1) * HD, 1, j, :],
                                         PS[HD:P, j % 4, s * 256:(s + 1) * 256])
                last.then_inc(ev_dve, 1)

            CKb = CK.rearrange("p (b c n) -> p b c n", b=NB, c=2)

            def rows_out(b, m):
                dve.wait_ge(w_done, b * 4 + (2 + m + 1))
                src = PS[:, 6 + m % 2, :].rearrange("p (c q d) -> p c q d", c=2, q=4)[:, :, m, :]
                dst = CKb if m < 2 else CV[:, :, :, :]
                h = m % 2
                bb = bass.ds(b, 1) if not isinstance(b, int) else slice(b, b + 1)
                V.tensor_copy(dst[:, bb, :, h * HD:(h + 1) * HD].rearrange("p a c d -> p (a c) d"), src)\
                    .then_inc(w_copied, 1)

            def compress(b, last):
                for j in range(8):
                    evac(b, 1, j)
                rows_out(b, 0)
                if not last:
                    for j in range(4):
                        evac(b + 1, 0, j)
                rows_out(b, 1)
                if not last:
                    for j in range(4, 7):
                        evac(b + 1, 0, j)
                rows_out(b, 2)
                if not last:
                    evac(b + 1, 0, 7)
                rows_out(b, 3)

            for j in range(8):
                evac(0, 0, j)
            with dve.Fori(0, NB - 1) as it:
                compress(it, False)
            compress(NB - 1, True)

            def hn(r, first_loads):
                for k in range(KD + 1):
                    if k < KD:
                        V.scalar_tensor_tensor(HNF[:, k, :].rearrange("p (h t) -> p h t", h=2),
                                               XT[:, k, :].rearrange("p (h t) -> p h t", h=2), NG[:, r, k:k + 1], RB,
                                               ALU.mult, ALU.mult).then_inc(rs[r]["f"], 1)
                    if k in (0, 1) and first_loads:
                        first_loads[k]()
                    if k:
                        dve.wait_ge(rs[r]["hi"], k)
                        V.tensor_tensor(HNL[:, k - 1, :], HNF[:, k - 1, :], HNH[:, k - 1, :].bitcast(F32), ALU.subtract)\
                            .then_inc(rs[r]["lo"], 1)

            def split(L):
                return L if L <= L_OUT else L - KD

            def remain(L, n, it=0, step=0):
                sl = L % RING
                dve.wait_ge(w_hi, it * step + (split(L) + 1))
                V.tensor_tensor(WLO[:, sl, 0:n], RAW[:, sl, 0:n], WHI[:, sl, 0:n].bitcast(F32), ALU.subtract)\
                    .then_inc(w_lo, 1)

            def ffn(f, after):
                for blk in range(2):
                    L0 = L_FFN[f] + blk * L_BLOCK
                    e0 = blk * (BCH + KD)

                    def hid_lo(m, it, step):
                        dve.wait_ge(ff[f]["hi"], it * step + (blk * BCH + m + 1))
                        dve.sem_inc(ff[f]["free"], 1)
                        row = bass.ds(it * step + m, 1) if step else slice(m, m + 1)
                        V.tensor_tensor(HIDL[:, row, :], HIDF[:, row, :], HIDH[:, row, :].bitcast(F32), ALU.subtract)\
                            .then_inc(ff[f]["lo"], 1)

                    def chunk(m, it, step, nxt):
                        e = e0 + m
                        remain(L0 + 2 * m + 2, nxt, it, 2 * step)
                        remain(L0 + 2 * m + 3, nxt, it, 2 * step)
                        dve.wait_ge(ff[f]["silu"], it * step + (blk * BCH + m + 1))
                        dve.wait_ge(w_used, it * (2 * step) + (L0 + 2 * m + 2))
                        row = bass.ds(it * step + m, 1) if step else slice(m, m + 1)
                        V.tensor_tensor(HIDF[:, row, :].rearrange("p a (h t) -> p (a h) t", h=2), GB[:, e % 2, :, :],
                                        PS[:, 4 * (e % 2) + 2:4 * (e % 2) + 4, 0:HALF], ALU.mult).then_inc(ff[f]["mul"], 1)
                        hid_lo(m, it, step)

                    with dve.Fori(0, BCH // 2) as it:
                        for u in range(2):
                            chunk(u, it, 2, KD * P)
                    chunk(BCH - 1, 0, 0, SLOT)
                    LO, eo = L0 + 2 * BCH, e0 + BCH
                    for oc in range(KD):
                        e = eo + oc
                        if oc + 2 < KD:
                            remain(LO + oc + 2, SLOT)
                        elif blk == 0:
                            remain(LO + oc + 2, KD * P)
                        elif after:
                            remain(LO + oc + 2, after)
                        dve.wait_ge(w_used, LO + oc + 1)
                        x = XT[:, oc, :].rearrange("p (h t) -> p h t", h=2)
                        V.scalar_tensor_tensor(x, PS[:, 4 * (e % 2):4 * (e % 2) + 2, 0:HALF], 0.5, x, ALU.mult, ALU.add)\
                            .then_inc(ff[f]["free"], 1)

            dve.wait_ge(m_done, 4 + 4 * NB)
            hn(0, [lambda: remain(0, KD * P), lambda: remain(1, KD * P)])
            dve.wait_ge(w_copied, 4 + 4 * NB)
            link(V.tensor_tensor(CKS, CK, CK, ALU.mult))
            V.tensor_reduce(SSC, CKS.rearrange("p (n d) -> p n d", d=HD), AX.X, ALU.add).then_inc(ck_ss, 1)
            dve.wait_ge(ck_sq, 1)
            link(V.reciprocal(SSC, SSC))
            ck3 = CK.rearrange("p (n d) -> p n d", d=HD)
            link(V.tensor_tensor(ck3, ck3, SSC.unsqueeze(2).to_broadcast([P, 32, HD]), ALU.mult))
            V.tensor_tensor(ck3, ck3, QG[:, 1:2, :].to_broadcast([P, 32, HD]), ALU.mult).then_inc(ck_n, 1)
            ffn(0, KH * CG)
            dve.wait_ge(ff[0]["free"], 2 + 2 * (BCH + KD))
            for k in range(KD):
                V.tensor_tensor(HNk[:, k, :], XT[:, k, :], XT[:, k, :], ALU.mult).then_inc(rs[1]["sq"], 1)
            dve.wait_ge(ck_t, 1)
            for n in range(4):
                last = V.tensor_copy(CKT[:, 2 * n:2 * n + 2, :], PS[:, 4 + n, :].rearrange("p (b c) -> p b c", b=2))
            last.then_inc(ck_ev, 1)
            dve.wait_ge(rs[1]["root"], 1)
            link(V.reciprocal(RB, RB))
            hn(1, None)
            def squares_of(n):
                c, nh, _, off = SECTIONS[n]
                dve.wait_ge(pj_ev, 5 * section_end(n))
                if n:
                    dve.wait_ge(hn_ss, n)
                for R, ts in ((P, (0, 2)), (P, (2, 4)), (NS, (4, 5))):
                    nt = ts[1] - ts[0]
                    x = PROJ[0:R, ts[0]:ts[1], c:c + nh * HD]
                    q = SQT[0:R, 0:nt * nh * HD]
                    link(V.tensor_tensor(q.rearrange("p (t n) -> p t n", t=nt), x, x, ALU.mult))
                    ins = V.tensor_reduce(SS[0:R, ts[0]:ts[1], off:off + nh], q.rearrange("p (t n d) -> p t n d", t=nt, d=HD),
                                          AX.X, ALU.add)
                    if R == NS:
                        ins.then_inc(hn_ss, 1)
                    else:
                        link(ins)

            def scale_by(n):
                c, nh, g, off = SECTIONS[n]
                dve.wait_ge(hn_rt, n + 1)
                for R, ts, nt in ((P, slice(0, 4), 4), (NS, slice(4, 5), 1)):
                    ss = SS[0:R, ts, off:off + nh]
                    link(V.reciprocal(ss, ss))
                    x = PROJ[0:R, ts, c:c + nh * HD].rearrange("p t (n d) -> p t n d", d=HD)
                    link(V.tensor_tensor(x, x, ss.unsqueeze(3).to_broadcast([R, nt, nh, HD]), ALU.mult))
                    gain = QG[0:R, g:g + 1, :].unsqueeze(1)
                    if n == 0:
                        for h in range(2):
                            ins = V.tensor_tensor(QP[0:R, ts, :, h, :], x[:, :, 3 * h:3 * h + 3, :],
                                                  gain.to_broadcast([R, nt, 3, HD]), ALU.mult)
                    else:
                        ins = V.tensor_tensor(x, x, gain.to_broadcast([R, nt, nh, HD]), ALU.mult)
                ins.then_inc(qn, 1)

            for c in range(NCG + 2):
                if c + 1 < NCG:
                    for x in range(2):
                        remain(L_IN + 2 * c + 2 + x, KH * min(CG, COLS - (c + 1) * CG))
                for n in range(len(SECTIONS)):
                    if section_end(n) == c:
                        squares_of(n)
                    if section_end(n) + 2 == c:
                        scale_by(n)
            dve.wait_ge(w_used, L_OUT)
            V.memset(UT[:, :, 0:16], 0.0).then_inc(po["zero"], 1)
            for m in range(ITEMS):
                dve.wait_ge(qt_mm, m + 1)
                dst = QN[:, m, :] if m < IT_U else UTS[:, m - IT_U, :, 15:19]
                src = PS[:, 2 * (m % 4) + 1, 0:NS]
                if m >= IT_U:
                    src = src.rearrange("p (b t) -> p b t", b=NB)
                V.tensor_copy(dst, src).then_inc(qt_dve, 1)
            dve.wait_ge(po["st"], 1)
            for c in range(2):
                last = V.tensor_copy(UTS[:, c, :, 0:15], PS[:, 4, c * P:c * P + 120].rearrange("p (b t) -> p b t", b=NB))
            last.then_inc(po["stev"], 1)
            dve.wait_ge(po["stev"], 1)
            dve.wait_ge(po["zero"], 1)
            dve.wait_ge(qt_act, ITEMS)
            dve.wait_ge(qt_dve, ITEMS)
            dve.wait_ge(qt_mm, ITEMS)
            dve.wait_ge(cp_act, 8)
            dve.wait_ge(st_cmp, 16)
            dve.wait_ge(st_out, 16 * N_STATES)

            def windows(u, a, b_, dl, n0, n, head, nt):
                src, dst = u, a
                for step, w in enumerate((2, 4, 8, 16)):
                    sh = w // 2
                    link(V.tensor_tensor(dst[..., w - 1:n], src[..., w - 1:n], src[..., w - 1 - sh:n - sh], ALU.add))
                    c, q = step // 2, step % 2
                    r = slice(q * HD, (q + 1) * HD)
                    pw = const("pool_w")[r, c:c + 1]
                    link(V.scalar_tensor_tensor(dl[r, c], dst[r, c][..., n0:n], pw, u[r, c][..., n0:n],
                                                ALU.mult, ALU.subtract))
                    if head:
                        hd = const("pool_head")[r, c * 16:(c + 1) * 16]
                        link(V.tensor_tensor(PHD[r, c, :], dst[r, c, n0:n0 + 16], hd, ALU.mult))
                        link(V.tensor_tensor(dl[r, c, 0:16], PHD[r, c, :], u[r, c, n0:n0 + 16], ALU.subtract))
                    src, dst = dst, (b_ if dst is a else a)

            windows(UT, T1, T2, DL, 16, 528, True, TP)
            windows(UTS, T1S, T2S, DLS, 15, 19, False, NS)
            V.sem_inc(po["dl"], 1)
            dve.wait_ge(pc["w"], 1)
            V.tensor_copy(CVP, PS[0:31, 3, 2 * HD:4 * HD])
            link(V.tensor_copy(CKP, PS[0:31, 3, 0:2 * HD]))
            link(V.tensor_tensor(CKPS, CKP, CKP, ALU.mult))
            V.tensor_reduce(SSP, CKPS.rearrange("p (n d) -> p n d", d=HD), AX.X, ALU.add).then_inc(pc["ss"], 1)
            dve.wait_ge(pc["rt"], 1)
            link(V.reciprocal(SSP, SSP))
            kp = CKP.rearrange("p (n d) -> p n d", d=HD)
            link(V.tensor_tensor(kp, kp, SSP.unsqueeze(2).to_broadcast([31, 2, HD]), ALU.mult))
            V.tensor_tensor(kp, kp, QG[0:31, 1:2, :].to_broadcast([31, 2, HD]), ALU.mult).then_inc(pc["n"], 1)
            dve.wait_ge(pc["t"], 1)
            V.tensor_copy(CKTP[:, 0:31], PS[:, 2, 0:31]).then_inc(pc["ev2"], 1)

            def cmp_scores(i):
                dve.wait_ge(pa["cs"], 2 * i + 2)
                if i:
                    dve.wait_ge(pa["t"], 3 * (8 * (i - 1) + 5) + 3)
                s = SC[:, :, 0:31]
                add = const("cmp_add")[:, i * 32:i * 32 + 31].unsqueeze(1).to_broadcast([P, 6, 31])
                link(V.tensor_tensor(s, PS[:, 7, 0:192].rearrange("p (h n) -> p h n", h=6)[:, :, 0:31], add, ALU.add))
                link(V.tensor_reduce(CMX, s, AX.X, ALU.max))
                V.tensor_tensor(s, s, CMX.unsqueeze(2).to_broadcast([P, 6, 31]), ALU.subtract).then_inc(pa["cnb"], 1)

            def cmp_weights(i):
                s = SC[:, :, 0:31]
                keep = const("cmp_keep")[:, i * 32:i * 32 + 31].unsqueeze(1).to_broadcast([P, 6, 31])
                dve.wait_ge(pa["cexp"], i + 1)
                link(V.tensor_tensor(s, s, keep, ALU.mult))
                link(V.tensor_reduce(CDN, s, AX.X, ALU.add))
                link(V.tensor_scalar(CDN, CDN, 1.0e-30, None, ALU.max))
                link(V.reciprocal(CDN, CDN))
                link(V.tensor_tensor(CWT, CDN, GT[:, i, :].rearrange("p (h c) -> p h c", c=3)[:, :, 0], ALU.mult))
                V.tensor_tensor(s, s, CWT.unsqueeze(2).to_broadcast([P, 6, 31]), ALU.mult).then_inc(pa["cp"], 1)

            def lift(u):
                U = units[u]
                i = U["i"]
                if U["new"]:
                    cmp_scores(i)
                if u >= 3:
                    dve.wait_ge(pa["t"], 3 * (u - 3) + 3)
                for x, b in enumerate(U["br"]):
                    B = U["s0"] + x
                    dve.wait_ge(pa["s"], B + 1)
                    n = i - b["j0"]
                    s = SB[:, u % 3, x, :]
                    if n:
                        src, dst = PS[:, B % 3, 0:n * P], s[:, 0:n * P]
                        if b["off"] is None:
                            V.tensor_copy(dst, src)
                        else:
                            m = const(b["off"]).unsqueeze(1).to_broadcast([P, n, P])
                            V.tensor_tensor(dst.rearrange("p (j c) -> p j c", c=P),
                                            src.rearrange("p (j c) -> p j c", c=P), m, ALU.add)
                    V.tensor_tensor(s[:, n * P:(n + 1) * P], PS[:, B % 3, n * P:(n + 1) * P], const(b["diag"]),
                                    ALU.add).then_inc(pa["sev"], 1)
                dve.wait_ge(pa["sev"], U["s0"] + len(U["br"]))
                nb = NBI[:, u % 3, :]
                if U["nsa"]:
                    link(V.tensor_reduce(MX[:, u % 3, 0:2], SB[:, u % 3, 0:2, 0:(i + 1) * P], AX.X, ALU.max))
                    V.tensor_scalar(nb[:, 0:2], MX[:, u % 3, 0:2], -SCALE, None, ALU.mult).then_inc(pa["nb"], 1)
                else:
                    for x, b in enumerate(U["br"]):
                        ins = V.tensor_reduce(MX[:, u % 3, x:x + 1], SB[:, u % 3, x, 0:(i + 1 - b["j0"]) * P], AX.X,
                                              ALU.max)
                    link(ins)
                    link(V.tensor_reduce(MX1[:, u % 3:u % 3 + 1], MX[:, u % 3, :], AX.X, ALU.max))
                    V.tensor_scalar(nb[:, 0:1], MX1[:, u % 3:u % 3 + 1], -SCALE, None, ALU.mult).then_inc(pa["nb"], 1)

            def weigh(u):
                U = units[u]
                i = U["i"]
                if U["new"]:
                    cmp_weights(i)
                dve.wait_ge(pa["exp"], u + 1)
                w, d = WT[:, u % 3, :], DEN[:, u % 3, :]
                if U["nsa"]:
                    link(V.reciprocal(w[:, 0:2], d[:, 0:2]))
                    link(V.tensor_tensor(w[:, 0:2], w[:, 0:2], GT[:, i, U["hq"] * 3 + 1:U["hq"] * 3 + 3], ALU.mult))
                else:
                    link(V.tensor_reduce(w[:, 2:3], d, AX.X, ALU.add))
                    link(V.reciprocal(w[:, 0:1], w[:, 2:3]))
                for x, b in enumerate(U["br"]):
                    n = (i + 1 - b["j0"]) * P
                    y = x if U["nsa"] else 0
                    ins = V.tensor_scalar(SB[:, u % 3, x, 0:n], SB[:, u % 3, x, 0:n], w[:, y:y + 1], None, ALU.mult)
                ins.then_inc(pa["p"], 1)

            def out(u):
                U = units[u]
                c = slice(U["i"] * P, (U["i"] + 1) * P)
                dve.wait_ge(pa["pv"], 3 * u + 3)
                if U["nsa"]:
                    r = slice(U["hq"] % 2 * HD, U["hq"] % 2 * HD + HD)
                    V.tensor_copy(MIXT[r, U["hq"] // 2, c], PS[r, 5 + u % 2, 0:P]).then_inc(pa["oev"], 1)
                else:
                    r = slice(U["h"] * HD, (U["h"] + 1) * HD)
                    V.tensor_copy(MIXT[r, 3:6, c], PS[r, 5 + u % 2, 0:3 * P].rearrange("p (g t) -> p g t", g=3))\
                        .then_inc(pa["oev"], 1)

            lift(0)
            lift(1)
            for u in range(NU):
                weigh(u)
                if u + 2 < NU:
                    lift(u + 2)
                if u >= 1:
                    out(u - 1)
            out(NU - 1)

            dve.wait_ge(pa["oev"], NU)
            link(V.memset(QA[:, :, :], 0.0))
            link(V.memset(QD[:, :, :, :], 0.0))
            for h in range(2):
                r = slice(h * HD, (h + 1) * HD)
                for g in range(3):
                    V.tensor_copy(QA[r, :, (h * 3 + g) * TS:(h * 3 + g + 1) * TS],
                                  QN[r, g, :].rearrange("p (b t) -> p b t", b=NB))
                    ins = V.tensor_copy(QD[r, g, :, h * TS:(h + 1) * TS],
                                        QN[r, IT_QB + g, :].rearrange("p (b t) -> p b t", b=NB))
            V.memset(SCS[:, :, 255:256], 0.0).then_inc(sa["q"], 1)
            dve.wait_ge(sa["gmm"], 1)
            link(V.tensor_tensor(GX, PS[0:24, 5, 0:144].rearrange("p (b c) -> p b c", b=NB),
                                 const("gate_pick").unsqueeze(1).to_broadcast([24, NB, 18]), ALU.mult))
            V.tensor_reduce(GS, GX.rearrange("p b (h c) -> p b c h", c=3), AX.X, ALU.add).then_inc(sa["gts"], 1)
            dve.wait_ge(sa["gts"], 1)

            def front(U):
                R, X = U["rows"], U["x"]
                if former(U):
                    dve.wait_ge(sa["pv"], former(U)["n"] + 1)
                for x, (tl, _, c, mask) in enumerate(U["tc"]):
                    s = U["s0"] + x
                    w = len(tl) * P
                    dve.wait_ge(sa["s"], s + 1)
                    src, dst = PS[0:R, 2 + s % 2, 0:w], U["buf"][:, c:c + w]
                    if mask[0] == "sel":
                        m = SELM[:, U["b"] * 64 + 8 * mask[1]:U["b"] * 64 + 8 * mask[1] + 8]
                        m = m.unsqueeze(1).unsqueeze(3).to_broadcast([24, 4, 8, 16])
                        V.tensor_tensor(dst.rearrange("p (j a r) -> p j a r", j=4, a=8),
                                        src.rearrange("p (j a r) -> p j a r", j=4, a=8), m, ALU.add)\
                            .then_inc(sa["sev"], 1)
                    elif mask[0] == "step":
                        m = const(mask[1]).unsqueeze(2).to_broadcast([R, 4, P])
                        V.tensor_tensor(dst.rearrange("p (j r) -> p j r", j=4), src.rearrange("p (j r) -> p j r", j=4),
                                        m, ALU.add).then_inc(sa["sev"], 1)
                    else:
                        V.tensor_tensor(dst, src, const(mask[1]), ALU.add).then_inc(sa["sev"], 1)
                for x, (_, _, c, w, mask) in enumerate(U["nc"]):
                    s = U["s0"] + len(U["tc"]) + x
                    dve.wait_ge(sa["s"], s + 1)
                    src, dst = PS[0:R, 2 + s % 2, 0:w], U["buf"][:, c:c + w]
                    if mask is None:
                        V.tensor_copy(dst, src).then_inc(sa["sev"], 1)
                    else:
                        V.tensor_tensor(dst, src, const(mask[0])[:, mask[1] * 32:mask[1] * 32 + 32], ALU.add)\
                            .then_inc(sa["sev"], 1)
                dve.wait_ge(sa["sev"], U["s0"] + len(U["tc"]) + len(U["nc"]))
                n = 255 if U["kind"] == "cmp" else U["buf"].shape[1]
                link(V.tensor_reduce(SMX[0:R, X:X + 1], U["buf"][:, 0:n], AX.X, ALU.max))
                V.tensor_scalar(SNB[0:R, X:X + 1], SMX[0:R, X:X + 1], -SCALE, None, ALU.mult).then_inc(sa["nb"], 1)

            def weights(U):
                R, X, k, b = U["rows"], U["x"], U["kind"], U["b"]
                dve.wait_ge(sa["exp"], U["f"] + 1)
                w = SWT[0:R, X:X + 1]
                if b >= 2:
                    dve.wait_ge(sa["pv"], U_[k, b - 2]["n"] + 1)
                link(V.reciprocal(w, SDEN[0:R, X:X + 1]))
                if k == "cmp":
                    link(V.tensor_scalar(EXR[:, b % 2, :], const("sum_heads")[:, b * 64:(b + 1) * 64], w, None, ALU.mult))
                if k != "dil":
                    br = KINDS.index(k)
                    link(V.tensor_tensor(w, w, GS[:, b, br:br + 1], ALU.mult))
                V.tensor_scalar(DG[0:R, X, 0:R], ident[0:R, 0:R], w, None, ALU.mult).then_inc(sw[k], 1)

            def outs(U):
                dve.wait_ge(sa["pv"], U["n"] + 1)
                src = PS[:, out_bank(U), 0:24]
                if U["kind"] == "cmp":
                    V.tensor_copy(U["out"], src).then_inc(sa["oev"], 1)
                elif U["kind"] == "dil":
                    V.tensor_copy(U["out"], src.rearrange("p (g r) -> p g r", g=3)).then_inc(sa["oev"], 1)
                else:
                    dve.wait_ge(sa["oev"], U["n"])
                    V.tensor_tensor(U["out"], src, U["out"], ALU.add).then_inc(sa["oev"], 1)

            def choose():
                dve.wait_ge(sa["imp"], 1)
                V.memset(SCR[:, 64:65], 0.0)
                link(V.memset(IM[:, 255:256], 0.0))
                link(V.tensor_copy(IM[:, 0:255], PS[0:64, 7, 0:255]))
                link(V.tensor_reduce(SCR[:, 0:64], IM.rearrange("p (j c) -> p j c", c=4), AX.X, ALU.add))
                link(V.tensor_tensor(SCR[:, 1:64], SCR[:, 1:64], IM[:, 3:252:4], ALU.add))
                link(V.tensor_tensor(SCR, SCR, const("force"), ALU.add))
                link(V.max(M8, SCR))
                link(V.match_replace(RPL, M8, SCR, NEG))
                V.tensor_tensor(SEL, RPL, SCR, ALU.not_equal).then_inc(sa["sel"], 1)
                dve.wait_ge(sa["selmm"], 1)
                V.tensor_scalar(SELM, PS[0:24, 7, :], -1.0, -NEG, ALU.add, ALU.mult).then_inc(sa["selm"], 1)
                dve.wait_ge(sa["selm"], 1)

            front(cmp_units[0])
            for b in range(NB):
                weights(cmp_units[b])
                if b + 1 < NB:
                    front(cmp_units[b + 1])
                outs(cmp_units[b])
            choose()
            front(U_["slc", 0])
            for b in range(NB):
                front(U_["win", b])
                weights(U_["slc", b])
                front(U_["dil", b])
                weights(U_["win", b])
                if b + 1 < NB:
                    front(U_["slc", b + 1])
                weights(U_["dil", b])
                outs(U_["win", b])
                outs(U_["dil", b])
                outs(U_["slc", b])
            dve.wait_ge(sa["oev"], NSU)
            for hq in range(6):
                h, g = hq // 3, hq % 3
                e = slice(hq % 2 * HD, hq % 2 * HD + HD)
                V.tensor_copy(MIXT[e, hq // 2, TP:T].rearrange("p (b t) -> p b t", b=NB),
                              OA[h * HD:(h + 1) * HD, :, hq * TS:(hq + 1) * TS])
            for h in range(2):
                r = slice(h * HD, (h + 1) * HD)
                for g in range(3):
                    ins = V.tensor_copy(MIXT[r, 3 + g, TP:T].rearrange("p (b t) -> p b t", b=NB),
                                        OD[r, :, g, h * TS:(h + 1) * TS])
            ins.then_inc(sa["ex"], 1)
            for oc in range(KD):
                dve.wait_ge(w_used, L_OUT + oc + 1)
                x = XT[:, oc, :].rearrange("p (h t) -> p h t", h=2)
                V.tensor_tensor(x, x, PS[:, 4 * (oc % 2):4 * (oc % 2) + 2, 0:HALF], ALU.add).then_inc(wo_ev, 1)
            dve.wait_ge(wo_ev, KD)
            squares(2)
            L0 = L_FFN[1]
            hn(2, [lambda: remain(L0, KD * P), lambda: remain(L0 + 1, KD * P)])
            ffn(1, 0)
            for x in range(0, 10, 2):
                R = tile_rows(x // 2)
                dve.wait_ge(y_tr, x + 1)
                if x:
                    dve.wait_ge(y_ev, x)
                V.tensor_copy(YO[0:R, x // 2, 0:512], PS[0:R, x % 4, :]).then_inc(y_ev, 1)


SMALL = 16 * 7
N_STATES = 7 + 12

_INS = ["x_prompt", "x_sample", "cache_cmp_kv", "cache_slc_kv", "cache_win_kv", "cache_dil0_kv", "cache_dil1_kv",
        "cache_dil2_kv", "state_pool", "page_table", "w_in", "w_out", "norm_gain", "qk_gain", "ffn_in", "ffn_out",
        "cmp_w1", "cmp_b1", "cmp_w2", "pool_w", "pool_scale"]
_OUTS = [("y_p", (1, TP, D)), ("y_s", (NB, TS, D)),
         ("cmp_p", (1, 1, TP, 2, 2, HD)), ("cmp_s", (1, NB, TS, 2, 2, HD)),
         ("slc_p", (1, 1, TP, 2, 2, HD)), ("slc_s", (1, NB, TS, 2, 2, HD)),
         ("win_p", (1, 1, 512, 2, 2, HD)), ("win_s", (1, NB, 512, 2, 2, HD)),
         ("dil0_p", (1, 1, 128, 2, 2, HD)), ("dil0_s", (1, NB, 128, 2, 2, HD)),
         ("dil1_p", (1, 1, 512, 2, 2, HD)), ("dil1_s", (1, NB, 512, 2, 2, HD)),
         ("dil2_p", (1, 1, 512, 2, 2, HD)), ("dil2_s", (1, NB, 2048, 2, 2, HD)),
         ("pool_p", (1, 1, 15, 256)), ("pool_s", (1, NB, 15, 256))]


def kernel(**inputs):
    import concourse.bacc as _bacc
    from concourse.bass_utils import run_bass_kernel_spmd as _run

    nc = _bacc.Bacc("TRN2", target_bir_lowering=False, num_devices=1)
    arrays, ins, outs = {}, {}, {}
    given = {n: np.ascontiguousarray(inputs[n]) for n in _INS}
    given["consts"] = constants()
    given["selp"] = page_selectors()
    given["rip"] = row_in_page()
    for name, a in given.items():
        arrays[f"in_{name}"] = a
        ins[name] = nc.dram_tensor(f"in_{name}", a.shape, mybir.dt.from_np(a.dtype), kind="ExternalInput").ap()
    for name, shape in _OUTS:
        outs[name] = nc.dram_tensor(f"out_{name}", shape, F32, kind="ExternalOutput").ap()
    build(nc, ins, outs)
    r = _run(nc, [arrays], core_ids=[0])
    return tuple(r.results[0][f"out_{name}"] for name, _ in _OUTS)
```

```python
from contextlib import ExitStack

import numpy as np

import concourse.bass as bass
from concourse import mybir

F32 = mybir.dt.float32
F32R = mybir.dt.float32r
I32 = mybir.dt.int32
U32 = mybir.dt.uint32
ALU = mybir.AluOpType
ACT = mybir.ActivationFunctionType
AX = mybir.AxisListType

P = 128
D = 1024
KD = D // P
TP, NB, TS = 512, 8, 4
NS = NB * TS
T = TP + NS
HALF = T // 2
QT_TILES = TP // P
PAGE, PAST = 128, 4096
NPG = PAST // PAGE
HD = 64
FF = 2816
FCH = FF // P
BCH = FCH // 2
COLS = 2578
SLOT = BCH * P
RING = 4
NCG = 8
CG = -(-COLS // (2 * NCG)) * 2
KH = KD // 2
L_BLOCK = 2 * BCH + KD
L_IN = 2 * L_BLOCK
L_OUT = L_IN + 2 * NCG
L_FFN = (0, L_OUT + KD)
L_ALL = L_FFN[1] + 2 * L_BLOCK
SLOTS = 7
SEL7 = SLOTS * 16
SCALE = HD ** -0.5
EPS = 1e-6
NEG = -1.0e30
WDIL = ((128, 1), (512, 4), (2048, 16))

C_Q, C_CMP, C_SLCK, C_SLCV, C_WINK, C_WINV, C_G = 0, 384, 640, 768, 896, 1024, 1152
C_QB, C_KB, C_VB, C_U = 1170, 1554, 1938, 2322
SECTIONS = ((C_Q, 6, 0, 0), (C_SLCK, 2, 2, 6), (C_WINK, 2, 3, 8), (C_QB, 6, 4, 10), (C_KB, 6, 5, 16))
IT_SLC, IT_WIN, IT_QB, IT_KB, IT_U, ITEMS = 3, 4, 5, 8, 11, 13


def const_layout():
    at, out = 0, {}
    for name, rows, n in (
        ("ident", P, P), ("ones", P, P), ("diag", P, P), ("band_prev", P, P),
        ("mod4_off", P, P), ("mod4_diag", P, P), ("mod16_off", P, P), ("mod16_diag", P, P),
        ("cmp_add", P, 4 * 32), ("cmp_keep", P, 4 * 32),
        ("win_past", P, 96), ("dil_past", P, 72), ("new_a", NS, NB * 24), ("new_d", NS, NB * 24),
        ("tok_rows", NS, NB * 24), ("seq_of", NB, 64), ("blocks", 64, 64), ("rows16", 64, 16), ("no_block", P, 1),
        ("pool_w", P, 2), ("pool_head", P, 32), ("force", 64, 64), ("eps", P, 1),
    ):
        out[name] = (at, rows, n)
        at += n
    return out, at


CL, CN = const_layout()


def constants():
    c = np.zeros((P, CN), np.float32)

    def put(name, a):
        at, rows, n = CL[name]
        c[:rows, at:at + n] = a.reshape(rows, n)

    q, k = np.arange(P)[:, None], np.arange(P)[None, :]
    add = lambda ok: np.where(ok, 0.0, NEG)
    put("ident", np.eye(P))
    put("ones", np.ones((P, P)))
    put("diag", add(k <= q))
    put("band_prev", add(k >= q))
    for d in (4, 16):
        put(f"mod{d}_off", add((q - k) % d == 0))
        put(f"mod{d}_diag", add(((q - k) % d == 0) & (k <= q)))
    pos = np.arange(4)[None, :, None] * P + np.arange(P)[:, None, None]
    seen = (np.arange(32)[None, None, :] * 16 + 31 <= pos) & (np.arange(32) < 31)[None, None, :]
    put("cmp_add", add(seen))
    put("cmp_keep", seen.astype(np.float32))
    ta, td = np.arange(24) % TS, np.arange(8) % TS
    key = np.arange(P)[:, None, None] * 4 + np.arange(4)[None, :, None]
    put("win_past", add(key > ta[None, None, :]))
    d0 = np.arange(P)[:, None] >= td[None, :]
    d12 = np.arange(4)[:, None] == td[None, :]
    put("dil_past", np.concatenate([add(d0)] + [np.tile(add(d12).reshape(1, 32), (P, 1))] * 2, 1))
    tok_b, tok_t = np.arange(NS)[:, None, None] // TS, np.arange(NS)[:, None, None] % TS
    own = tok_b == np.arange(NB)[None, :, None]
    put("new_a", add(own & (tok_t <= ta)))
    put("new_d", add(np.concatenate([own & (tok_t <= td)] + [own & (tok_t == td)] * 2, 2)))
    put("tok_rows", (own & (tok_t == ta)).astype(np.float32))
    put("seq_of", (np.arange(64)[None, :] // 8 == np.arange(NB)[:, None]).astype(np.float32))
    put("blocks", np.tile(np.arange(64.0), (64, 1)))
    put("rows16", np.tile(np.arange(16.0), (64, 1)))
    last = np.zeros((P, 1))
    last[P - 1] = NEG
    put("no_block", last)
    w = np.array([[2, 8], [4, 16]])[(np.arange(P) // 64)]
    put("pool_w", 1.0 / w)
    put("pool_head", 1.0 / np.minimum(w[:, :, None], np.arange(16)[None, None, :] + 1))
    f = np.zeros((64, 64))
    f[:, [0, 63]] = 1.0e4
    put("force", f)
    put("eps", np.full((P, 1), EPS))
    return c


def row_in_page():
    return (np.arange(P) % 8).astype(np.float32)[:, None]


def page_selectors():
    s = np.zeros((NPG, 2, P), np.float32)
    for half in range(2):
        s[half * 16 + np.arange(P) // 8, half, np.arange(P)] = 1.0
    return s.reshape(NPG, 2 * P)


def build(nc, I, O):
    ctx = ExitStack()
    with ctx:
        ctx.enter_context(nc.allow_non_contiguous_dma(reason="small transposed tables"))

        def sb(name, shape, dt=F32):
            return ctx.enter_context(nc.sbuf_tensor(name, shape, dt))

        def sem(name):
            return ctx.enter_context(nc.semaphore(name))

        FLOATS = dict(XT=KD * T, H=KD * T, BIG=5 * COLS, WR=2 * RING * SLOT, QTR=11 * TP, CKT=NB * 256, CV=NB * 2 * P,
                      VV=5 * 640, CO=CN, GB=4 * HALF)
        total = sum(8 * -(-n // 8) for n in FLOATS.values()) + 8
        sb("arena", [P, total])
        base = -(-(nc.sbuf_base - 4 * total) // 32) * 32
        place, at = {}, base
        for name, n in FLOATS.items():
            place[name] = at
            at += 32 * -(-n // 8)

        def put(name, shape, region, off=0, dt=F32):
            return nc.alloc_sbuf_tensor_at(name, shape, dt, offset=place[region] + 4 * off)

        XT = put("XT", [P, KD, T], "XT")
        HN = put("HN", [P, KD * T], "H")
        HNH = put("HNH", [P, KD, T], "H", dt=F32R)
        BIG = put("BIG", [P, 5 * COLS], "BIG")
        HIDH = put("HIDH", [P, BCH, T], "BIG", dt=F32R)
        HIDL = put("HIDL", [P, BCH, T], "BIG", BCH * T, dt=F32R)
        WR = put("WR", [P, 2 * RING * SLOT], "WR")
        WLO = put("WLO", [P, RING, SLOT], "WR", dt=F32R)
        WHI = put("WHI", [P, RING, SLOT], "WR", RING * SLOT, dt=F32R)
        QTR = put("QTR", [P, 11 * TP], "QTR")
        HNL = put("HNL", [P, KD, T], "QTR", dt=F32R)
        CKT = put("CKT", [P, NB, 256], "CKT")
        CV = put("CV", [P, NB, 2, P], "CV")
        VV = put("VV", [P, 5, 640], "VV")
        CO = put("CO", [P, CN], "CO")
        GB = put("GB", [P, 2, 2, HALF], "GB")
        NG = sb("NG", [P, 3, KD])
        QG = sb("QG", [P, 6, HD])
        B1 = sb("B1", [P, 2])
        W2 = sb("W2", [P, 2, HD])
        PW = sb("PW", [P, 2, HD])
        PSC = sb("PSC", [P, 2])
        RIP = sb("RIP", [P, 1])
        I8 = sb("I8", [64, 8], U32)
        IXC = sb("IXC", [P, 2, NB], U32)
        IXS = sb("IXS", [SEL7, 64], U32)
        PT8 = sb("PT8", [NB, NPG], I32)
        PT8F = sb("PT8F", [NB, NPG])
        PTI = sb("PTI", [NPG, NB], I32)
        PTF = sb("PTF", [NPG, NB])
        GT = sb("GT", [P, 5, 18])
        SM = sb("SM", [P, 600])
        QA = sb("QA", [P, NB, 24])
        QD = sb("QD", [P, 3, NB, 8])
        QN = sb("QN", [P, 11, NS])
        GW = sb("GW", [P, NB, 3, 24])
        OP = sb("OP", [P, NB, 2, 24])
        SA = sb("SA", [P, 4, 56])
        SDG = sb("SDG", [56, 57])
        PS = ctx.enter_context(nc.psum_tensor("PS", [P, 8, 512], F32))

        HNk = HN[:, :].rearrange("p (k t) -> p k t", k=KD)
        MIXT = HNk
        MIXH, MIXL = HNL, HNH
        PROJ = BIG[:, :].rearrange("p (t c) -> p t c", t=5)
        QT = QTR[:, :].rearrange("p (m t) -> p m t", m=11)
        RAW = WR[:, 0:RING * SLOT].rearrange("p (s n) -> p s n", s=RING)
        HNF = QTR[:, 0:KD * T].rearrange("p (k t) -> p k t", k=KD)
        HIDF = BIG[:, BCH * T:2 * BCH * T].rearrange("p (n t) -> p n t", n=BCH)

        def const(name):
            at, rows, n = CL[name]
            return CO[0:rows, at:at + n]

        ident, ones = const("ident"), const("ones")
        eps = const("eps")
        RB = GB[:, 0, :, :]
        SQ, SQA = GB[:, 0, :, :], GB[:, 1, :, :]

        ld = {n: sem("ld_" + n) for n in ("const", "cw1", "small", "x", "page", "cw1b", "pieces")}
        d_ch = sem("dve_chain")
        g_rows = [sem("g_rows0"), sem("g_rows1")]
        ix_f, ix_mm, ix_ok = sem("ix_f"), sem("ix_mm"), sem("ix_ok")
        x_tr, x_ev = sem("x_tr"), sem("x_ev")
        t_done, ev_act, ev_dve = sem("t_done"), sem("ev_act"), sem("ev_dve")
        m_done, silu_done, w_done, w_copied = sem("m_done"), sem("silu_done"), sem("w_done"), sem("w_copied")
        ck_ss, ck_sq, ck_n, ck_t, ck_ev = sem("ck_ss"), sem("ck_sq"), sem("ck_n"), sem("ck_t"), sem("ck_ev")
        landed = [sem(f"ring{s}_landed") for s in range(RING)]
        w_hi, w_lo, w_used = sem("w_hi"), sem("w_lo"), sem("w_used")
        rs = [{n: sem(f"rms{r}_{n}") for n in ("sq", "sum", "root", "f", "hi", "lo")} for r in range(3)]
        ff = [{n: sem(f"ffn{f}_{n}") for n in ("silu", "free", "mul", "hi", "lo")} for f in range(2)]
        pj_mm, pj_ev = sem("pj_mm"), sem("pj_ev")
        hn_ss, hn_rt, qn, cp_act = sem("hn_ss"), sem("hn_rt"), sem("qn"), sem("cp_act")
        qt_mm, qt_act, qt_dve = sem("qt_mm"), sem("qt_act"), sem("qt_dve")
        st_cmp, st_out = sem("st_cmp"), sem("st_out")
        pc = {n: sem("pc_" + n) for n in ("tr", "ev", "mm", "silu", "w", "ss", "rt", "n", "t", "ev2")}
        po = {n: sem("po_" + n) for n in ("st", "stev", "dl", "mm", "ev")}
        pa = {n: sem("pa_" + n) for n in ("s", "sev", "nb", "exp", "p", "t", "tev", "pv", "oev",
                                          "cs", "cnb", "cexp", "cp")}
        sc = {n: sem("sc_" + n) for n in ("gx", "gm", "s", "mx", "mt", "dg", "bc", "sub", "exp", "sum", "den",
                                          "im", "imt", "pv", "br", "rows", "turn", "ix")}
        sa = {n: sem("sa_" + n) for n in ("pack", "kt", "ktev", "ks", "add", "mx", "mt", "dg", "bc", "sub", "exp", "sum", "pv",
                                          "rev", "ot", "out", "ex")}
        ld_kv = [[sem(f"ld_kv{u}_pair{g}") for g in range(4)] for u in range(3)]
        ld_wd = [sem("ld_wd0"), sem("ld_wd1")]
        wo_ev = sem("wo_ev")
        mx = {n: sem("mix_" + n) for n in ("hi", "lo")}
        y_tr, y_ev, y_out = sem("y_tr"), sem("y_ev"), sem("y_out")
        cpy = sem("state_copies")
        block = ctx.enter_context(nc.Block())

        XIN = BIG[:, 0:5 * D].rearrange("p (t n) -> p t n", t=5)
        PB = [t[:, 0:8192].rearrange("p (h n) -> p h n", h=2) for t in (WR, BIG)]
        YO = BIG[:, 0:5 * D].rearrange("p (t n) -> p t n", t=5)
        PTB = [BIG[:, 8192:12288].rearrange("p (h s n) -> p h s n", h=2, s=8),
               HN[:, 0:4096].rearrange("p (h s n) -> p h s n", h=2, s=8)]
        HIDC = BIG[:, 12288:12800].rearrange("p (u n) -> p u n", u=2)
        CW1 = QTR[:, 0:4096].rearrange("p (v c e) -> p v c e", v=2, c=16)
        SELP = QTR[0:NPG, 4096:4096 + 2 * P].rearrange("p (s m) -> p s m", s=2)
        CK = VV[:, :, :].rearrange("p a b -> p (a b)")[:, 0:2048]
        CKS = BIG[:, 0:2048]
        QP = VV[:, :, :].rearrange("p a b -> p (a b)")[:, 0:5 * 384].rearrange("p (t g h d) -> p t g h d", t=5, g=3, h=2)
        SQT = GB[:, :, :, :].rearrange("p a b c -> p (a b c)")
        CW1B = WR[:, 0:4096].rearrange("p (v c e) -> p v c e", v=2, c=16)
        PCS = HN[0:32, 0:4096]
        o = 8192
        UT = WR[:, o:o + 1056].rearrange("p (c t) -> p c t", c=2)
        UTS = WR[:, o + 1056:o + 1360].rearrange("p (c b t) -> p c b t", c=2, b=NB)
        PTC = WR[:, o + 1360:o + 2384].rearrange("p (v h s n) -> p v h s n", v=2, h=2, s=8)
        HIDP = WR[:, o + 2384:o + 2512].rearrange("p (q n) -> p q n", q=4)
        PST = WR[0:120, o + 2512:o + 2768]
        CKTP = WR[:, o + 2768:o + 2800]
        CVP = WR[0:31, o + 2800:o + 2928]
        CKP = WR[0:31, o + 2928:o + 3056]
        T1 = BIG[:, 6400:7456].rearrange("p (c t) -> p c t", c=2)
        T2 = BIG[:, 7456:8512].rearrange("p (c t) -> p c t", c=2)
        T1S = BIG[:, 8512:8816].rearrange("p (c b t) -> p c b t", c=2, b=NB)
        T2S = BIG[:, 8816:9120].rearrange("p (c b t) -> p c b t", c=2, b=NB)
        DL = BIG[:, 9120:10144].rearrange("p (c t) -> p c t", c=2)
        DLS = BIG[:, 10144:10208].rearrange("p (c b t) -> p c b t", c=2, b=NB)
        PHD = BIG[:, 10208:10240].rearrange("p (c t) -> p c t", c=2)
        CKPS = BIG[0:31, 10240:10368]
        SB = BIG[:, 0:4608].rearrange("p (u b n) -> p u b n", u=3, b=3)
        PTS = BIG[:, 4608:6144].rearrange("p (u n) -> p u n", u=3)
        SC = BIG[:, 6144:6336].rearrange("p (h n) -> p h n", h=6)
        SS = SM[:, 0:110].rearrange("p (t n) -> p t n", t=5)
        SSC = SM[:, 110:142]
        SSP = SM[0:31, 142:144]
        MX, DEN, WT, NBI = (SM[:, 144 + 9 * n:153 + 9 * n].rearrange("p (u n) -> p u n", u=3) for n in range(4))
        CMX, CDN, CWT = SM[:, 180:186], SM[:, 186:192], SM[:, 192:198]
        MX1 = SM[:, 198:201]

        def section_end(n):
            return -(-(SECTIONS[n][0] + SECTIONS[n][1] * HD) // CG)

        def tile_rows(tt):
            return P if tt < QT_TILES else NS

        def tok(tt):
            return slice(tt * P, tt * P + tile_rows(tt))

        units = []
        s_count = 0
        for i in range(QT_TILES):
            for hq in range(6):
                h, g = hq // 3, hq % 3
                br = [dict(q=g, k=k, h=h, j0=0, v=v * P + h * HD, off=None, diag="diag")
                      for v, k in enumerate((IT_SLC, IT_WIN))]
                units.append(dict(i=i, nsa=True, hq=hq, h=h, br=br, s0=s_count, new=hq == 0))
                s_count += 2
            for h in range(2):
                br = [dict(q=IT_QB + g, k=IT_KB + g, h=h, j0=max(0, i - 1) if g == 0 else 0,
                           v=256 + g * P + h * HD, off=("band_prev", "mod4_off", "mod16_off")[g],
                           diag=("diag", "mod4_diag", "mod16_diag")[g]) for g in range(3)]
                units.append(dict(i=i, nsa=False, h=h, br=br, s0=s_count, new=False))
                s_count += 3
        NU = len(units)

        SAR = put("SAR", [P, 33888], "BIG")
        KV = [WR[:, 0:8192], BIG[:, 0:8192], SAR[:, 24160:32352]]
        W0, W1 = BIG[:, 8192:11520], WR[:, 8192:11264]
        KWIN = [W0[:, 0:1024], W1[:, 0:1024]]
        KDL1 = [W0[:, 1024:2048], W1[:, 1024:2048]]
        KDL2 = [W0[:, 2048:3072], W1[:, 2048:3072]]
        KDL0 = [W0[:, 3072:3328], BIG[:, 11520:11776]]
        KTBS = [BIG[:, 11776:12288], BIG[:, 12288:12800]]
        VVf = VV[:, :, :].rearrange("p a b -> p (a b)")
        GBf = GB[:, :, :, :].rearrange("p a b c -> p (a b c)")
        SCO = VVf[:, 0:336]
        EXS = [VVf[:, 336:672], VVf[:, 672:1008]]
        ODR, OSR, OWR = VVf[0:8, 1008:1392], VVf[0:6, 1392:1904], VVf[0:24, 1904:2032]
        KPK = [GBf[0:SEL7, 512 * n:512 * (n + 1)].rearrange("p (j c) -> p j c", j=4) for n in range(2)]
        OA = SM[:, 204:396].rearrange("p (b r) -> p b r", b=NB)
        OD = SM[:, 396:588].rearrange("p (b g r) -> p b g r", b=NB, g=3)
        SMX, SSUM, SINV, SWG = (SA[:, n, :] for n in range(4))
        CS = WR[:, 4096:8192]
        SCM, ECM = (CS[:, 384 * n:384 * (n + 1)].rearrange("p (c n) -> p c n", c=2) for n in range(2))
        MXC, SUC, RCC = (CS[:, 768 + 192 * n:960 + 192 * n] for n in range(3))
        MXR = CS[0:96, 1344:1346]
        DGC = CS[0:96, 1346:1538].rearrange("p (n m) -> p n m", n=2)
        IMT = CS[:, 1538:1666].rearrange("p (c r) -> p c r", c=2)
        IM = CS[0:64, 1666:1922]
        SCR, M8 = CS[0:64, 1922:1986], CS[0:64, 1986:1994]
        GX = CS[0:NS, 1994:2570].rearrange("p (c n) -> p c n", c=3)
        BROW = CS[0:64, 2570:2634].rearrange("p (g c) -> p g c", c=2)
        SLOT7 = CS[0:64, 2634:2641]
        HOT = CS[0:64, 2641:3089].rearrange("p (s n) -> p s n", s=SLOTS)
        ROWS = CS[0:64, 3089:3201].rearrange("p (s r) -> p s r", s=SLOTS)

        newK = lambda item: QN[:, item, :]
        newV = lambda c: VV[0:NS, 4, c:c + P]
        SECT = ((0, 5, 24), (120, 5, 24), (240, 12, 8))
        NGR = 8

        def of_token(a, t):
            return a.rearrange("p (n t) -> p t n", t=TS)[:, t, :]

        def cached(b, x):
            w = b % 2
            ps = PS[:, 2 + w, :]
            if x < 4:
                return ([KPK[x % 2][:, j, :] for j in range(4)], SEL7, of_token(QA[:, b, :], x),
                        [of_token(ps[0:SEL7, 24 * j:24 * j + 24], x) for j in range(4)])
            n, kk, at = ((4, KWIN, 120), (1, KDL0, 240), (4, KDL1, 248), (4, KDL2, 280))[x - 4]
            q = QA[:, b, :] if x == 4 else QD[:, x - 5, b, :]
            R = 24 if x == 4 else 8
            return [kk[w][:, j * 256:j * 256 + P] for j in range(n)], P, q, [ps[:, at + R * j:at + R * (j + 1)]
                                                                            for j in range(n)]

        def value_tiles(b):
            w, kv, ex = b % 2, KV[b % 3], EXS[b % 2]
            for t in range(TS):
                for h in range(2):
                    cols = lambda j: (2 * t + h) * 1024 + j * 256 + P + h * HD
                    tiles = [(of_token(ex[0:SEL7, 24 * j:24 * j + 24], t), kv[0:SEL7, cols(j):cols(j) + HD])
                             for j in range(4)]
                    tiles.append((of_token(ex[0:NS, 96:120], t), VV[0:NS, 4, h * HD:(h + 1) * HD]))
                    yield PS[0:6, 6, t * P + h * HD:t * P + (h + 1) * HD], tiles
            at = lambda t, j: t[:, j * 256 + P:(j + 1) * 256]
            yield PS[0:24, 7, 0:P], [(ex[:, 120 + 24 * j:144 + 24 * j], at(KWIN[w], j)) for j in range(4)] \
                + [(ex[0:NS, 216:240], newV(P))]
            yield PS[0:8, 7, P:2 * P], [(ex[:, 240:248], at(KDL0[w], 0)), (ex[0:NS, 312:320], newV(256))]
            yield PS[0:8, 7, 2 * P:3 * P], [(ex[:, 248 + 8 * j:256 + 8 * j], at(KDL1[w], j)) for j in range(4)] \
                + [(ex[0:NS, 320:328], newV(256 + P))]
            yield PS[0:8, 7, 3 * P:4 * P], [(ex[:, 280 + 8 * j:288 + 8 * j], at(KDL2[w], j)) for j in range(4)] \
                + [(ex[0:NS, 328:336], newV(256 + 2 * P))]

        @block.sync
        def _(sp):
            sp.dma_start(PTI[:, :], I["page_table"].rearrange("b n -> n b")).then_inc(ld["page"], 16)
            sp.dma_start(SELP, I["selp"].rearrange("p (s m) -> p s m", s=2)).then_inc(ld["page"], 16)
            sp.dma_start(RIP[:, :], I["rip"]).then_inc(ld["page"], 16)
            sp.dma_start(XIN[:, 0:4, :], I["x_prompt"][0].rearrange("(t p) n -> p t n", p=P)).then_inc(ld["x"], 16)
            sp.dma_start(XIN[0:NS, 4, :], I["x_sample"].rearrange("b t n -> (b t) n")).then_inc(ld["x"], 16)
            sp.dma_start(CO[:, :], I["consts"]).then_inc(ld["const"], 16)
            sp.dma_start(CW1, I["cmp_w1"][0].rearrange("v (c p) e -> p v c e", p=P)).then_inc(ld["cw1"], 16)

            sp.wait_ge(t_done, 16 * (NB - 1))

            def chunk_loads(f, first, c, used):
                src = I["ffn_in"][0, f].rearrange("(k p) n -> p k n", p=P)
                for gs in range(2):
                    sl = (first + gs) % RING
                    if used is not None:
                        sp.wait_ge(w_used, used + gs)
                    dst = RAW[:, sl, 0:KD * P].rearrange("p (k n) -> p k n", k=KD)
                    sp.dma_start(dst, src[:, :, bass.ds(c * P + gs * FF, P)]).then_inc(landed[sl], 16)

            def ffn_loads(f):
                for blk in range(2):
                    L = L_FFN[f] + blk * L_BLOCK
                    c = blk * BCH
                    n = 0
                    if L == 0:
                        for n in range(2):
                            chunk_loads(f, L + 2 * n, c + n, None)
                        n = 2
                    else:
                        chunk_loads(f, L, c, L - RING + 1)
                        n = 1
                    pairs = (BCH - n) // 2
                    with sp.Fori(0, pairs) as it:
                        for u in range(2):
                            m = n + u
                            chunk_loads(f, L + 2 * m, it * 2 + (c + m), it * 4 + (L + 2 * m - RING + 1))
                    for m in range(n + 2 * pairs, BCH):
                        chunk_loads(f, L + 2 * m, c + m, L + 2 * m - RING + 1)
                    L += 2 * BCH
                    src = I["ffn_out"][0, f].rearrange("(k p) n -> p k n", p=P)[:, blk * BCH:(blk + 1) * BCH, :]
                    for oc in range(KD):
                        sl = (L + oc) % RING
                        sp.wait_ge(w_used, L + oc - RING + 1)
                        sp.dma_start(RAW[:, sl, :].rearrange("p (k n) -> p k n", k=BCH),
                                     src[:, :, oc * P:(oc + 1) * P]).then_inc(landed[sl], 16)

            ffn_loads(0)
            w_in = I["w_in"][0].rearrange("(k p) n -> p k n", p=P)
            for c in range(NCG):
                n = min(CG, COLS - c * CG)
                for x in range(2):
                    L = L_IN + 2 * c + x
                    sp.wait_ge(w_used, L - RING + 1)
                    sp.dma_start(RAW[:, L % RING, 0:KH * n].rearrange("p (k n) -> p k n", k=KH),
                                 w_in[:, x * KH:(x + 1) * KH, c * CG:c * CG + n]).then_inc(landed[L % RING], 16)
                if c == 4:
                    sp.wait_ge(pj_ev, 5 * -(-(C_CMP + 256) // CG))
                    cmp_p = O["cmp_p"].rearrange("a b t x h d -> (a b t) (x h d)")
                    sp.dma_start(cmp_p.rearrange("(t p) c -> p t c", p=P), PROJ[:, 0:4, C_CMP:C_CMP + 256])\
                        .then_inc(st_cmp, 16)
            sp.wait_ge(w_used, L_OUT)
            sp.wait_ge(st_cmp, 16)
            sp.dma_start(PST, I["state_pool"][0].rearrange("b t c -> (b t) c")).then_inc(ld["pieces"], 16)
            sp.dma_start(PCS, cmp_p.rearrange("(p s) c -> p (s c)", s=16)).then_inc(ld["pieces"], 16)
            sp.dma_start(CW1B, I["cmp_w1"][0].rearrange("v (c p) e -> p v c e", p=P)).then_inc(ld["cw1b"], 16)

            def states():
                def flat(name):
                    return O[name].rearrange("a b t x h d -> (a b) t (x h d)")

                u_p, u_s = O["pool_p"][0, 0], O["pool_s"][0]
                yield O["cmp_s"].rearrange("a b t x h d -> (a b t) (x h d)"), PROJ[0:NS, 4, C_CMP:C_CMP + 256]
                yield u_p, PROJ[P - 15:P, 3, C_U:C_U + 256]
                yield u_s[:, 11:15, :], PROJ[0:NS, 4, C_U:C_U + 256]
                for name, c in (("slc", C_SLCK), ("win", C_WINK)):
                    yield flat(name + "_p")[0].rearrange("(t p) c -> p t c", p=P), PROJ[:, 0:4, c:c + 256]
                yield O["slc_s"].rearrange("a b t x h d -> (a b t) (x h d)"), PROJ[0:NS, 4, C_SLCK:C_SLCK + 256]
                yield flat("win_s")[:, 508:512, :], PROJ[0:NS, 4, C_WINK:C_WINK + 256]
                for g, (w, _) in enumerate(WDIL):
                    n = min(w, TP) // P
                    for x, c in enumerate((C_KB + g * P, C_VB + g * P)):
                        yield (flat(f"dil{g}_p")[0].rearrange("(t p) c -> p t c", p=P)[:, :, x * P:(x + 1) * P],
                               PROJ[:, 4 - n:4, c:c + P])
                        yield flat(f"dil{g}_s")[:, w - TS:w, x * P:(x + 1) * P], PROJ[0:NS, 4, c:c + P]

            sp.wait_ge(qn, 5)
            sp.wait_ge(pj_ev, 5 * NCG)
            n_states = 0
            for dst, src in states():
                sp.dma_start(dst, src).then_inc(st_out, 16)
                n_states += 1
            assert n_states == N_STATES

            def load_wd(b):
                x = b % 2
                sp.dma_start(KWIN[x], I["cache_win_kv"][0, b].rearrange("(p j) x h d -> p (j x h d)", j=4))\
                    .then_inc(ld_wd[x], 16)
                sp.dma_start(KDL0[x], I["cache_dil0_kv"][0, b].rearrange("p x h d -> p (x h d)")).then_inc(ld_wd[x], 16)
                sp.dma_start(KDL1[x], I["cache_dil1_kv"][0, b].rearrange("(p j) x h d -> p (j x h d)", j=4))\
                    .then_inc(ld_wd[x], 16)
                sp.dma_start(KDL2[x], I["cache_dil2_kv"][0, b].rearrange("(p j) x h d -> p j (x h d)", j=16)[:, 0:4, :])\
                    .then_inc(ld_wd[x], 16)

            sp.wait_ge(po["ev"], 4)
            sp.wait_ge(pc["ev2"], 1)
            load_wd(0)
            sp.wait_ge(pa["pv"], 3 * NU)
            load_wd(1)
            for b in range(2, NB):
                sp.wait_ge(sa["pv"], b - 1)
                load_wd(b)
            sp.wait_ge(sa["pv"], NB - 1)
            w_out = I["w_out"][0].rearrange("(k p) n -> p k n", p=P)
            for c in range(KD):
                L = L_OUT + c
                if c >= RING:
                    sp.wait_ge(w_used, L - RING + 1)
                sp.dma_start(RAW[:, L % RING, 0:KD * P].rearrange("p (k n) -> p k n", k=KD),
                             w_out[:, :, c * P:(c + 1) * P]).then_inc(landed[L % RING], 16)
            ffn_loads(1)

            for tt in range(5):
                R = tile_rows(tt)
                sp.wait_ge(y_ev, 2 * (tt + 1))
                dst = O["y_p"][0, tt * P:(tt + 1) * P, :] if tt < 4 else O["y_s"].rearrange("b t n -> (b t) n")
                sp.dma_start(dst, YO[0:R, tt, :]).then_inc(y_out, 16)
            sp.wait_ge(y_out, 16 * 5)
            sp.wait_ge(st_out, 16 * n_states)
            sp.wait_ge(cpy, 16 * N_COPIES)

        @block.gpsimd
        def _(pool):
            cmp_rows = I["cache_cmp_kv"][0].rearrange("n (r s) x h d -> (n r) (s x h d)", s=16)
            slc_rows = I["cache_slc_kv"][0].rearrange("n (r s) x h d -> (n r) (s x h d)", s=4)
            pool.wait_ge(ix_ok, 1)
            for b in range(NB):
                if b == 1:
                    pool.wait_ge(x_ev, KD + 1)
                if b >= 2:
                    pool.wait_ge(t_done, 16 * (b - 1))
                for half in range(2):
                    pool.indirect_dma_start(PB[b % 2][:, half, :], None, cmp_rows,
                                            bass.IndirectOffsetOnAxis(ap=IXC[:, half, b:b + 1], axis=0))\
                        .then_inc(g_rows[b % 2], 16)
            pieces = []
            for name, src, w, n in (("win_s", "cache_win_kv", 512, 4), ("dil0_s", "cache_dil0_kv", 128, 8),
                                    ("dil1_s", "cache_dil1_kv", 512, 4), ("dil2_s", "cache_dil2_kv", 2048, 1)):
                for b in range(0, NB, n):
                    pieces.append((O[name][0, b:b + n].rearrange("b t x h d -> b t (x h d)")[:, 0:w - TS, :],
                                   I[src][0, b:b + n].rearrange("b t x h d -> b t (x h d)")[:, TS:w, :]))
            pieces.append((O["pool_s"][0][:, 0:15 - TS], I["state_pool"][0][:, TS:15]))
            assert len(pieces) == N_COPIES
            for n, (dst, src) in enumerate(pieces):
                pool.wait_ge(w_used, 3 * n + 4)
                pool.dma_start(dst, src).then_inc(cpy, 16)

            def load_slc(b):
                for t in range(TS):
                    for h in range(2):
                        u = (2 * t + h) * 1024
                        row = b * 8 + h * TS + t
                        pool.indirect_dma_start(KV[b % 3][0:SEL7, u:u + 1024], None, slc_rows,
                                                bass.IndirectOffsetOnAxis(ap=IXS[:, row:row + 1], axis=0))\
                            .then_inc(ld_kv[b % 3][t], 16)

            pool.wait_ge(sc["ix"], 1)
            pool.wait_ge(pc["mm"], 1)
            load_slc(0)
            pool.wait_ge(pa["pv"], 3 * NU)
            pool.wait_ge(pa["oev"], NU)
            load_slc(1)
            load_slc(2)
            for b in range(3, NB):
                pool.wait_ge(sa["pv"], b - 2)
                load_slc(b)

        @block.tensor
        def _(pe):
            pe.sem_inc(m_done, 4)
            pe.wait_ge(ld["page"], 48)
            pe.wait_ge(ix_f, 1)
            for s in range(2):
                mm = pe.matmul(PS[:, 7, s * NB:(s + 1) * NB], SELP[:, s, :], PTF[:, :], start=True, stop=True)
            mm.then_inc(ix_mm, 1)
            pe.wait_ge(ld["x"], 32)
            pe.wait_ge(ld["const"], 16)
            for k in range(KD):
                if k >= 6:
                    pe.wait_ge(x_ev, k - 5)
                for tt in range(4):
                    pe.transpose(PS[:, k % 6, tt * P:(tt + 1) * P], XIN[:, tt, k * P:(k + 1) * P], ident)
                pe.transpose(PS[:, 6, k * NS:(k + 1) * NS], XIN[0:NS, 4, k * P:(k + 1) * P], ident[0:NS, 0:NS])\
                    .then_inc(x_tr, 1)

            def rms(r):
                pe.wait_ge(rs[r]["sq"], 1)
                for hf in range(2):
                    mm = pe.matmul(PS[:, hf, 0:HALF], ones, SQA[:, hf, :], start=True, stop=True)
                mm.then_inc(rs[r]["sum"], 1)

            pe.wait_ge(x_ev, KD + 1)
            rms(0)
            pe.wait_ge(rs[0]["root"], 1)
            pe.wait_ge(ix_ok, 1)
            pe.wait_ge(ld["cw1"], 16)
            pe.wait_ge(ld["small"], SMALL)

            def tr_unit(b, par, kv, j, rows_ready):
                if rows_ready is not None:
                    pe.wait_ge(g_rows[par], rows_ready)
                n = b * 16 + (8 * kv + j + 1)
                pe.wait_ge(ev_act, n)
                pe.wait_ge(ev_dve, n)
                for s in range(2):
                    for half in range(2):
                        c = (2 * j + s) * 256 + kv * P
                        mm = pe.transpose(PS[:, j % 4, s * 256 + half * P:s * 256 + (half + 1) * P],
                                          PB[par][:, half, c:c + P], ident)
                mm.then_inc(t_done, 1)

            def hidden(b, kv, h, spread):
                m = 2 * kv + h
                pe.wait_ge(ev_act, b * 16 + (4 + 8 * kv + 8))
                pe.wait_ge(ev_dve, b * 16 + (4 + 8 * kv + 8))
                pe.wait_ge(silu_done, b * 4 + (m + 1))
                for c in range(2):
                    for s in range(8):
                        mm = pe.matmul(PS[:, 4 + m % 2, 0:255], CW1[:, kv, 8 * c + s, :], PTB[kv][:, h, s, c:c + 255],
                                       start=(c == 0 and s == 0), stop=(c == 1 and s == 7))
                        if (c, s) in spread:
                            spread[(c, s)]()
                mm.then_inc(m_done, 1)

            def second(b, m):
                pe.wait_ge(silu_done, b * 4 + (2 + m + 1))
                pe.wait_ge(w_copied, b * 4 + (m + 3))
                for ct in range(2):
                    c = (ct * 4 + m) * HD
                    mm = pe.matmul(PS[:, 6 + m % 2, c:c + HD], HIDC[:, m % 2, ct * P:(ct + 1) * P], W2[:, m // 2, :],
                                   start=True, stop=True)
                mm.then_inc(w_done, 1)

            def compress(b, par, count, last):
                T1u = lambda j: (lambda: tr_unit(b, par, 1, j, None))
                at = [(0, 1), (0, 4), (0, 7), (1, 2)]
                hidden(b, 0, 0, {at[n]: T1u(n) for n in range(4)})
                hidden(b, 0, 1, {**{at[n]: T1u(4 + n) for n in range(4)}, (1, 5): lambda: second(b, 0)})
                nxt = {} if last else {at[n]: (lambda n=n: tr_unit(b + 1, 1 - par, 0, n, count if n == 0 else None))
                                       for n in range(4)}
                hidden(b, 1, 0, {**nxt, (1, 5): lambda: second(b, 1)})
                nxt = {} if last else {at[n]: (lambda n=n: tr_unit(b + 1, 1 - par, 0, 4 + n, None)) for n in range(3)}
                hidden(b, 1, 1, {**nxt, (1, 5): lambda: second(b, 2)})
                if not last:
                    tr_unit(b + 1, 1 - par, 0, 7, None)
                second(b, 3)

            for j in range(8):
                tr_unit(0, 0, 0, j, 32 if j == 0 else None)
            with pe.Fori(0, NB // 2 - 1) as it:
                compress(it * 2, 0, it * 32 + 32, False)
                compress(it * 2 + 1, 1, it * 32 + 64, False)
            compress(NB - 2, 0, 32 * (NB // 2), False)
            compress(NB - 1, 1, 0, True)
            pe.wait_ge(ev_act, 4 + 16 * NB)
            pe.wait_ge(ev_dve, 4 + 16 * NB)
            pe.wait_ge(w_copied, 4 + 4 * NB)

            def three(out, a, b, first, last):
                pe.matmul(out, a[0], b[0], start=first, stop=False)
                pe.matmul(out, a[0], b[1], start=False, stop=False)
                return pe.matmul(out, a[1], b[0], start=False, stop=last)

            def weights(sl, k, n, w):
                return tuple(t[:, sl, k * w + n[0]:k * w + n[1]] for t in (WHI, WLO))

            def halves(hf):
                return slice(hf * HALF, (hf + 1) * HALF)

            def ffn(f):
                pe.sem_inc(ff[f]["free"], 2)
                r = rs[2 * f]
                for blk in range(2):
                    L0 = L_FFN[f] + blk * L_BLOCK
                    e0 = blk * (BCH + KD)

                    def chunk(m, it, step):
                        L, e = L0 + 2 * m, e0 + m
                        pe.wait_ge(ff[f]["free"], it * step + (e + 1))
                        for gs in range(2):
                            pe.wait_ge(w_hi, it * (2 * step) + (L + gs + 1))
                            pe.wait_ge(w_lo, it * (2 * step) + (L + gs + 1))
                            sl = (L0 + 2 * m + gs) % RING
                            for hf in range(2):
                                for k in range(KD):
                                    if m == 0 and gs == 0 and hf == 0 and blk == 0:
                                        pe.wait_ge(r["hi"], k + 1)
                                        pe.wait_ge(r["lo"], k + 1)
                                    mm = three(PS[:, 4 * (e % 2) + 2 * gs + hf, 0:HALF], weights(sl, k, (0, P), P),
                                               (HNH[:, k, halves(hf)], HNL[:, k, halves(hf)]), k == 0, k == KD - 1)
                            mm.then_inc(w_used, 1)

                    with pe.Fori(0, BCH // 2) as it:
                        for u in range(2):
                            chunk(u, it, 2)
                    chunk(BCH - 1, 0, 0)
                    LO, eo = L0 + 2 * BCH, e0 + BCH

                    def out_chunk(oc, it, step, wait_last):
                        L, e = LO + oc, eo + oc
                        pe.wait_ge(ff[f]["free"], it * step + (e + 1))
                        pe.wait_ge(w_hi, it * step + (L + 1))
                        pe.wait_ge(w_lo, it * step + (L + 1))
                        sl = (LO + oc) % RING
                        for hf in range(2):
                            for n in range(BCH):
                                if wait_last and hf == 0 and n >= BCH - 2:
                                    pe.wait_ge(ff[f]["hi"], blk * BCH + n + 1)
                                    pe.wait_ge(ff[f]["lo"], blk * BCH + n + 1)
                                mm = three(PS[:, 4 * (e % 2) + hf, 0:HALF], weights(sl, n, (0, P), P),
                                           (HIDH[:, n, halves(hf)], HIDL[:, n, halves(hf)]), n == 0, n == BCH - 1)
                        mm.then_inc(w_used, 1)

                    pe.wait_ge(ff[f]["hi"], blk * BCH + BCH - 2)
                    pe.wait_ge(ff[f]["lo"], blk * BCH + BCH - 2)
                    with pe.Fori(0, KD // 4) as it:
                        for oc in range(4):
                            out_chunk(oc, it, 4, oc == 0)
                pe.wait_ge(ff[f]["free"], 2 + 2 * (BCH + KD))

            ffn(0)
            pe.wait_ge(ck_n, 1)
            for b in range(NB):
                for ct in range(2):
                    n = 2 * b + ct
                    mm = pe.transpose(PS[:, 4 + n // 4, (n % 4) * P:(n % 4 + 1) * P], CK[:, n * P:(n + 1) * P], ident)
            mm.then_inc(ck_t, 1)
            rms(1)
            pe.wait_ge(rs[1]["root"], 1)
            pe.wait_ge(ck_ev, 1)
            for c in range(NCG):
                L = L_IN + 2 * c
                pe.wait_ge(w_hi, L + 2)
                pe.wait_ge(w_lo, L + 2)
                n = min(CG, COLS - c * CG)
                for tt in range(5):
                    x = c * 5 + tt
                    ts = tok(tt) if tt < 4 else slice(T - P, T)
                    if x >= 8:
                        pe.wait_ge(pj_ev, x - 7)
                    for k in range(KD):
                        if x == 0:
                            pe.wait_ge(rs[1]["hi"], k + 1)
                            pe.wait_ge(rs[1]["lo"], k + 1)
                        mm = three(PS[:, x % 8, 0:n], (HNH[:, k, ts], HNL[:, k, ts]),
                                   weights((L + k // KH) % RING, k % KH, (0, n), n), k == 0, k == KD - 1)
                    mm.then_inc(pj_mm, 1)
                    if tt == 4:
                        pe.wait_ge(pj_mm, x + 1)
                        pe.sem_inc(w_used, 2)
            pe.wait_ge(pj_ev, 5 * NCG)
            pe.wait_ge(qn, 5)
            pcol = {IT_SLC: C_SLCK, IT_WIN: C_WINK}
            pcol.update({IT_QB + g: C_QB + g * P for g in range(3)})
            pcol.update({IT_KB + g: C_KB + g * P for g in range(3)})
            pcol.update({IT_U + c: C_U + c * P for c in range(2)})
            for m in range(ITEMS):
                if m >= 4:
                    pe.wait_ge(qt_act, m - 3)
                    pe.wait_ge(qt_dve, m - 3)
                for tt in range(5):
                    R = tile_rows(tt)
                    src = QP[0:R, tt, m, :, :].rearrange("p h d -> p (h d)") if m < 3 else \
                        PROJ[0:R, tt, pcol[m]:pcol[m] + P]
                    dst = PS[:, 2 * (m % 4), tt * P:(tt + 1) * P] if tt < 4 else PS[:, 2 * (m % 4) + 1, 0:NS]
                    mm = pe.transpose(dst, src, ident[0:R, 0:R])
                mm.then_inc(qt_mm, 1)
            pe.wait_ge(qt_act, ITEMS)
            pe.wait_ge(qt_dve, ITEMS)
            pe.wait_ge(ld["pieces"], 32)
            for c in range(2):
                mm = pe.transpose(PS[:, 4, c * P:c * P + 120], PST[:, c * P:(c + 1) * P], ident[0:120, 0:120])
            mm.then_inc(po["st"], 1)
            for kv in range(2):
                for s in range(16):
                    c = s * 256 + kv * P
                    mm = pe.transpose(PS[:, kv, s * 32:(s + 1) * 32], PCS[:, c:c + P], ident[0:32, 0:32])
                mm.then_inc(pc["tr"], 1)
            pe.wait_ge(sc["gx"], 1)
            for c in range(3):
                mm = pe.matmul(PS[:, 6 + c // 2, c % 2 * 192:(c % 2 + 1) * 192], ones[0:NS, :], GX[:, c, :],
                               start=True, stop=True)
            mm = pe.matmul(PS[0:64, 7, 192:192 + NPG], const("seq_of"), PT8F[:, :], start=True, stop=True)
            mm.then_inc(sc["gm"], 1)
            for ct in range(2):
                for b in range(NB):
                    c = ct * 192 + b * 24
                    mm = pe.matmul(PS[:, 5, c:c + 24], CKT[:, b, ct * P:(ct + 1) * P], QA[:, b, :], start=True, stop=True)
            mm.then_inc(sc["s"], 1)

            def rows_max():
                pe.wait_ge(sc["mx"], 1)
                for n in range(2):
                    mm = pe.transpose(PS[0:96, 5, n * P:(n + 1) * P], MXC[:, n * 96:(n + 1) * 96], ident)
                mm.then_inc(sc["mt"], 1)

            def spread_max():
                pe.wait_ge(sc["dg"], 1)
                for n in range(2):
                    mm = pe.matmul(PS[:, 6, n * 96:(n + 1) * 96], ones[0:96, :], DGC[:, n, :], start=True, stop=True)
                mm.then_inc(sc["bc"], 1)

            def spread_sum():
                pe.wait_ge(sc["sum"], 1)
                pe.matmul(PS[:, 7, 0:192], ones, SUC, start=True, stop=True).then_inc(sc["den"], 1)

            def importance():
                pe.wait_ge(sc["im"], 1)
                for ct in range(2):
                    mm = pe.transpose(PS[0:64, 5, ct * P:(ct + 1) * P], IMT[:, ct, :], ident)
                mm.then_inc(sc["imt"], 1)
                for b in range(NB):
                    for ct in range(2):
                        mm = pe.matmul(PS[:, 6, b * 24:(b + 1) * 24], CV[:, b, ct, :], ECM[:, ct, b * 24:(b + 1) * 24],
                                       start=(ct == 0), stop=(ct == 1))
                mm.then_inc(sc["pv"], 1)

            rows_max()
            pe.wait_ge(ld["cw1b"], 16)
            pe.wait_ge(pc["ev"], 2)
            for m in range(4):
                for c in range(2):
                    for s in range(8):
                        mm = pe.matmul(PS[:, 2, m * 32:m * 32 + 31], CW1B[:, m // 2, 8 * c + s, :],
                                       PTC[:, m // 2, m % 2, s, c:c + 31], start=(c == 0 and s == 0),
                                       stop=(c == 1 and s == 7))
                if m < 3:
                    (spread_max, spread_sum, importance)[m]()
            mm.then_inc(pc["mm"], 1)
            pe.wait_ge(pc["silu"], 2)
            for m in range(4):
                mm = pe.matmul(PS[0:31, 3, m * HD:(m + 1) * HD], HIDP[:, m, 0:31], W2[:, m // 2, :],
                               start=True, stop=True)
            mm.then_inc(pc["w"], 1)
            pe.wait_ge(po["dl"], 1)
            pe.wait_ge(po["stev"], 1)
            for c in range(2):
                for q in range(2):
                    r = slice(q * HD, (q + 1) * HD)
                    pe.matmul(PS[r, c, 0:TP], PW[r, c, :], DL[r, c, :], start=True, stop=True)
                    mm = pe.matmul(PS[r, 4, c * NS:(c + 1) * NS], PW[r, c, :],
                                   DLS[r, c, :, :].rearrange("p b t -> p (b t)"), start=True, stop=True)
            mm.then_inc(po["mm"], 1)
            pe.wait_ge(sc["rows"], 1)
            pe.transpose(PS[0:SEL7, 7, 0:64], ROWS.rearrange("p s r -> p (s r)"), ident[0:64, 0:64]).then_inc(sc["turn"], 1)
            pe.wait_ge(pc["n"], 1)
            pe.transpose(PS[:, 2, 0:31], CKP, ident[0:31, 0:31]).then_inc(pc["t"], 1)
            pe.wait_ge(sc["ix"], 1)
            pe.wait_ge(pc["ev2"], 1)
            pe.wait_ge(po["ev"], 4)
            pe.wait_ge(po["stev"], 1)

            def scores(u):
                U = units[u]
                i = U["i"]
                if U["new"]:
                    if i:
                        pe.wait_ge(pa["cp"], i)
                    for hq in range(6):
                        r = slice(hq // 3 * HD, hq // 3 * HD + HD)
                        mm = pe.matmul(PS[:, 7, hq * 32:hq * 32 + 31], QT[r, hq % 3, i * P:(i + 1) * P],
                                       CKTP[r, 0:31], start=True, stop=True)
                        if hq % 3 == 2:
                            mm.then_inc(pa["cs"], 1)
                            pe.wait_ge(pa["cs"], 2 * i + hq // 3 + 1)
                for x, b in enumerate(U["br"]):
                    B = U["s0"] + x
                    if B >= 3:
                        pe.wait_ge(pa["sev"], B - 2)
                    r = slice(b["h"] * HD, b["h"] * HD + HD)
                    n = (i + 1 - b["j0"]) * P
                    pe.matmul(PS[:, B % 3, 0:n], QT[r, b["q"], i * P:(i + 1) * P],
                              QT[r, b["k"], b["j0"] * P:(i + 1) * P], start=True, stop=True).then_inc(pa["s"], 1)

            def turn(u, x):
                U = units[u]
                B = 3 * u + x
                if B >= 2:
                    pe.wait_ge(pa["tev"], B - 1)
                if U["nsa"] and x == 2:
                    pe.wait_ge(pa["cp"], U["i"] + 1)
                    pe.transpose(PS[0:31, 3 + B % 2, 0:P], SC[:, U["hq"], 0:31], ident).then_inc(pa["t"], 1)
                    return
                pe.wait_ge(pa["p"], u + 1)
                for y in range(U["i"] + 1 - U["br"][x]["j0"]):
                    mm = pe.transpose(PS[:, 3 + B % 2, y * P:(y + 1) * P], SB[:, u % 3, x, y * P:(y + 1) * P], ident)
                mm.then_inc(pa["t"], 1)

            def values(u, x):
                U = units[u]
                B = 3 * u + x
                if x == 0 and u >= 2:
                    pe.wait_ge(pa["oev"], u - 1)
                pe.wait_ge(pa["tev"], B + 1)
                if U["nsa"]:
                    e = U["hq"] % 2
                    out = PS[e * HD:(e + 1) * HD, 5 + u % 2, 0:P]
                else:
                    out = PS[U["h"] * HD:(U["h"] + 1) * HD, 5 + u % 2, x * P:(x + 1) * P]
                if U["nsa"] and x == 2:
                    pe.matmul(out, CVP[:, U["h"] * HD:(U["h"] + 1) * HD], PTS[0:31, B % 3, 0:P],
                              start=False, stop=True).then_inc(pa["pv"], 1)
                    return
                b = U["br"][x]
                n = U["i"] + 1 - b["j0"]
                for y in range(n):
                    mm = pe.matmul(out, VV[:, b["j0"] + y, b["v"]:b["v"] + HD], PTS[:, B % 3, y * P:(y + 1) * P],
                                   start=(y == 0 and (x == 0 or not U["nsa"])),
                                   stop=(y == n - 1 and not U["nsa"]))
                mm.then_inc(pa["pv"], 1)

            scores(0)
            scores(1)
            for u in range(NU):
                if u + 2 < NU:
                    scores(u + 2)
                turn(u, 0)
                turn(u, 1)
                values(u, 0)
                turn(u, 2)
                values(u, 1)
                values(u, 2)

            def keys(b, x):
                n = NGR * b + x
                if x < NGR:
                    tiles, rows, _, _ = cached(b, x)
                    if x < 4:
                        pe.wait_ge(sa["pack"], 8 * b + 2 * (x + 1))
                    if x == 4:
                        pe.wait_ge(ld_wd[b % 2], 64 * (b // 2 + 1))
                    if n >= 2:
                        pe.wait_ge(sa["ktev"], n - 1)
                    for y, kt in enumerate(tiles):
                        mm = pe.transpose(PS[:, n % 2, y * P:y * P + rows], kt, ident[0:rows, 0:rows])
                    mm.then_inc(sa["kt"], 1)
                if x:
                    tiles, rows, q, dst = cached(b, x - 1)
                    pe.wait_ge(sa["ktev"], n)
                    if b >= 2 and x == 1:
                        pe.wait_ge(sa["add"], b - 1)
                    if x == NGR:
                        ps = PS[0:NS, 2 + b % 2, :]
                        pe.matmul(ps[:, 96:120], newK(IT_SLC), QA[:, b, :], start=True, stop=True)
                        pe.matmul(ps[:, 216:240], newK(IT_WIN), QA[:, b, :], start=True, stop=True)
                        for g in range(3):
                            pe.matmul(ps[:, 312 + 8 * g:320 + 8 * g], newK(IT_KB + g), QD[:, g, b, :],
                                      start=True, stop=True)
                    for y in range(len(tiles)):
                        mm = pe.matmul(dst[y], KTBS[(n - 1) % 2][:, y * P:y * P + rows], q, start=True, stop=True)
                    mm.then_inc(sa["ks"], 1)

            pe.wait_ge(pa["oev"], NU)
            for x in range(NGR + 1):
                keys(0, x)

            def top(b):
                pe.wait_ge(sa["mx"], b + 1)
                if b:
                    pe.wait_ge(sa["out"], b)
                pe.transpose(PS[0:56, 5, 0:P], SMX, ident).then_inc(sa["mt"], 1)

            def spread(b):
                pe.wait_ge(sa["dg"], b + 1)
                pe.matmul(PS[:, 5, P:P + 56], ones[0:56, :], SDG[:, 1:57], start=True, stop=True).then_inc(sa["bc"], 1)

            def values(b):
                pe.wait_ge(sa["exp"], b + 1)
                if b:
                    pe.wait_ge(sa["rev"], 3 * b)
                for dst, tiles in value_tiles(b):
                    for y, (ex, v) in enumerate(tiles):
                        mm = pe.matmul(dst, ex, v, start=(y == 0), stop=(y == len(tiles) - 1))
                mm.then_inc(sa["pv"], 1)

            def turned(b):
                pe.wait_ge(sa["rev"], 3 * b + 3)
                for t in range(TS):
                    pe.transpose(of_token(PS[:, 5, 192:216], t), OSR[:, t * P:(t + 1) * P], ident[0:6, 0:6])
                pe.transpose(PS[:, 5, 216:240], OWR, ident[0:24, 0:24])
                for g in range(3):
                    pe.transpose(PS[:, 5, 240 + 8 * g:248 + 8 * g], ODR[:, g * P:(g + 1) * P], ident[0:8, 0:8])
                pe.wait_ge(sa["sum"], b + 1)
                pe.matmul(PS[:, 5, 264:320], ones, SSUM, start=True, stop=True).then_inc(sa["ot"], 1)

            for b in range(NB):
                for x in range(NGR + 1):
                    if b + 1 < NB:
                        keys(b + 1, x)
                    if x == 1 and b:
                        turned(b - 1)
                    if x == 2:
                        top(b)
                    if x == 5:
                        spread(b)
                values(b)
            turned(NB - 1)

            pe.wait_ge(sa["ex"], 1)
            for oc in range(KD):
                L = L_OUT + oc
                pe.wait_ge(w_hi, L + 1)
                pe.wait_ge(w_lo, L + 1)
                if oc >= 2:
                    pe.wait_ge(wo_ev, oc - 1)
                for hf in range(2):
                    for k in range(KD):
                        if oc == 0 and hf == 0:
                            pe.wait_ge(mx["hi"], k + 1)
                            pe.wait_ge(mx["lo"], k + 1)
                        mm = three(PS[:, 4 * (oc % 2) + hf, 0:HALF], weights(L % RING, k, (0, P), P),
                                   (MIXH[:, k, halves(hf)], MIXL[:, k, halves(hf)]), k == 0, k == KD - 1)
                mm.then_inc(w_used, 1)
            pe.wait_ge(wo_ev, KD)
            rms(2)
            pe.wait_ge(rs[2]["root"], 1)
            ffn(1)
            for tt in range(5):
                R = tile_rows(tt)
                for hf in range(2):
                    x = 2 * tt + hf
                    if x >= 4:
                        pe.wait_ge(y_ev, x - 3)
                    for k in range(4):
                        mm = pe.transpose(PS[0:R, x % 4, k * P:(k + 1) * P], XT[:, 4 * hf + k, tok(tt)], ident)
                    mm.then_inc(y_tr, 1)

        @block.scalar
        def _(act):
            act.sem_inc(ev_act, 4)
            act.sem_inc(silu_done, 2)
            act.dma_start(NG[:, :, :], I["norm_gain"][0].rearrange("r (k p) -> p r k", p=P)).then_inc(ld["small"], 16)
            act.dma_start(QG[:, :, :].rearrange("p a d -> p (a d)"),
                          I["qk_gain"].rearrange("l a d -> l (a d)").to_broadcast([P, 6 * HD])).then_inc(ld["small"], 16)
            act.dma_start(PT8[:, :], I["page_table"]).then_inc(ld["small"], 16)
            act.dma_start(B1[:, :], I["cmp_b1"][0].rearrange("v e -> e v")).then_inc(ld["small"], 16)
            act.dma_start(W2[:, :, :], I["cmp_w2"][0].rearrange("v e d -> e v d")).then_inc(ld["small"], 16)
            for q in range(2):
                act.dma_start(PW[q * HD:(q + 1) * HD, :, :],
                              I["pool_w"][0].rearrange("(c q) i e -> q i c e", q=2)[q]).then_inc(ld["small"], 16)
            act.dma_start(PSC[:, :], I["pool_scale"][0].rearrange("(c p) -> p c", p=P)).then_inc(ld["small"], 16)
            act.wait_ge(ld["small"], SMALL)
            act.wait_ge(ld["const"], 16)

            def lead(L, n, it=0, step=0, shift=0):
                sl = L % RING
                act.wait_ge(landed[sl], it * (4 * step) + 16 * (L // RING + 1))
                act.activation(WHI[:, sl, 0:n], RAW[:, sl, 0:n], ACT.Copy).then_inc(w_hi, 1)

            def evac(b, kv, j):
                n = 8 * kv + j
                act.wait_ge(t_done, b * 16 + (n + 1))
                act.wait_ge(m_done, b * 4 + (2 * kv + 2))
                for s in range(2):
                    last = act.activation(PTB[kv][s * HD:(s + 1) * HD, 0, j, :], PS[0:HD, j % 4, s * 256:(s + 1) * 256],
                                          ACT.Copy)
                last.then_inc(ev_act, 1)

            def silu(b, m):
                act.wait_ge(m_done, b * 4 + (4 + m + 1))
                act.wait_ge(w_done, b * 4 + (m + 1))
                act.activation(HIDC[:, m % 2, 0:255], PS[:, 4 + m % 2, 0:255], ACT.Silu, bias=B1[:, m // 2:m // 2 + 1])\
                    .then_inc(silu_done, 1)

            def compress(b, last):
                for j in range(4):
                    evac(b, 1, j)
                silu(b, 0)
                for j in range(4, 8):
                    evac(b, 1, j)
                if last:
                    lead(0, KD * P)
                    lead(1, KD * P)
                silu(b, 1)
                if not last:
                    for j in range(4):
                        evac(b + 1, 0, j)
                silu(b, 2)
                if not last:
                    for j in range(4, 7):
                        evac(b + 1, 0, j)
                silu(b, 3)
                if not last:
                    evac(b + 1, 0, 7)

            def rms(r):
                act.wait_ge(rs[r]["sum"], 1)
                act.activation(RB, PS[:, 0:2, 0:HALF], ACT.Sqrt, bias=eps, scale=1.0 / D).then_inc(rs[r]["root"], 1)

            rms(0)
            act.sem_inc(w_done, 2)
            for j in range(8):
                evac(0, 0, j)
            with act.Fori(0, NB - 1) as it:
                compress(it, False)
            compress(NB - 1, True)
            def parts(r):
                for k in range(KD):
                    act.wait_ge(rs[r]["f"], k + 1)
                    act.activation(HNH[:, k, :], HNF[:, k, :], ACT.Copy).then_inc(rs[r]["hi"], 1)

            def ffn(f, after):
                for blk in range(2):
                    L0 = L_FFN[f] + blk * L_BLOCK
                    e0 = blk * (BCH + KD)

                    def chunk(m, it, step, nxt):
                        e = e0 + m
                        lead(L0 + 2 * m + 2, nxt, it, 2 * step)
                        lead(L0 + 2 * m + 3, nxt, it, 2 * step)
                        act.wait_ge(w_used, it * (2 * step) + (L0 + 2 * m + 1))
                        act.wait_ge(ff[f]["free"], it * step + (e + 1))
                        act.activation(GB[:, e % 2, :, :], PS[:, 4 * (e % 2):4 * (e % 2) + 2, 0:HALF], ACT.Silu)\
                            .then_inc(ff[f]["silu"], 1)
                        act.wait_ge(ff[f]["mul"], it * step + (blk * BCH + m + 1))
                        row = bass.ds(it * step + m, 1) if step else slice(m, m + 1)
                        act.activation(HIDH[:, row, :], HIDF[:, row, :], ACT.Copy).then_inc(ff[f]["hi"], 1)

                    with act.Fori(0, BCH // 2) as it:
                        for u in range(2):
                            chunk(u, it, 2, KD * P)
                    chunk(BCH - 1, 0, 0, SLOT)
                    LO = L0 + 2 * BCH
                    for oc in range(KD):
                        if oc + 2 < KD:
                            lead(LO + oc + 2, SLOT)
                        elif blk == 0:
                            lead(LO + oc + 2, KD * P)
                        elif after:
                            lead(LO + oc + 2, after)

            parts(0)
            act.wait_ge(ck_ss, 1)
            act.activation(SSC, SSC, ACT.Sqrt, bias=eps, scale=1.0 / HD).then_inc(ck_sq, 1)
            ffn(0, KH * CG)
            rms(1)
            parts(1)
            due = {}
            for n, (_, nh, _, off) in enumerate(SECTIONS):
                due.setdefault(5 * section_end(n) + 4, []).append((n, nh, off))
            for x in range(5 * NCG):
                c, tt = x // 5, x % 5
                R, n = tile_rows(tt), min(CG, COLS - c * CG)
                if tt == 0 and c + 1 < NCG:
                    m = min(CG, COLS - (c + 1) * CG)
                    lead(L_IN + 2 * c + 2, KH * m)
                    lead(L_IN + 2 * c + 3, KH * m)
                act.wait_ge(pj_mm, x + 1)
                src = PS[0:P, x % 8, 0:n] if tt < 4 else PS[P - NS:P, x % 8, 0:n]
                act.activation(PROJ[0:R, tt, c * CG:c * CG + n], src, ACT.Copy).then_inc(pj_ev, 1)
                for m, nh, off in due.get(x, []):
                    act.wait_ge(hn_ss, m + 1)
                    ss = slice(off, off + nh)
                    act.activation(SS[:, 0:4, ss], SS[:, 0:4, ss], ACT.Sqrt, bias=eps, scale=1.0 / HD)
                    act.activation(SS[0:NS, 4, ss], SS[0:NS, 4, ss], ACT.Sqrt, bias=eps[0:NS, :], scale=1.0 / HD)\
                        .then_inc(hn_rt, 1)
            act.wait_ge(pj_ev, 5 * NCG)
            for m in range(ITEMS):
                act.wait_ge(qt_mm, m + 1)
                dst = QT[:, m, :] if m < IT_U else UT[:, m - IT_U, 16:528]
                act.activation(dst, PS[:, 2 * (m % 4), :], ACT.Copy).then_inc(qt_act, 1)
            for rr, ts in ((P, slice(0, 4)), (NS, slice(4, 5))):
                act.activation(GT[0:rr, ts, :], PROJ[0:rr, ts, C_G:C_G + 18], ACT.Sigmoid).then_inc(cp_act, 1)
                for at, c, n in ((0, C_SLCV, P), (P, C_WINV, P), (256, C_VB, 384)):
                    act.activation(VV[0:rr, ts, at:at + n], PROJ[0:rr, ts, c:c + n], ACT.Copy).then_inc(cp_act, 1)
            for kv in range(2):
                act.wait_ge(pc["tr"], kv + 1)
                for h in range(2):
                    for s in range(2):
                        src = PS[h * HD:(h + 1) * HD, kv, :].rearrange("p (s u n) -> p s u n", s=8, u=2)[:, :, s, :]
                        last = act.activation(PTC[s * HD:(s + 1) * HD, kv, h, :, :], src, ACT.Copy)
                last.then_inc(pc["ev"], 1)
            act.wait_ge(sc["sub"], 1)
            act.activation(ECM, ECM, ACT.Exp, scale=SCALE).then_inc(sc["exp"], 1)
            act.wait_ge(pc["mm"], 1)
            for kv in range(2):
                act.activation(HIDP[:, 2 * kv:2 * kv + 2, 0:31],
                               PS[:, 2, 64 * kv:64 * kv + 64].rearrange("p (q n) -> p q n", q=2)[:, :, 0:31],
                               ACT.Silu, bias=B1[:, kv:kv + 1]).then_inc(pc["silu"], 1)
            act.wait_ge(pc["ss"], 1)
            act.activation(SSP, SSP, ACT.Sqrt, bias=eps[0:31, :], scale=1.0 / HD).then_inc(pc["rt"], 1)
            act.wait_ge(po["mm"], 1)
            for c in range(2):
                act.activation(MIXT[:, 6 + c, 0:TP], PS[:, c, :], ACT.Copy, scale=PSC[:, c:c + 1]).then_inc(po["ev"], 1)
                act.activation(MIXT[:, 6 + c, TP:T], PS[:, 4, c * NS:(c + 1) * NS], ACT.Copy, scale=PSC[:, c:c + 1])\
                    .then_inc(po["ev"], 1)

            def exps(u):
                U = units[u]
                i = U["i"]
                if U["new"]:
                    act.wait_ge(pa["cnb"], i + 1)
                    act.activation(SC[:, :, 0:31], SC[:, :, 0:31], ACT.Exp, scale=SCALE).then_inc(pa["cexp"], 1)
                act.wait_ge(pa["nb"], u + 1)
                for x, b in enumerate(U["br"]):
                    n = (i + 1 - b["j0"]) * P
                    y = x if U["nsa"] else 0
                    last = act.activation(SB[:, u % 3, x, 0:n], SB[:, u % 3, x, 0:n], ACT.Exp,
                                          bias=NBI[:, u % 3, y:y + 1], scale=SCALE, accum_out=DEN[:, u % 3, x:x + 1])
                last.then_inc(pa["exp"], 1)

            def tevac(u):
                U = units[u]
                for x in range(3):
                    B = 3 * u + x
                    act.wait_ge(pa["t"], B + 1)
                    if B >= 3:
                        act.wait_ge(pa["pv"], B - 2)
                    if U["nsa"] and x == 2:
                        act.activation(PTS[0:31, B % 3, 0:P], PS[0:31, 3 + B % 2, 0:P], ACT.Copy).then_inc(pa["tev"], 1)
                    else:
                        n = (U["i"] + 1 - U["br"][x]["j0"]) * P
                        act.activation(PTS[:, B % 3, 0:n], PS[:, 3 + B % 2, 0:n], ACT.Copy).then_inc(pa["tev"], 1)

            exps(0)
            for u in range(NU):
                if u + 1 < NU:
                    exps(u + 1)
                tevac(u)

            def pack(b, t):
                act.wait_ge(ld_kv[b % 3][t], 32 * (b // 3 + 1))
                if t >= 2:
                    act.wait_ge(sa["kt"], NGR * b + t - 1)
                elif b:
                    act.wait_ge(sa["kt"], NGR * (b - 1) + t + 3)
                for h in range(2):
                    src = KV[b % 3][0:SEL7, (2 * t + h) * 1024:(2 * t + h + 1) * 1024].rearrange("p (j c) -> p j c", j=4)
                    act.activation(KPK[t % 2][:, :, h * HD:(h + 1) * HD], src[:, :, h * HD:(h + 1) * HD], ACT.Copy)\
                        .then_inc(sa["pack"], 1)

            def kevac(b, x):
                n = NGR * b + x
                tiles, rows, _, _ = cached(b, x)
                act.wait_ge(sa["kt"], n + 1)
                if n >= 2:
                    act.wait_ge(sa["ks"], n - 1)
                w = len(tiles)
                cols = lambda a: a.rearrange("p (j c) -> p j c", c=P)[:, :, 0:rows]
                act.activation(cols(KTBS[n % 2][:, 0:w * P]), cols(PS[:, n % 2, 0:w * P]), ACT.Copy)\
                    .then_inc(sa["ktev"], 1)

            def keys(b, x):
                if x < 3:
                    pack(b, x + 1)
                if x == NGR - 1 and b + 1 < NB:
                    pack(b + 1, 0)
                kevac(b, x)

            def rows_out(b):
                act.wait_ge(sa["pv"], b + 1)
                if b:
                    act.wait_ge(sa["ot"], b)
                act.activation(OSR, PS[0:6, 6, :], ACT.Copy).then_inc(sa["rev"], 1)
                act.activation(OWR, PS[0:24, 7, 0:P], ACT.Copy).then_inc(sa["rev"], 1)
                act.activation(ODR, PS[0:8, 7, P:4 * P], ACT.Copy).then_inc(sa["rev"], 1)

            act.wait_ge(pa["pv"], 3 * NU)
            pack(0, 0)
            for x in range(NGR):
                keys(0, x)
            for b in range(NB):
                for x in range(NGR):
                    if x == 1 and b:
                        rows_out(b - 1)
                    if x == 6:
                        act.wait_ge(sa["sub"], b + 1)
                        act.activation(EXS[b % 2], EXS[b % 2], ACT.Exp, scale=SCALE).then_inc(sa["exp"], 1)
                    if b + 1 < NB:
                        keys(b + 1, x)
            rows_out(NB - 1)

            act.wait_ge(sa["pv"], NB)
            lead(L_OUT, KD * P)
            lead(L_OUT + 1, KD * P)
            act.wait_ge(sa["ex"], 1)
            for k in range(KD):
                act.activation(MIXH[:, k, :], MIXT[:, k, :], ACT.Copy).then_inc(mx["hi"], 1)
            for L in range(L_OUT + 2, L_FFN[1] + 2):
                lead(L, KD * P)
            rms(2)
            parts(2)
            ffn(1, 0)
            for x in range(1, 10, 2):
                R = tile_rows(x // 2)
                act.wait_ge(y_tr, x + 1)
                act.wait_ge(y_ev, x)
                act.activation(YO[0:R, x // 2, 512:1024], PS[0:R, x % 4, :], ACT.Copy).then_inc(y_ev, 1)

        @block.vector
        def _(dve):
            n_link = [0]

            def link(ins):
                n_link[0] += 1
                ins.then_inc(d_ch, 1)
                dve.wait_ge(d_ch, n_link[0])

            V = nc.vector
            dve.sem_inc(ev_dve, 4)
            dve.sem_inc(w_copied, 4)
            dve.wait_ge(ld["page"], 48)
            V.tensor_copy(PTF[:, :], PTI[:, :]).then_inc(ix_f, 1)
            dve.wait_ge(ix_mm, 1)
            V.tensor_scalar(IXC[:, :, :], PS[:, 7, 0:2 * NB].rearrange("p (s b) -> p s b", s=2), 8.0, RIP[:, 0:1],
                            ALU.mult, ALU.add).then_inc(ix_ok, 1)
            for k in range(KD):
                dve.wait_ge(x_tr, k + 1)
                V.tensor_copy(XT[:, k, 0:TP], PS[:, k % 6, :]).then_inc(x_ev, 1)
            V.memset(HIDC[:, :, 255:256], 0.0)
            V.tensor_copy(XT[:, :, TP:T], PS[:, 6, 0:KD * NS].rearrange("p (k t) -> p k t", k=KD)).then_inc(x_ev, 1)

            def square(r, k):
                x = XT[:, k, :].rearrange("p (h t) -> p h t", h=2)
                if k == 0:
                    link(V.tensor_tensor(SQA, x, x, ALU.mult))
                    return
                link(V.tensor_tensor(SQ, x, x, ALU.mult))
                ins = V.tensor_tensor(SQA, SQA, SQ, ALU.add)
                if k < KD - 1:
                    link(ins)
                else:
                    ins.then_inc(rs[r]["sq"], 1)

            def inverse(r):
                dve.wait_ge(rs[r]["root"], 1)
                link(V.reciprocal(RB, RB))

            dve.wait_ge(x_ev, KD + 1)
            for k in range(KD):
                square(0, k)
            dve.wait_ge(ld["small"], SMALL)

            def remain(L, n, it=0, step=0):
                sl = L % RING
                dve.wait_ge(w_hi, it * step + (L + 1))
                V.tensor_tensor(WLO[:, sl, 0:n], RAW[:, sl, 0:n], WHI[:, sl, 0:n].bitcast(F32), ALU.subtract)\
                    .then_inc(w_lo, 1)

            def evac(b, kv, j):
                n = 8 * kv + j
                dve.wait_ge(t_done, b * 16 + (n + 1))
                dve.wait_ge(m_done, b * 4 + (2 * kv + 2))
                for s in range(2):
                    last = V.tensor_copy(PTB[kv][s * HD:(s + 1) * HD, 1, j, :],
                                         PS[HD:P, j % 4, s * 256:(s + 1) * 256])
                last.then_inc(ev_dve, 1)

            CKb = CK.rearrange("p (b c n) -> p b c n", b=NB, c=2)

            def rows_out(b, m):
                dve.wait_ge(w_done, b * 4 + (2 + m + 1))
                src = PS[:, 6 + m % 2, :].rearrange("p (c q d) -> p c q d", c=2, q=4)[:, :, m, :]
                dst = CKb if m < 2 else CV[:, :, :, :]
                h = m % 2
                bb = bass.ds(b, 1) if not isinstance(b, int) else slice(b, b + 1)
                V.tensor_copy(dst[:, bb, :, h * HD:(h + 1) * HD].rearrange("p a c d -> p (a c) d"), src)\
                    .then_inc(w_copied, 1)

            def compress(b, last):
                for j in range(8):
                    evac(b, 1, j)
                if last:
                    inverse(0)
                    remain(0, KD * P)
                    remain(1, KD * P)
                rows_out(b, 0)
                if not last:
                    for j in range(4):
                        evac(b + 1, 0, j)
                rows_out(b, 1)
                if not last:
                    for j in range(4, 7):
                        evac(b + 1, 0, j)
                rows_out(b, 2)
                if not last:
                    evac(b + 1, 0, 7)
                rows_out(b, 3)

            for j in range(8):
                evac(0, 0, j)
            with dve.Fori(0, NB - 1) as it:
                compress(it, False)
            compress(NB - 1, True)

            def hn(r):
                for k in range(KD + 1):
                    if k < KD:
                        V.scalar_tensor_tensor(HNF[:, k, :].rearrange("p (h t) -> p h t", h=2),
                                               XT[:, k, :].rearrange("p (h t) -> p h t", h=2), NG[:, r, k:k + 1], RB,
                                               ALU.mult, ALU.mult).then_inc(rs[r]["f"], 1)
                    if k:
                        dve.wait_ge(rs[r]["hi"], k)
                        V.tensor_tensor(HNL[:, k - 1, :], HNF[:, k - 1, :], HNH[:, k - 1, :].bitcast(F32), ALU.subtract)\
                            .then_inc(rs[r]["lo"], 1)

            def ffn(f, after):
                for blk in range(2):
                    L0 = L_FFN[f] + blk * L_BLOCK
                    e0 = blk * (BCH + KD)

                    def hid_lo(m, it, step):
                        dve.wait_ge(ff[f]["hi"], it * step + (blk * BCH + m + 1))
                        dve.sem_inc(ff[f]["free"], 1)
                        row = bass.ds(it * step + m, 1) if step else slice(m, m + 1)
                        V.tensor_tensor(HIDL[:, row, :], HIDF[:, row, :], HIDH[:, row, :].bitcast(F32), ALU.subtract)\
                            .then_inc(ff[f]["lo"], 1)

                    def chunk(m, it, step, nxt):
                        e = e0 + m
                        remain(L0 + 2 * m + 2, nxt, it, 2 * step)
                        remain(L0 + 2 * m + 3, nxt, it, 2 * step)
                        dve.wait_ge(ff[f]["silu"], it * step + (blk * BCH + m + 1))
                        dve.wait_ge(w_used, it * (2 * step) + (L0 + 2 * m + 2))
                        row = bass.ds(it * step + m, 1) if step else slice(m, m + 1)
                        V.tensor_tensor(HIDF[:, row, :].rearrange("p a (h t) -> p (a h) t", h=2), GB[:, e % 2, :, :],
                                        PS[:, 4 * (e % 2) + 2:4 * (e % 2) + 4, 0:HALF], ALU.mult).then_inc(ff[f]["mul"], 1)
                        hid_lo(m, it, step)

                    with dve.Fori(0, BCH // 2) as it:
                        for u in range(2):
                            chunk(u, it, 2, KD * P)
                    chunk(BCH - 1, 0, 0, SLOT)
                    LO, eo = L0 + 2 * BCH, e0 + BCH
                    for oc in range(KD):
                        e = eo + oc
                        if oc + 2 < KD:
                            remain(LO + oc + 2, SLOT)
                        elif blk == 0:
                            remain(LO + oc + 2, KD * P)
                        elif after:
                            remain(LO + oc + 2, after)
                        dve.wait_ge(w_used, LO + oc + 1)
                        x = XT[:, oc, :].rearrange("p (h t) -> p h t", h=2)
                        V.scalar_tensor_tensor(x, PS[:, 4 * (e % 2):4 * (e % 2) + 2, 0:HALF], 0.5, x, ALU.mult, ALU.add)\
                            .then_inc(ff[f]["free"], 1)
                        if f == 0 and blk == 1:
                            dve.wait_ge(ff[f]["free"], 2 + eo + oc + 1)
                            square(1, oc)

            dve.wait_ge(m_done, 4 + 4 * NB)
            hn(0)
            dve.wait_ge(w_copied, 4 + 4 * NB)
            link(V.tensor_tensor(CKS, CK, CK, ALU.mult))
            V.tensor_reduce(SSC, CKS.rearrange("p (n d) -> p n d", d=HD), AX.X, ALU.add).then_inc(ck_ss, 1)
            dve.wait_ge(ck_sq, 1)
            link(V.reciprocal(SSC, SSC))
            ck3 = CK.rearrange("p (n d) -> p n d", d=HD)
            link(V.tensor_tensor(ck3, ck3, SSC.unsqueeze(2).to_broadcast([P, 32, HD]), ALU.mult))
            V.tensor_tensor(ck3, ck3, QG[:, 1:2, :].to_broadcast([P, 32, HD]), ALU.mult).then_inc(ck_n, 1)
            ffn(0, KH * CG)
            dve.wait_ge(ck_t, 1)
            for n in range(4):
                last = V.tensor_copy(CKT[:, 2 * n:2 * n + 2, :], PS[:, 4 + n, :].rearrange("p (b c) -> p b c", b=2))
            last.then_inc(ck_ev, 1)
            inverse(1)
            hn(1)
            def squares_of(n):
                c, nh, _, off = SECTIONS[n]
                dve.wait_ge(pj_ev, 5 * section_end(n))
                if n:
                    dve.wait_ge(hn_ss, n)
                for R, ts in ((P, (0, 2)), (P, (2, 4)), (NS, (4, 5))):
                    nt = ts[1] - ts[0]
                    x = PROJ[0:R, ts[0]:ts[1], c:c + nh * HD]
                    q = SQT[0:R, 0:nt * nh * HD]
                    link(V.tensor_tensor(q.rearrange("p (t n) -> p t n", t=nt), x, x, ALU.mult))
                    ins = V.tensor_reduce(SS[0:R, ts[0]:ts[1], off:off + nh], q.rearrange("p (t n d) -> p t n d", t=nt, d=HD),
                                          AX.X, ALU.add)
                    if R == NS:
                        ins.then_inc(hn_ss, 1)
                    else:
                        link(ins)

            def scale_by(n):
                c, nh, g, off = SECTIONS[n]
                dve.wait_ge(hn_rt, n + 1)
                for R, ts, nt in ((P, slice(0, 4), 4), (NS, slice(4, 5), 1)):
                    ss = SS[0:R, ts, off:off + nh]
                    link(V.reciprocal(ss, ss))
                    x = PROJ[0:R, ts, c:c + nh * HD].rearrange("p t (n d) -> p t n d", d=HD)
                    link(V.tensor_tensor(x, x, ss.unsqueeze(3).to_broadcast([R, nt, nh, HD]), ALU.mult))
                    gain = QG[0:R, g:g + 1, :].unsqueeze(1)
                    if n == 0:
                        for h in range(2):
                            ins = V.tensor_tensor(QP[0:R, ts, :, h, :], x[:, :, 3 * h:3 * h + 3, :],
                                                  gain.to_broadcast([R, nt, 3, HD]), ALU.mult)
                    else:
                        ins = V.tensor_tensor(x, x, gain.to_broadcast([R, nt, nh, HD]), ALU.mult)
                ins.then_inc(qn, 1)

            for c in range(NCG + 1):
                if c + 1 < NCG:
                    for x in range(2):
                        remain(L_IN + 2 * c + 2 + x, KH * min(CG, COLS - (c + 1) * CG))
                for n in range(len(SECTIONS)):
                    if section_end(n) == c:
                        squares_of(n)
                    if section_end(n) + 1 == c:
                        scale_by(n)
            dve.wait_ge(w_used, L_OUT)
            link(V.memset(UT[:, :, 0:16], 0.0))
            for m in range(ITEMS):
                dve.wait_ge(qt_mm, m + 1)
                dst = QN[:, m, :] if m < IT_U else UTS[:, m - IT_U, :, 15:19]
                src = PS[:, 2 * (m % 4) + 1, 0:NS]
                if m >= IT_U:
                    src = src.rearrange("p (b t) -> p b t", b=NB)
                V.tensor_copy(dst, src).then_inc(qt_dve, 1)
            dve.wait_ge(qt_dve, ITEMS)
            link(V.memset(QA[:, :, :], 0.0))
            link(V.memset(QD[:, :, :, :], 0.0))
            for h in range(2):
                r = slice(h * HD, (h + 1) * HD)
                for g in range(3):
                    V.tensor_copy(QA[r, :, (h * 3 + g) * TS:(h * 3 + g + 1) * TS],
                                  QN[r, g, :].rearrange("p (b t) -> p b t", b=NB))
                    ins = V.tensor_copy(QD[r, g, :, h * TS:(h + 1) * TS],
                                        QN[r, IT_QB + g, :].rearrange("p (b t) -> p b t", b=NB))
            dve.wait_ge(cp_act, 8)
            V.tensor_copy(PT8F[:, :], PT8[:, :])
            own = const("tok_rows").rearrange("p (b h t) -> p b h t", b=NB, h=6)
            gt = GT[0:NS, 4, :].rearrange("p (h c) -> p c h", c=3)
            for c in range(3):
                ins = V.tensor_tensor(GX[:, c, :].rearrange("p (b h t) -> p b h t", b=NB, h=6), own,
                                      gt[:, c, :].unsqueeze(1).unsqueeze(3).to_broadcast([NS, NB, 6, TS]), ALU.mult)
            ins.then_inc(sc["gx"], 1)
            dve.wait_ge(po["st"], 1)
            for c in range(2):
                last = V.tensor_copy(UTS[:, c, :, 0:15], PS[:, 4, c * P:c * P + 120].rearrange("p (b t) -> p b t", b=NB))
            last.then_inc(po["stev"], 1)
            dve.wait_ge(po["stev"], 1)
            dve.wait_ge(qt_act, ITEMS)
            dve.wait_ge(qt_dve, ITEMS)
            dve.wait_ge(qt_mm, ITEMS)
            dve.wait_ge(cp_act, 8)
            dve.wait_ge(st_cmp, 16)
            dve.wait_ge(st_out, 16 * N_STATES)

            def windows(u, a, b_, dl, n0, n, head, nt):
                src, dst = u, a
                for step, w in enumerate((2, 4, 8, 16)):
                    sh = w // 2
                    link(V.tensor_tensor(dst[..., w - 1:n], src[..., w - 1:n], src[..., w - 1 - sh:n - sh], ALU.add))
                    c, q = step // 2, step % 2
                    r = slice(q * HD, (q + 1) * HD)
                    pw = const("pool_w")[r, c:c + 1]
                    link(V.scalar_tensor_tensor(dl[r, c], dst[r, c][..., n0:n], pw, u[r, c][..., n0:n],
                                                ALU.mult, ALU.subtract))
                    if head:
                        hd = const("pool_head")[r, c * 16:(c + 1) * 16]
                        link(V.tensor_tensor(PHD[r, c, :], dst[r, c, n0:n0 + 16], hd, ALU.mult))
                        link(V.tensor_tensor(dl[r, c, 0:16], PHD[r, c, :], u[r, c, n0:n0 + 16], ALU.subtract))
                    src, dst = dst, (b_ if dst is a else a)

            dve.wait_ge(sc["s"], 1)
            V.tensor_copy(SCM[:, 0, :], PS[:, 5, 0:192])
            link(V.tensor_scalar(SCM[:, 1, :], PS[:, 5, 192:384], const("no_block"), None, ALU.add))
            V.tensor_tensor(MXC, SCM[:, 0, :], SCM[:, 1, :], ALU.max).then_inc(sc["mx"], 1)
            dve.wait_ge(sc["gm"], 1)
            V.tensor_copy(GW[:, :, 0:2, :], PS[:, 6, 0:384].rearrange("p (c b r) -> p b c r", c=2, b=NB))
            V.tensor_copy(GW[:, :, 2, :], PS[:, 7, 0:192].rearrange("p (b r) -> p b r", b=NB))
            V.tensor_scalar(BROW[:, :, 0], PS[0:64, 7, 192:192 + NPG], 32.0, None, ALU.mult)
            link(V.tensor_scalar(BROW[:, :, 1], PS[0:64, 7, 192:192 + NPG], 32.0, 16.0, ALU.mult, ALU.add))
            dve.wait_ge(sc["mt"], 1)
            link(V.tensor_reduce(MXR, PS[0:96, 5, 0:256].rearrange("p (n k) -> p n k", n=2), AX.X, ALU.max))
            V.tensor_scalar(DGC[:, 0, :], ident[0:96, 0:96], MXR[:, 0:1], None, ALU.mult)
            V.tensor_scalar(DGC[:, 1, :], ident[0:96, 0:96], MXR[:, 1:2], None, ALU.mult).then_inc(sc["dg"], 1)
            dve.wait_ge(sc["bc"], 1)
            V.tensor_tensor(ECM, SCM, PS[:, 6, 0:192].unsqueeze(1).to_broadcast([P, 2, 192]), ALU.subtract)\
                .then_inc(sc["sub"], 1)
            windows(UT, T1, T2, DL, 16, 528, True, TP)
            dve.wait_ge(sc["exp"], 1)
            V.tensor_tensor(SUC, ECM[:, 0, :], ECM[:, 1, :], ALU.add).then_inc(sc["sum"], 1)
            dve.wait_ge(sc["den"], 1)
            link(V.reciprocal(RCC, PS[:, 7, 0:192]))
            link(V.tensor_tensor(ECM, ECM, RCC.unsqueeze(1).to_broadcast([P, 2, 192]), ALU.mult))
            for ct in range(2):
                ins = V.tensor_reduce(IMT[:, ct, :].rearrange("p (n t) -> p n t", t=TS),
                                      ECM[:, ct, :].rearrange("p (n g t) -> p n t g", g=3, t=TS), AX.X, ALU.add)
            ins.then_inc(sc["im"], 1)
            windows(UTS, T1S, T2S, DLS, 15, 19, False, NS)
            V.sem_inc(po["dl"], 1)
            dve.wait_ge(sc["imt"], 1)
            link(V.tensor_copy(IM, PS[0:64, 5, 0:256]))
            link(V.tensor_reduce(SCR, IM.rearrange("p (j c) -> p j c", c=4), AX.X, ALU.add))
            link(V.tensor_tensor(SCR[:, 1:64], SCR[:, 1:64], IM[:, 3:252:4], ALU.add))
            link(V.tensor_tensor(SCR, SCR, const("force"), ALU.add))
            link(V.max(M8, SCR))
            link(V.max_index(I8[:, :], M8, SCR))
            link(V.tensor_copy(SLOT7, I8[:, 0:SLOTS]))
            link(V.tensor_tensor(HOT, const("blocks").unsqueeze(1).to_broadcast([64, SLOTS, 64]),
                                 SLOT7.unsqueeze(2).to_broadcast([64, SLOTS, 64]), ALU.is_equal))
            link(V.tensor_tensor(HOT, HOT, BROW.rearrange("p g c -> p (g c)").unsqueeze(1)
                                 .to_broadcast([64, SLOTS, 64]), ALU.mult))
            link(V.tensor_reduce(SLOT7, HOT, AX.X, ALU.add))
            V.tensor_tensor(ROWS, SLOT7.unsqueeze(2).to_broadcast([64, SLOTS, 16]),
                            const("rows16").unsqueeze(1).to_broadcast([64, SLOTS, 16]), ALU.add).then_inc(sc["rows"], 1)
            dve.wait_ge(sc["pv"], 1)
            V.tensor_tensor(OA, PS[:, 6, 0:192].rearrange("p (b r) -> p b r", b=NB), GW[:, :, 0, :], ALU.mult)
            dve.wait_ge(sc["turn"], 1)
            V.tensor_copy(IXS[:, :], PS[0:SEL7, 7, 0:64]).then_inc(sc["ix"], 1)
            dve.wait_ge(pc["w"], 1)
            V.tensor_copy(CVP, PS[0:31, 3, 2 * HD:4 * HD])
            link(V.tensor_copy(CKP, PS[0:31, 3, 0:2 * HD]))
            link(V.tensor_tensor(CKPS, CKP, CKP, ALU.mult))
            V.tensor_reduce(SSP, CKPS.rearrange("p (n d) -> p n d", d=HD), AX.X, ALU.add).then_inc(pc["ss"], 1)
            dve.wait_ge(pc["rt"], 1)
            link(V.reciprocal(SSP, SSP))
            kp = CKP.rearrange("p (n d) -> p n d", d=HD)
            link(V.tensor_tensor(kp, kp, SSP.unsqueeze(2).to_broadcast([31, 2, HD]), ALU.mult))
            V.tensor_tensor(kp, kp, QG[0:31, 1:2, :].to_broadcast([31, 2, HD]), ALU.mult).then_inc(pc["n"], 1)
            dve.wait_ge(pc["t"], 1)
            V.tensor_copy(CKTP[:, 0:31], PS[:, 2, 0:31]).then_inc(pc["ev2"], 1)

            def cmp_scores(i):
                dve.wait_ge(pa["cs"], 2 * i + 2)
                if i:
                    dve.wait_ge(pa["t"], 3 * (8 * (i - 1) + 5) + 3)
                s = SC[:, :, 0:31]
                add = const("cmp_add")[:, i * 32:i * 32 + 31].unsqueeze(1).to_broadcast([P, 6, 31])
                link(V.tensor_tensor(s, PS[:, 7, 0:192].rearrange("p (h n) -> p h n", h=6)[:, :, 0:31], add, ALU.add))
                link(V.tensor_reduce(CMX, s, AX.X, ALU.max))
                V.tensor_tensor(s, s, CMX.unsqueeze(2).to_broadcast([P, 6, 31]), ALU.subtract).then_inc(pa["cnb"], 1)

            def cmp_weights(i):
                s = SC[:, :, 0:31]
                keep = const("cmp_keep")[:, i * 32:i * 32 + 31].unsqueeze(1).to_broadcast([P, 6, 31])
                dve.wait_ge(pa["cexp"], i + 1)
                link(V.tensor_tensor(s, s, keep, ALU.mult))
                link(V.tensor_reduce(CDN, s, AX.X, ALU.add))
                link(V.tensor_scalar(CDN, CDN, 1.0e-30, None, ALU.max))
                link(V.reciprocal(CDN, CDN))
                link(V.tensor_tensor(CWT, CDN, GT[:, i, :].rearrange("p (h c) -> p h c", c=3)[:, :, 0], ALU.mult))
                V.tensor_tensor(s, s, CWT.unsqueeze(2).to_broadcast([P, 6, 31]), ALU.mult).then_inc(pa["cp"], 1)

            def lift(u):
                U = units[u]
                i = U["i"]
                if U["new"]:
                    cmp_scores(i)
                if u >= 3:
                    dve.wait_ge(pa["t"], 3 * (u - 3) + 3)
                for x, b in enumerate(U["br"]):
                    B = U["s0"] + x
                    dve.wait_ge(pa["s"], B + 1)
                    n = i - b["j0"]
                    s = SB[:, u % 3, x, :]
                    if n:
                        src, dst = PS[:, B % 3, 0:n * P], s[:, 0:n * P]
                        if b["off"] is None:
                            V.tensor_copy(dst, src)
                        else:
                            m = const(b["off"]).unsqueeze(1).to_broadcast([P, n, P])
                            V.tensor_tensor(dst.rearrange("p (j c) -> p j c", c=P),
                                            src.rearrange("p (j c) -> p j c", c=P), m, ALU.add)
                    V.tensor_tensor(s[:, n * P:(n + 1) * P], PS[:, B % 3, n * P:(n + 1) * P], const(b["diag"]),
                                    ALU.add).then_inc(pa["sev"], 1)
                dve.wait_ge(pa["sev"], U["s0"] + len(U["br"]))
                nb = NBI[:, u % 3, :]
                if U["nsa"]:
                    link(V.tensor_reduce(MX[:, u % 3, 0:2], SB[:, u % 3, 0:2, 0:(i + 1) * P], AX.X, ALU.max))
                    V.tensor_scalar(nb[:, 0:2], MX[:, u % 3, 0:2], -SCALE, None, ALU.mult).then_inc(pa["nb"], 1)
                else:
                    for x, b in enumerate(U["br"]):
                        ins = V.tensor_reduce(MX[:, u % 3, x:x + 1], SB[:, u % 3, x, 0:(i + 1 - b["j0"]) * P], AX.X,
                                              ALU.max)
                    link(ins)
                    link(V.tensor_reduce(MX1[:, u % 3:u % 3 + 1], MX[:, u % 3, :], AX.X, ALU.max))
                    V.tensor_scalar(nb[:, 0:1], MX1[:, u % 3:u % 3 + 1], -SCALE, None, ALU.mult).then_inc(pa["nb"], 1)

            def weigh(u):
                U = units[u]
                i = U["i"]
                if U["new"]:
                    cmp_weights(i)
                dve.wait_ge(pa["exp"], u + 1)
                w, d = WT[:, u % 3, :], DEN[:, u % 3, :]
                if U["nsa"]:
                    link(V.reciprocal(w[:, 0:2], d[:, 0:2]))
                    link(V.tensor_tensor(w[:, 0:2], w[:, 0:2], GT[:, i, U["hq"] * 3 + 1:U["hq"] * 3 + 3], ALU.mult))
                else:
                    link(V.tensor_reduce(w[:, 2:3], d, AX.X, ALU.add))
                    link(V.reciprocal(w[:, 0:1], w[:, 2:3]))
                for x, b in enumerate(U["br"]):
                    n = (i + 1 - b["j0"]) * P
                    y = x if U["nsa"] else 0
                    ins = V.tensor_scalar(SB[:, u % 3, x, 0:n], SB[:, u % 3, x, 0:n], w[:, y:y + 1], None, ALU.mult)
                ins.then_inc(pa["p"], 1)

            def out(u):
                U = units[u]
                c = slice(U["i"] * P, (U["i"] + 1) * P)
                dve.wait_ge(pa["pv"], 3 * u + 3)
                if U["nsa"]:
                    r = slice(U["hq"] % 2 * HD, U["hq"] % 2 * HD + HD)
                    V.tensor_copy(MIXT[r, U["hq"] // 2, c], PS[r, 5 + u % 2, 0:P]).then_inc(pa["oev"], 1)
                else:
                    r = slice(U["h"] * HD, (U["h"] + 1) * HD)
                    V.tensor_copy(MIXT[r, 3:6, c], PS[r, 5 + u % 2, 0:3 * P].rearrange("p (g t) -> p g t", g=3))\
                        .then_inc(pa["oev"], 1)

            lift(0)
            lift(1)
            for u in range(NU):
                weigh(u)
                if u + 2 < NU:
                    lift(u + 2)
                if u >= 1:
                    out(u - 1)
            out(NU - 1)

            dve.wait_ge(pa["oev"], NU)
            link(V.memset(SCO, NEG))

            def masked(b):
                dve.wait_ge(sa["ks"], NGR * (b + 1))
                if b:
                    dve.wait_ge(sa["sub"], b)
                src, dst = PS[:, 2 + b % 2, :], SCO
                na, nd = (const(n)[:, b * 24:(b + 1) * 24] for n in ("new_a", "new_d"))
                V.tensor_copy(dst[0:SEL7, 0:96], src[0:SEL7, 0:96])
                V.tensor_tensor(dst[:, 120:216], src[:, 120:216], const("win_past"), ALU.add)
                V.tensor_tensor(dst[:, 240:312], src[:, 240:312], const("dil_past"), ALU.add)
                two = lambda a: a[0:NS, 0:240].rearrange("p (n c) -> p n c", n=2)[:, :, 96:120]
                V.tensor_tensor(two(dst), two(src), na.unsqueeze(1).to_broadcast([NS, 2, 24]), ALU.add)
                V.tensor_tensor(dst[0:NS, 312:336], src[0:NS, 312:336], nd, ALU.add).then_inc(sa["add"], 1)

            def over_tiles(src, dst, op):
                at = 0
                for c, n, R in SECT:
                    ins = V.tensor_reduce(dst[:, at:at + R], src[:, c:c + n * R].rearrange("p (n r) -> p r n", r=R), AX.X, op)
                    at += R
                return ins

            def maxima(b):
                dve.wait_ge(sa["add"], b + 1)
                over_tiles(SCO, SMX, ALU.max).then_inc(sa["mx"], 1)

            def diagonal(b):
                dve.wait_ge(sa["mt"], b + 1)
                link(V.tensor_reduce(SDG[:, 0:1], PS[0:56, 5, 0:P], AX.X, ALU.max))
                V.tensor_scalar(SDG[:, 1:57], ident[0:56, 0:56], SDG[:, 0:1], None, ALU.mult).then_inc(sa["dg"], 1)

            def below(b):
                dve.wait_ge(sa["bc"], b + 1)
                if b >= 2:
                    dve.wait_ge(sa["pv"], b - 1)
                at = P
                for c, n, R in SECT:
                    ins = V.tensor_tensor(EXS[b % 2][:, c:c + n * R].rearrange("p (n r) -> p n r", r=R),
                                          SCO[:, c:c + n * R].rearrange("p (n r) -> p n r", r=R),
                                          PS[:, 5, at:at + R].unsqueeze(1).to_broadcast([P, n, R]), ALU.subtract)
                    at += R
                ins.then_inc(sa["sub"], 1)

            def sums(b):
                dve.wait_ge(sa["exp"], b + 1)
                over_tiles(EXS[b % 2], SSUM, ALU.add).then_inc(sa["sum"], 1)

            def outs(b):
                dve.wait_ge(sa["ot"], b + 1)
                ps = PS[:, 5, 192:320]
                link(V.reciprocal(SINV, ps[:, 72:128]))
                link(V.tensor_tensor(SWG[:, 0:48], SINV[:, 0:48], GW[:, b, 1:3, :].rearrange("p c r -> p (c r)"), ALU.mult))
                V.tensor_tensor(OP[:, b, :, :].rearrange("p c r -> p (c r)"), ps[:, 0:48], SWG[:, 0:48], ALU.mult)
                V.tensor_tensor(OD[:, b, :, :], ps[:, 48:72].rearrange("p (g r) -> p g r", g=3),
                                SINV[:, 48:56].unsqueeze(1).to_broadcast([P, 3, 8]), ALU.mult).then_inc(sa["out"], 1)

            masked(0)
            for b in range(NB):
                maxima(b)
                if b:
                    outs(b - 1)
                diagonal(b)
                below(b)
                sums(b)
                if b + 1 < NB:
                    masked(b + 1)
            outs(NB - 1)
            dve.wait_ge(sa["out"], NB)
            link(V.tensor_tensor(OA, OA, OP[:, :, 0, :], ALU.add))
            link(V.tensor_tensor(OA, OA, OP[:, :, 1, :], ALU.add))
            for hq in range(6):
                h, g = hq // 3, hq % 3
                e = slice(hq % 2 * HD, hq % 2 * HD + HD)
                V.tensor_copy(MIXT[e, hq // 2, TP:T].rearrange("p (b t) -> p b t", b=NB),
                              OA[h * HD:(h + 1) * HD, :, hq * TS:(hq + 1) * TS])
            for h in range(2):
                r = slice(h * HD, (h + 1) * HD)
                for g in range(3):
                    ins = V.tensor_copy(MIXT[r, 3 + g, TP:T].rearrange("p (b t) -> p b t", b=NB),
                                        OD[r, :, g, h * TS:(h + 1) * TS])
            ins.then_inc(sa["ex"], 1)
            remain(L_OUT, KD * P)
            remain(L_OUT + 1, KD * P)
            for k in range(KD):
                dve.wait_ge(mx["hi"], k + 1)
                V.tensor_tensor(MIXL[:, k, :], MIXT[:, k, :], MIXH[:, k, :].bitcast(F32), ALU.subtract)\
                    .then_inc(mx["lo"], 1)
            for oc in range(KD):
                remain(L_OUT + oc + 2, KD * P)
                dve.wait_ge(w_used, L_OUT + oc + 1)
                x = XT[:, oc, :].rearrange("p (h t) -> p h t", h=2)
                V.tensor_tensor(x, x, PS[:, 4 * (oc % 2):4 * (oc % 2) + 2, 0:HALF], ALU.add).then_inc(wo_ev, 1)
                dve.wait_ge(wo_ev, oc + 1)
                square(2, oc)
            inverse(2)
            hn(2)
            ffn(1, 0)
            for x in range(0, 10, 2):
                R = tile_rows(x // 2)
                dve.wait_ge(y_tr, x + 1)
                if x:
                    dve.wait_ge(y_ev, x)
                V.tensor_copy(YO[0:R, x // 2, 0:512], PS[0:R, x % 4, :]).then_inc(y_ev, 1)


SMALL = 16 * 8
N_STATES = 7 + 12
N_COPIES = 2 + 1 + 2 + 8 + 1

_INS = ["x_prompt", "x_sample", "cache_cmp_kv", "cache_slc_kv", "cache_win_kv", "cache_dil0_kv", "cache_dil1_kv",
        "cache_dil2_kv", "state_pool", "page_table", "w_in", "w_out", "norm_gain", "qk_gain", "ffn_in", "ffn_out",
        "cmp_w1", "cmp_b1", "cmp_w2", "pool_w", "pool_scale"]
_OUTS = [("y_p", (1, TP, D)), ("y_s", (NB, TS, D)),
         ("cmp_p", (1, 1, TP, 2, 2, HD)), ("cmp_s", (1, NB, TS, 2, 2, HD)),
         ("slc_p", (1, 1, TP, 2, 2, HD)), ("slc_s", (1, NB, TS, 2, 2, HD)),
         ("win_p", (1, 1, 512, 2, 2, HD)), ("win_s", (1, NB, 512, 2, 2, HD)),
         ("dil0_p", (1, 1, 128, 2, 2, HD)), ("dil0_s", (1, NB, 128, 2, 2, HD)),
         ("dil1_p", (1, 1, 512, 2, 2, HD)), ("dil1_s", (1, NB, 512, 2, 2, HD)),
         ("dil2_p", (1, 1, 512, 2, 2, HD)), ("dil2_s", (1, NB, 2048, 2, 2, HD)),
         ("pool_p", (1, 1, 15, 256)), ("pool_s", (1, NB, 15, 256))]


def kernel(**inputs):
    import concourse.bacc as _bacc
    from concourse.bass_utils import run_bass_kernel_spmd as _run

    nc = _bacc.Bacc("TRN2", target_bir_lowering=False, num_devices=1)
    arrays, ins, outs = {}, {}, {}
    given = {n: np.ascontiguousarray(inputs[n]) for n in _INS}
    given["consts"] = constants()
    given["selp"] = page_selectors()
    given["rip"] = row_in_page()
    for name, a in given.items():
        arrays[f"in_{name}"] = a
        ins[name] = nc.dram_tensor(f"in_{name}", a.shape, mybir.dt.from_np(a.dtype), kind="ExternalInput").ap()
    for name, shape in _OUTS:
        outs[name] = nc.dram_tensor(f"out_{name}", shape, F32, kind="ExternalOutput").ap()
    build(nc, ins, outs)
    r = _run(nc, [arrays], core_ids=[0])
    return tuple(r.results[0][f"out_{name}"] for name, _ in _OUTS)
```
